# Optimizing a Trainium2 kernel written in Bass

```python
import jax, jax.numpy as jnp
from jax import lax
import numpy as np
import math

D_MODEL = 1024
BATCH = 1
SEQ = 512
DEPTH = 2

GRID_W = 64
CTX_LEN = 256
N_MIXERS = 4
Q_BLOCK = 128
ROPE_THETA = 10000.0
NORM_EPS = 1e-6
CONV_WIDTH = 31
CONV_PAD = CONV_WIDTH // 2
GQA_HEADS = 16
GQA_KV_HEADS = 4
GQA_GROUP = GQA_HEADS // GQA_KV_HEADS
GQA_HEAD_DIM = D_MODEL // GQA_HEADS
POOL_WINDOWS = (2, 4, 8, 16)
POOL_GROUP = D_MODEL // len(POOL_WINDOWS)
MLA_HEADS = 16
MLA_NOPE = 64
MLA_ROPE = 32
MLA_V = 64
MLA_QK = MLA_NOPE + MLA_ROPE
MLA_Q_LORA = 768
MLA_KV_LORA = 256
D_FF = 4 * D_MODEL
N_CONV = (DEPTH + 3) // N_MIXERS
N_GQA = (DEPTH + 2) // N_MIXERS
N_POOL = (DEPTH + 1) // N_MIXERS
N_MLA = DEPTH // N_MIXERS


def rms_norm(x, g):
    xf = x.astype(jnp.float32)
    y = xf * lax.rsqrt(jnp.mean(xf * xf, axis=-1, keepdims=True) + NORM_EPS)
    return (y * g.astype(jnp.float32)).astype(x.dtype)

def layer_norm(x, g, b):
    xf = x.astype(jnp.float32)
    mu = jnp.mean(xf, axis=-1, keepdims=True)
    var = jnp.mean(jnp.square(xf - mu), axis=-1, keepdims=True)
    y = (xf - mu) * lax.rsqrt(var + NORM_EPS)
    return (y * g.astype(jnp.float32) + b.astype(jnp.float32)).astype(x.dtype)

def modulate(h, shift, scale):
    return h * (1 + scale[..., None, :]) + shift[..., None, :]

def axial_tables(row, col, rot_dim):
    quarter = rot_dim // 4
    inv = ROPE_THETA ** (-jnp.arange(quarter, dtype=jnp.float32) / quarter)
    ang_r = row[:, None] * inv
    ang_c = col[:, None] * inv
    return (jnp.cos(ang_r), jnp.sin(ang_r), jnp.cos(ang_c), jnp.sin(ang_c))

def _rotate(v, cos, sin):
    a, b = jnp.split(v, 2, axis=-1)
    cos = cos.astype(v.dtype)
    sin = sin.astype(v.dtype)
    return jnp.concatenate([a * cos - b * sin, b * cos + a * sin], axis=-1)

def apply_axial_rope(x, tables):
    cr, sr, cc, sc = tables
    xr, xc = jnp.split(x, 2, axis=-1)
    return jnp.concatenate([_rotate(xr, cr, sr), _rotate(xc, cc, sc)], axis=-1)

def softmax_attend(q, k, v):
    s = jnp.einsum('bkgqd,bkld->bkgql', q, k).astype(jnp.float32) * (q.shape[-1] ** -0.5)
    p = jax.nn.softmax(s, axis=-1).astype(v.dtype)
    return jnp.einsum('bkgql,bkld->bkgqd', p, v)

def blocked_attend(q, k, v):
    b, kh, g, t, dq = q.shape
    nb = t // Q_BLOCK
    qb = q.reshape(b, kh, g, nb, Q_BLOCK, dq).transpose(3, 0, 1, 2, 4, 5)
    out = lax.map(lambda qq: softmax_attend(qq, k, v), qb)
    return out.transpose(1, 2, 3, 0, 4, 5).reshape(b, kh, g, t, v.shape[-1])

def merge_heads(o):
    b, kh, g, t, dv = o.shape
    return o.transpose(0, 3, 1, 2, 4).reshape(b, t, kh * g * dv)

def conv_module(h, w_pw1, w_dw, b_dw, ln_g, ln_b, w_pw2):
    u = h @ w_pw1
    a, gate = jnp.split(u, 2, axis=-1)
    u = a * jax.nn.sigmoid(gate)
    u = lax.conv_general_dilated(
        u, w_dw[:, None, :].astype(u.dtype), window_strides=(1,),
        padding=[(CONV_PAD, CONV_PAD)], dimension_numbers=('NWC', 'WIO', 'NWC'),
        feature_group_count=D_MODEL) + b_dw
    u = jax.nn.silu(layer_norm(u, ln_g, ln_b))
    return u @ w_pw2

def gqa_project(h, w_qkv, q_norm, k_norm):
    b, t, _ = h.shape
    nq = GQA_HEADS * GQA_HEAD_DIM
    nk = GQA_KV_HEADS * GQA_HEAD_DIM
    qkv = h @ w_qkv
    q = qkv[..., :nq].reshape(b, t, GQA_KV_HEADS, GQA_GROUP, GQA_HEAD_DIM).transpose(0, 2, 3, 1, 4)
    k = qkv[..., nq:nq + nk].reshape(b, t, GQA_KV_HEADS, GQA_HEAD_DIM).transpose(0, 2, 1, 3)
    v = qkv[..., nq + nk:].reshape(b, t, GQA_KV_HEADS, GQA_HEAD_DIM).transpose(0, 2, 1, 3)
    return rms_norm(q, q_norm), rms_norm(k, k_norm), v

def gqa_mixer(hl, hc, w_qkv, q_norm, k_norm, w_o, tables, with_ctx):
    ql, kl, vl = gqa_project(hl, w_qkv, q_norm, k_norm)
    qc, kc, vc = gqa_project(hc, w_qkv, q_norm, k_norm)
    ql = apply_axial_rope(ql, tables)
    kl = apply_axial_rope(kl, tables)
    k_all = jnp.concatenate([kc, kl], axis=2)
    v_all = jnp.concatenate([vc, vl], axis=2)
    ol = merge_heads(blocked_attend(ql, k_all, v_all)) @ w_o
    oc = merge_heads(softmax_attend(qc, kc, vc)) @ w_o if with_ctx else None
    return ol, oc

def pool_mixer(h, w_pool, scale):
    b, t, _ = h.shape
    hf = h.astype(jnp.float32)
    cs = jnp.concatenate([jnp.zeros((b, 1, D_MODEL), jnp.float32), jnp.cumsum(hf, axis=1)], axis=1)
    pos = jnp.arange(t)
    outs = []
    for g, w in enumerate(POOL_WINDOWS):
        lo = jnp.clip(pos - w // 2, 0, t)
        hi = jnp.clip(pos + w - w // 2, 0, t)
        csg = cs[..., g * POOL_GROUP:(g + 1) * POOL_GROUP]
        win = jnp.take(csg, hi, axis=1) - jnp.take(csg, lo, axis=1)
        cnt = (hi - lo).astype(jnp.float32)[:, None]
        outs.append(win / cnt - hf[..., g * POOL_GROUP:(g + 1) * POOL_GROUP])
    p = jnp.stack(outs, axis=2).astype(h.dtype)
    y = jnp.einsum('btgc,gcd->btgd', p, w_pool).reshape(b, t, D_MODEL)
    return y * scale

def mla_project(h, w_dq, q_lora_norm, w_uq, w_dkv, kv_lora_norm, w_ukv, q_norm, k_norm):
    b, t, _ = h.shape
    cq = rms_norm(h @ w_dq, q_lora_norm)
    q = (cq @ w_uq).reshape(b, t, MLA_HEADS, MLA_QK).transpose(0, 2, 1, 3)
    dkv = h @ w_dkv
    ckv = rms_norm(dkv[..., :MLA_KV_LORA], kv_lora_norm)
    k_rope = dkv[..., MLA_KV_LORA:]
    kv = (ckv @ w_ukv).reshape(b, t, MLA_HEADS, MLA_NOPE + MLA_V).transpose(0, 2, 1, 3)
    k_nope, v = kv[..., :MLA_NOPE], kv[..., MLA_NOPE:]
    k = jnp.concatenate([k_nope, jnp.broadcast_to(k_rope[:, None], (b, MLA_HEADS, t, MLA_ROPE))], axis=-1)
    return rms_norm(q, q_norm), rms_norm(k, k_norm), v

def rope_tail(x, tables):
    return jnp.concatenate([x[..., :MLA_NOPE], apply_axial_rope(x[..., MLA_NOPE:], tables)], axis=-1)

def mla_mixer(hl, hc, w_dq, q_lora_norm, w_uq, w_dkv, kv_lora_norm, w_ukv, q_norm, k_norm, w_o,
              tables, with_ctx):
    args = (w_dq, q_lora_norm, w_uq, w_dkv, kv_lora_norm, w_ukv, q_norm, k_norm)
    ql, kl, vl = mla_project(hl, *args)
    qc, kc, vc = mla_project(hc, *args)
    ql = rope_tail(ql, tables)[:, :, None]
    kl = rope_tail(kl, tables)
    k_all = jnp.concatenate([kc, kl], axis=2)
    v_all = jnp.concatenate([vc, vl], axis=2)
    ol = merge_heads(blocked_attend(ql, k_all, v_all)) @ w_o
    oc = merge_heads(softmax_attend(qc[:, :, None], kc, vc)) @ w_o if with_ctx else None
    return ol, oc

def sq_relu_mlp(h, w1, w2):
    return jnp.square(jax.nn.relu(h @ w1)) @ w2

def first_inputs(seed: int = 0) -> dict:
    key = jax.random.key(seed)
    ks = jax.random.split(key, 31)
    f32 = jnp.float32

    def nrm(k, shape, scale):
        return jax.random.normal(k, shape, f32) * scale

    def gain(k, shape):
        return 1.0 + 0.05 * jax.random.normal(k, shape, f32)

    d = D_MODEL
    return {
        'x': nrm(ks[0], (BATCH, SEQ, d), 1.0),
        'c': nrm(ks[1], (BATCH, d), 1.0),
        'ctx': nrm(ks[2], (BATCH, CTX_LEN, d), 1.0),
        'c_ctx': nrm(ks[3], (d,), 1.0),
        'norm1_g': gain(ks[4], (DEPTH, d)),
        'norm2_g': gain(ks[5], (DEPTH, d)),
        'w_mod': nrm(ks[6], (DEPTH, d, 6 * d), 0.5 * d ** -0.5),
        'b_mod': nrm(ks[7], (DEPTH, 6 * d), 0.02),
        'w_ff1': nrm(ks[8], (DEPTH, d, D_FF), d ** -0.5),
        'w_ff2': nrm(ks[9], (DEPTH, D_FF, d), D_FF ** -0.5),
        'conv_w_pw1': nrm(ks[10], (N_CONV, d, 2 * d), d ** -0.5),
        'conv_w_dw': nrm(ks[11], (N_CONV, CONV_WIDTH, d), CONV_WIDTH ** -0.5),
        'conv_b_dw': nrm(ks[12], (N_CONV, d), 0.02),
        'conv_ln_g': gain(ks[13], (N_CONV, d)),
        'conv_ln_b': nrm(ks[14], (N_CONV, d), 0.02),
        'conv_w_pw2': nrm(ks[15], (N_CONV, d, d), d ** -0.5),
        'gqa_w_qkv': nrm(ks[16], (N_GQA, d, (GQA_HEADS + 2 * GQA_KV_HEADS) * GQA_HEAD_DIM), d ** -0.5),
        'gqa_q_norm': gain(ks[17], (N_GQA, GQA_HEAD_DIM)),
        'gqa_k_norm': gain(ks[18], (N_GQA, GQA_HEAD_DIM)),
        'gqa_w_o': nrm(ks[19], (N_GQA, GQA_HEADS * GQA_HEAD_DIM, d), (GQA_HEADS * GQA_HEAD_DIM) ** -0.5),
        'pool_w': nrm(ks[20], (N_POOL, len(POOL_WINDOWS), POOL_GROUP, POOL_GROUP), POOL_GROUP ** -0.5),
        'pool_scale': gain(ks[21], (N_POOL, d)),
        'mla_w_dq': nrm(ks[22], (N_MLA, d, MLA_Q_LORA), d ** -0.5),
        'mla_q_lora_norm': gain(ks[23], (N_MLA, MLA_Q_LORA)),
        'mla_w_uq': nrm(ks[24], (N_MLA, MLA_Q_LORA, MLA_HEADS * MLA_QK), MLA_Q_LORA ** -0.5),
        'mla_w_dkv': nrm(ks[25], (N_MLA, d, MLA_KV_LORA + MLA_ROPE), d ** -0.5),
        'mla_kv_lora_norm': gain(ks[26], (N_MLA, MLA_KV_LORA)),
        'mla_w_ukv': nrm(ks[27], (N_MLA, MLA_KV_LORA, MLA_HEADS * (MLA_NOPE + MLA_V)), MLA_KV_LORA ** -0.5),
        'mla_q_norm': gain(ks[28], (N_MLA, MLA_QK)),
        'mla_k_norm': gain(ks[29], (N_MLA, MLA_QK)),
        'mla_w_o': nrm(ks[30], (N_MLA, MLA_HEADS * MLA_V, d), (MLA_HEADS * MLA_V) ** -0.5),
    }

def first_block(x, c, ctx, c_ctx, norm1_g, norm2_g, w_mod, b_mod, w_ff1, w_ff2,
              conv_w_pw1, conv_w_dw, conv_b_dw, conv_ln_g, conv_ln_b, conv_w_pw2,
              gqa_w_qkv, gqa_q_norm, gqa_k_norm, gqa_w_o, pool_w, pool_scale,
              mla_w_dq, mla_q_lora_norm, mla_w_uq, mla_w_dkv, mla_kv_lora_norm, mla_w_ukv,
              mla_q_norm, mla_k_norm, mla_w_o):
    seq = x.shape[1]
    rows = seq // GRID_W
    row_ids = jnp.repeat(jnp.arange(rows, dtype=jnp.float32), GRID_W)
    col_ids = jnp.tile(jnp.arange(GRID_W, dtype=jnp.float32), rows)
    tab_gqa = axial_tables(row_ids, col_ids, GQA_HEAD_DIM)
    tab_mla = axial_tables(row_ids, col_ids, MLA_ROPE)

    sc = jax.nn.silu(c)
    scc = jax.nn.silu(c_ctx)
    xl, xc = x, ctx
    for i in range(DEPTH):
        m = i % N_MIXERS
        j = i // N_MIXERS
        with_ctx = i < DEPTH - 1
        mod_l = jnp.split(sc @ w_mod[i] + b_mod[i], 6, axis=-1)
        mod_c = jnp.split(scc @ w_mod[i] + b_mod[i], 6, axis=-1)

        hl = modulate(rms_norm(xl, norm1_g[i]), mod_l[0], mod_l[1])
        hc = modulate(rms_norm(xc, norm1_g[i]), mod_c[0], mod_c[1])
        if m == 0:
            cargs = (conv_w_pw1[j], conv_w_dw[j], conv_b_dw[j], conv_ln_g[j], conv_ln_b[j], conv_w_pw2[j])
            ol = conv_module(hl, *cargs)
            oc = conv_module(hc, *cargs) if with_ctx else None
        elif m == 1:
            ol, oc = gqa_mixer(hl, hc, gqa_w_qkv[j], gqa_q_norm[j], gqa_k_norm[j], gqa_w_o[j],
                               tab_gqa, with_ctx)
        elif m == 2:
            ol = pool_mixer(hl, pool_w[j], pool_scale[j])
            oc = pool_mixer(hc, pool_w[j], pool_scale[j]) if with_ctx else None
        else:
            ol, oc = mla_mixer(hl, hc, mla_w_dq[j], mla_q_lora_norm[j], mla_w_uq[j], mla_w_dkv[j],
                               mla_kv_lora_norm[j], mla_w_ukv[j], mla_q_norm[j], mla_k_norm[j],
                               mla_w_o[j], tab_mla, with_ctx)
        xl = xl + mod_l[2][:, None, :] * ol
        if with_ctx:
            xc = xc + mod_c[2] * oc

        hl = modulate(rms_norm(xl, norm2_g[i]), mod_l[3], mod_l[4])
        xl = xl + mod_l[5][:, None, :] * sq_relu_mlp(hl, w_ff1[i], w_ff2[i])
        if with_ctx:
            hc = modulate(rms_norm(xc, norm2_g[i]), mod_c[3], mod_c[4])
            xc = xc + mod_c[5] * sq_relu_mlp(hc, w_ff1[i], w_ff2[i])
    return xl


DEPTH_2 = 1

EPS = 1e-6
CHUNK = 128
GM_GROUPS = 8
GM_GROUP_DIM = 64
GM_WIDTH = GM_GROUPS * GM_GROUP_DIM
WINDOW = 128
Q_HEADS = 8
KV_HEADS = 2
Q_PER_KV = Q_HEADS // KV_HEADS
HEAD_DIM = 64
ATTN_WIDTH = Q_HEADS * HEAD_DIM
KV_WIDTH = KV_HEADS * HEAD_DIM
REL_BUCKETS = 32
REL_MAX_EXACT = REL_BUCKETS // 2
REL_MAX_DIST = 128
N_GROUPS_MOE = 4
EXPERTS_PER_GROUP = 4
N_EXPERTS = N_GROUPS_MOE * EXPERTS_PER_GROUP
TOP_K = 2
EXPERT_FF = 512
MASK_VALUE = -1e30

SPLIT_SIZES = (GM_WIDTH, GM_WIDTH, ATTN_WIDTH, KV_WIDTH, KV_WIDTH, D_MODEL, D_MODEL)
SPLIT_POINTS = tuple(int(v) for v in np.cumsum(SPLIT_SIZES)[:-1])
IN_WIDTH = int(sum(SPLIT_SIZES))


def rms_norm_2(x, g):
    xf = x.astype(jnp.float32)
    y = xf * lax.rsqrt(jnp.mean(xf * xf, axis=-1, keepdims=True) + EPS)
    return (y * g.astype(jnp.float32)).astype(x.dtype)

def layer_norm_2(x, g):
    xf = x.astype(jnp.float32)
    mu = jnp.mean(xf, axis=-1, keepdims=True)
    xc = xf - mu
    y = xc * lax.rsqrt(jnp.mean(xc * xc, axis=-1, keepdims=True) + EPS)
    return (y * g.astype(jnp.float32)).astype(x.dtype)

def t5_causal_bucket(dist):
    is_small = dist < REL_MAX_EXACT
    nf = jnp.maximum(dist, 1).astype(jnp.float32)
    large = REL_MAX_EXACT + (
        jnp.log(nf / REL_MAX_EXACT) / math.log(REL_MAX_DIST / REL_MAX_EXACT)
        * (REL_BUCKETS - REL_MAX_EXACT)).astype(jnp.int32)
    large = jnp.minimum(large, REL_BUCKETS - 1)
    return jnp.where(is_small, dist, large)

def gmlp_chunk_mixer(u_raw, v_raw, v_norm_g, w_s, b_s):
    B, S, _ = u_raw.shape
    u = jax.nn.gelu(u_raw)
    v = layer_norm_2(jax.nn.gelu(v_raw), v_norm_g)
    v = v.reshape(B, S // CHUNK, CHUNK, GM_GROUPS, GM_GROUP_DIM)
    causal = jnp.tril(jnp.ones((CHUNK, CHUNK), dtype=bool))
    ws = jnp.where(causal[None], w_s, jnp.zeros((), w_s.dtype)).astype(v.dtype)
    sv = jnp.einsum("gts,bcsgd->bctgd", ws, v)
    sv = sv + b_s.T.astype(v.dtype)[None, None, :, :, None]
    return u * sv.reshape(B, S, GM_WIDTH)

def swa_sink_attention(q, k, v, sinks, rel_bias):
    B, S, _ = q.shape
    nb = S // WINDOW
    q = q.reshape(B, nb, WINDOW, KV_HEADS, Q_PER_KV, HEAD_DIM)
    k = k.reshape(B, nb, WINDOW, KV_HEADS, HEAD_DIM)
    v = v.reshape(B, nb, WINDOW, KV_HEADS, HEAD_DIM)
    k_prev = jnp.concatenate([jnp.zeros_like(k[:, :1]), k[:, :-1]], axis=1)
    v_prev = jnp.concatenate([jnp.zeros_like(v[:, :1]), v[:, :-1]], axis=1)
    kb = jnp.concatenate([k_prev, k], axis=2)
    vb = jnp.concatenate([v_prev, v], axis=2)

    scores = jnp.einsum("bnqkgd,bnskd->bnkgqs", q, kb,
                        preferred_element_type=jnp.float32) * (HEAD_DIM ** -0.5)

    qi = jnp.arange(WINDOW, dtype=jnp.int32)[:, None]
    sj = jnp.arange(2 * WINDOW, dtype=jnp.int32)[None, :]
    dist = qi + WINDOW - sj
    in_window = (dist >= 0) & (dist < WINDOW)
    bucket = t5_causal_bucket(jnp.clip(dist, 0, WINDOW - 1))
    bias = rel_bias.astype(jnp.float32)[bucket]
    bias = bias.transpose(2, 0, 1).reshape(KV_HEADS, Q_PER_KV, WINDOW, 2 * WINDOW)
    blk = jnp.arange(nb, dtype=jnp.int32)[:, None, None]
    valid = in_window[None] & ((blk > 0) | (sj[None] >= WINDOW))

    scores = scores + bias[None, None]
    scores = jnp.where(valid[None, :, None, None], scores, MASK_VALUE)
    sink = sinks.astype(jnp.float32).reshape(KV_HEADS, Q_PER_KV)[None, None, :, :, None, None]
    m = jnp.maximum(jnp.max(scores, axis=-1, keepdims=True), sink)
    p = jnp.exp(scores - m)
    denom = jnp.sum(p, axis=-1, keepdims=True) + jnp.exp(sink - m)
    probs = (p / denom).astype(vb.dtype)
    out = jnp.einsum("bnkgqs,bnskd->bnqkgd", probs, vb)
    return out.reshape(B, S, ATTN_WIDTH)

def hierarchical_moe(h, rg_w, rg_b, re_w, re_b, w_gate, w_up, w_down):
    B, S, D = h.shape
    t = h.reshape(-1, D)
    g_logits = jnp.dot(t, rg_w, preferred_element_type=jnp.float32) + rg_b.astype(jnp.float32)
    g_probs = jax.nn.softmax(g_logits, axis=-1)
    g_top_p, g_top_i = lax.top_k(g_probs, 1)
    e_all = jnp.einsum("td,gde->tge", t, re_w,
                       preferred_element_type=jnp.float32) + re_b.astype(jnp.float32)
    e_logits = jnp.take_along_axis(e_all, g_top_i[:, :, None], axis=1)[:, 0]
    e_top_v, e_top_i = lax.top_k(e_logits, TOP_K)
    w_top = jax.nn.softmax(e_top_v, axis=-1) * g_top_p
    expert_id = g_top_i * EXPERTS_PER_GROUP + e_top_i
    combine = jnp.einsum("tk,tke->te", w_top,
                         jax.nn.one_hot(expert_id, N_EXPERTS, dtype=jnp.float32))
    combine = combine.astype(t.dtype)
    out = jnp.zeros_like(t)
    for e in range(N_EXPERTS):
        hid = jax.nn.silu(t @ w_gate[e]) * (t @ w_up[e])
        out = out + combine[:, e:e + 1] * (hid @ w_down[e])
    return out.reshape(B, S, D)

def second_inputs(seed: int = 0) -> dict:
    key = jax.random.key(seed)
    ks = jax.random.split(key, 20)
    f32 = jnp.float32
    nrm = lambda k, shape, scale: jax.random.normal(k, shape, f32) * scale
    L = DEPTH_2
    return {
        "x": jax.random.normal(ks[0], (BATCH, SEQ, D_MODEL), f32),
        "attn_norm_g": 1.0 + nrm(ks[1], (L, D_MODEL), 0.02),
        "w_in": nrm(ks[2], (L, D_MODEL, IN_WIDTH), D_MODEL ** -0.5),
        "gm_v_norm_g": 1.0 + nrm(ks[3], (L, GM_WIDTH), 0.02),
        "gm_w_spatial": nrm(ks[4], (L, GM_GROUPS, CHUNK, CHUNK), CHUNK ** -0.5),
        "gm_b_spatial": 1.0 + nrm(ks[5], (L, GM_GROUPS, CHUNK), 0.02),
        "attn_sinks": nrm(ks[6], (L, Q_HEADS), 0.5),
        "rel_bias": nrm(ks[7], (REL_BUCKETS, Q_HEADS), 0.5),
        "w_proj_a": nrm(ks[8], (L, GM_WIDTH, D_MODEL), GM_WIDTH ** -0.5),
        "w_proj_b": nrm(ks[9], (L, ATTN_WIDTH, D_MODEL), ATTN_WIDTH ** -0.5),
        "w_out": nrm(ks[10], (L, D_MODEL, D_MODEL), D_MODEL ** -0.5),
        "ffn_norm_g": 1.0 + nrm(ks[11], (L, D_MODEL), 0.02),
        "router_group_w": nrm(ks[12], (L, D_MODEL, N_GROUPS_MOE), D_MODEL ** -0.5),
        "router_group_b": nrm(ks[13], (L, N_GROUPS_MOE), 0.01),
        "router_expert_w": nrm(ks[14], (L, N_GROUPS_MOE, D_MODEL, EXPERTS_PER_GROUP), D_MODEL ** -0.5),
        "router_expert_b": nrm(ks[15], (L, N_GROUPS_MOE, EXPERTS_PER_GROUP), 0.01),
        "expert_w_gate": nrm(ks[16], (L, N_EXPERTS, D_MODEL, EXPERT_FF), D_MODEL ** -0.5),
        "expert_w_up": nrm(ks[17], (L, N_EXPERTS, D_MODEL, EXPERT_FF), D_MODEL ** -0.5),
        "expert_w_down": nrm(ks[18], (L, N_EXPERTS, EXPERT_FF, D_MODEL), EXPERT_FF ** -0.5),
        "final_norm_g": 1.0 + nrm(ks[19], (D_MODEL,), 0.02),
    }

def second_block(x, attn_norm_g, w_in, gm_v_norm_g, gm_w_spatial, gm_b_spatial, attn_sinks,
              rel_bias, w_proj_a, w_proj_b, w_out, ffn_norm_g, router_group_w, router_group_b,
              router_expert_w, router_expert_b, expert_w_gate, expert_w_up, expert_w_down,
              final_norm_g):
    h = x
    for l in range(DEPTH_2):
        hn = rms_norm_2(h, attn_norm_g[l])
        proj = hn @ w_in[l]
        u_raw, v_raw, q, k, v, gate_a, gate_b = jnp.split(proj, SPLIT_POINTS, axis=-1)
        a = gmlp_chunk_mixer(u_raw, v_raw, gm_v_norm_g[l], gm_w_spatial[l], gm_b_spatial[l])
        b = swa_sink_attention(q, k, v, attn_sinks[l], rel_bias)
        merged = (jax.nn.sigmoid(gate_a) * (a @ w_proj_a[l])
                  + jax.nn.sigmoid(gate_b) * (b @ w_proj_b[l]))
        h = h + merged @ w_out[l]
        hn = rms_norm_2(h, ffn_norm_g[l])
        h = h + hierarchical_moe(hn, router_group_w[l], router_group_b[l], router_expert_w[l],
                                 router_expert_b[l], expert_w_gate[l], expert_w_up[l],
                                 expert_w_down[l])
    return rms_norm_2(h, final_norm_g)


def setup_inputs(seed=0):
    out = dict(first_inputs(seed))
    for name, value in second_inputs(seed + 1).items():
        if name != "x":
            out[name + "_2"] = value
    return out


def reference(
    x, c, ctx, c_ctx, norm1_g, norm2_g, w_mod, b_mod, w_ff1, w_ff2, conv_w_pw1, conv_w_dw,
    conv_b_dw, conv_ln_g, conv_ln_b, conv_w_pw2, gqa_w_qkv, gqa_q_norm, gqa_k_norm, gqa_w_o,
    pool_w, pool_scale, mla_w_dq, mla_q_lora_norm, mla_w_uq, mla_w_dkv, mla_kv_lora_norm,
    mla_w_ukv, mla_q_norm, mla_k_norm, mla_w_o, attn_norm_g_2, w_in_2, gm_v_norm_g_2,
    gm_w_spatial_2, gm_b_spatial_2, attn_sinks_2, rel_bias_2, w_proj_a_2, w_proj_b_2, w_out_2,
    ffn_norm_g_2, router_group_w_2, router_group_b_2, router_expert_w_2, router_expert_b_2,
    expert_w_gate_2, expert_w_up_2, expert_w_down_2, final_norm_g_2,
):
    x = first_block(
        x, c, ctx, c_ctx, norm1_g, norm2_g, w_mod, b_mod, w_ff1, w_ff2, conv_w_pw1, conv_w_dw,
        conv_b_dw, conv_ln_g, conv_ln_b, conv_w_pw2, gqa_w_qkv, gqa_q_norm, gqa_k_norm, gqa_w_o,
        pool_w, pool_scale, mla_w_dq, mla_q_lora_norm, mla_w_uq, mla_w_dkv, mla_kv_lora_norm,
        mla_w_ukv, mla_q_norm, mla_k_norm, mla_w_o,
    )
    return second_block(
        x, attn_norm_g_2, w_in_2, gm_v_norm_g_2, gm_w_spatial_2, gm_b_spatial_2, attn_sinks_2,
        rel_bias_2, w_proj_a_2, w_proj_b_2, w_out_2, ffn_norm_g_2, router_group_w_2,
        router_group_b_2, router_expert_w_2, router_expert_b_2, expert_w_gate_2, expert_w_up_2,
        expert_w_down_2, final_norm_g_2,
    )


_drawn_inputs = setup_inputs


def setup_inputs(seed=0):
    import zlib

    import numpy as np

    out = dict(_drawn_inputs(seed))
    spreads = {}
    factors = {'ctx': 2.958,
     'norm1_g': 3.973,
     'conv_b_dw': 4.95,
     'conv_ln_g': 2.813,
     'conv_ln_b': 4.475,
     'gqa_q_norm': 8.0,
     'gqa_k_norm': 8.0,
     'attn_norm_g_2': 3.785,
     'gm_v_norm_g_2': 6.774,
     'gm_b_spatial_2': 4.823,
     'attn_sinks_2': 45.508,
     'ffn_norm_g_2': 3.121,
     'router_group_b_2': 4.605,
     'router_expert_b_2': 21.621}
    for name, (base, spread) in spreads.items():
        noise = np.random.default_rng([zlib.crc32(name.encode()), seed]).standard_normal(out[name].shape)
        drawn = base * np.exp(spread * noise) if base else spread * noise
        out[name] = __import__('jax').numpy.asarray(drawn.astype(out[name].dtype))
    for name, factor in factors.items():
        out[name] = (out[name] * factor).astype(out[name].dtype)
    return out
```

```python
from contextlib import ExitStack, contextmanager

import numpy as np

import concourse.bass as bass
from concourse import mybir

F32 = mybir.dt.float32
F32R = mybir.dt.float32r
I32 = mybir.dt.int32
U32 = mybir.dt.uint32
ALU = mybir.AluOpType
ACT = mybir.ActivationFunctionType
AX = mybir.AxisListType

P = 128
D = 1024
KT = D // P
CTX, LAT = 256, 512
TOK = CTX + LAT
NB_C, NB_L = CTX // P, LAT // P
EPS = 1e-6
TAPS = 31
PAD = TAPS // 2
DFF = 4 * D
HD = 64
NEG = -1e30
N_EXP, E_FF = 16, 512
SLOTS_MAX = N_EXP + (2 * LAT - N_EXP) // P
LIST = SLOTS_MAX + 1
RING = 4
BUCKETS = 32
WIN = 128

C_BMOD, C_VEC, C_TAP_A, C_TAP_B = 0, 128, 256, 384
(V_N1, V_N1B, V_N2, V_N2B, V_CB, V_LG, V_LB, V_C, V_CC, V_AN, V_FN) = range(11)
TAP_SPLIT = 15

(M_ID, M_MEAN, M_HEAD, M_ROT, M_DUP0, M_DUP1, M_TRI, M_ONE, M_FLIP, M_SEL) = range(10)
N_MATS = 10


def shape_constants():
    m = np.zeros((N_MATS, P, P), np.float32)
    i = np.arange(P)
    m[M_ID] = np.eye(P)
    m[M_MEAN] = 1.0 / D
    m[M_HEAD] = (i[:, None] // HD == i[None, :] // HD) / float(HD)
    for d in range(P):
        if d % 32 < 16:
            m[M_ROT, d + 16, d] = -1.0
        else:
            m[M_ROT, d - 16, d] = 1.0
        m[M_DUP0, d % HD, d] = 1.0
        m[M_DUP1, HD + d % HD, d] = 1.0
    m[M_TRI] = i[:, None] < i[None, :]
    m[M_ONE] = 1.0
    m[M_FLIP] = (i[:, None] + i[None, :]) == P - 1
    quarter = 16
    inv = (np.float32(10000.0) ** (-np.arange(quarter, dtype=np.float32) / np.float32(quarter))).astype(np.float32)
    t = np.arange(LAT)
    row, col = (t // 64).astype(np.float32), (t % 64).astype(np.float32)
    ang = np.zeros((P, LAT), np.float32)
    for d in range(P):
        ang[d] = (row if (d % HD) < 32 else col) * inv[d % 16]
    rope = np.stack([np.cos(ang), np.sin(ang)]).astype(np.float32)
    one_hot = np.zeros((BUCKETS + 1, 3 * P), np.float32)
    half = BUCKETS // 2
    for c in range(3 * P):
        dist = 2 * WIN - 1 - c
        if 0 <= dist < WIN:
            if dist < half:
                b = dist
            else:
                b = half + int(np.float32(np.log(np.float32(dist) / np.float32(half))
                                          / np.float32(np.log(128 / half)) * np.float32(BUCKETS - half)))
                b = min(b, BUCKETS - 1)
            one_hot[b, c] = 1.0
        else:
            one_hot[BUCKETS, c] = 1.0
    group = np.zeros((8, 4, P), np.float32)
    for g in range(8):
        group[g, g // 2, (g % 2) * HD:(g % 2) * HD + HD] = 1.0
    ramp = np.zeros((P, 64), np.float32)
    ramp[:, 0:16] = np.arange(16) - 16.0
    ramp[:, 16:16 + LIST] = np.arange(LIST)
    ramp[:, 48:52] = np.arange(4) * 128.0
    ids = (i[:, None] + P * np.arange(4)[None, :]).astype(np.int32)
    return {"mats": m, "rope": rope, "one_hot": one_hot, "group": group.reshape(8, 4 * P),
            "ramp": ramp, "ids": ids}


class Program:

    def __init__(self, eng, chain=None, counts="cgqu"):
        self.eng, self.chain, self.counts = eng, chain, counts
        self.n = {"c": 0, "g": 0, "q": 0, "u": 0}
        self.r = {"c": 0, "g": 0, "q": 0, "u": 0}

    def at(self, key, more=0):
        return self.n[key] + more + self.r[key]

    def step(self, ins):
        ins.then_inc(self.chain, 1)
        self.n["c"] += 1
        self.eng.wait_ge(self.chain, self.at("c"))

    def laps(self):
        return self.n["g"] // RING + 1 + self.r["g"]

    @contextmanager
    def loop(self, count, start=0, **per):
        assert per.get("g", 0) % RING == 0
        per = {k: v for k, v in per.items() if k in self.counts}
        n0, r0 = dict(self.n), dict(self.r)
        with self.eng.Fori(start, count) as i:
            for k, v in per.items():
                if v:
                    self.r[k] = r0[k] + (i - start if start else i) * (v // RING if k == "g" else v)
            yield i
            for k in self.counts:
                assert self.n[k] - n0[k] == per.get(k, 0), (k, self.n[k] - n0[k], per)
        self.r = r0
        self.n = {k: n0[k] + (count - start) * per.get(k, 0) for k in self.n}


def build(nc, A, out):
    with ExitStack() as ctx:
        _build(nc, ctx, A, out)


def _build(nc, ctx, A, out):
    place = [16512]

    def region(nbytes):
        at = place[0]
        place[0] += nbytes
        assert place[0] <= 229344, place[0]
        return at

    def sb(name, shape, dt=F32, at=None):
        size = int(np.prod(shape[1:])) * 4
        size += -size % 32
        return nc.alloc_sbuf_tensor_at(name, shape, dt, offset=region(size) if at is None else at)

    class Sems(dict):
        def __missing__(self, name):
            self[name] = ctx.enter_context(nc.semaphore(name))
            return self[name]

    S = Sems()

    x = sb("x", [P, KT, TOK])
    ah_at = region(KT * TOK * 4)
    al_at = region(KT * TOK * 4)
    ah = sb("ah", [P, KT, TOK], F32R, ah_at)
    al = sb("al", [P, KT, TOK], F32R, al_at)
    h_at = region(4 * 4 * TOK * 4)
    u_at = region(KT * TOK * 4)
    raw_at = region(RING * D * 4)
    raw = [sb(f"raw{r}", [P, D], at=raw_at + 4 * D * r) for r in range(RING)]
    whi_at = region(2 * D * 4)
    whi = [sb(f"whi{r}", [P, D], F32R, whi_at + 4 * D * r) for r in range(2)]
    wlo = [sb(f"wlo{r}", [P, D], F32R) for r in range(2)]
    mats = sb("mats", [P, N_MATS - 1, P])
    cols = sb("cols", [P, 512])
    mod = sb("mod", [P, 96, 2])
    silu_c = sb("silu_c", [P, KT, 2])
    msc = sb("msc", [P, 4, KT, 2])
    qk_gain = sb("qk_gain", [P, 2])
    e_at = region(20480)

    hid_hi = [sb(f"hid_hi{b}", [P, 4, TOK], F32R, h_at + b * 4 * TOK * 4) for b in range(2)]
    hid_lo = [sb(f"hid_lo{b}", [P, 4, TOK], F32R, h_at + (2 + b) * 4 * TOK * 4) for b in range(2)]
    sq = sb("sq", [P, KT, TOK], at=h_at)
    y = sb("y", [P, KT, TOK], at=u_at)
    rstd = sb("rstd", [P, TOK], at=e_at)
    tmp = sb("tmp", [P, TOK], at=e_at + TOK * 4)
    tmp2 = sb("tmp2", [P, TOK], at=e_at + 2 * TOK * 4)
    tmp3 = sb("tmp3", [P, TOK], at=e_at + 3 * TOK * 4)
    xin = sb("xin", [P, NB_C + NB_L, D], at=u_at)
    vec_rows = sb("vec_rows", [P, 4, P], at=h_at)
    cv = sb("cv", [P, KT, TOK], at=u_at)
    sig = sb("sig", [P, TOK], at=h_at)
    upb = sb("upb", [P, PAD + CTX + PAD + LAT + PAD], at=h_at + 3072)
    csum = [sb(f"csum{b}", [P, CTX + PAD + LAT], at=h_at + 6400 + 3200 * b) for b in range(2)]
    taps = sb("taps", [P, 32], at=h_at + 12800)
    mu = sb("mu", [P, TOK], at=e_at + 4 * TOK * 4)
    zero_rows = sb("zero_rows", [P, D], at=u_at)
    qf = sb("qf", [P, KT, LAT], at=u_at)
    kf = sb("kf", [P, 2, TOK], at=u_at + KT * LAT * 4)
    vt = sb("vt", [P, 6, 256], at=h_at)
    kdup = sb("kdup", [P, 4, TOK], at=h_at + 6144)
    kst = sb("kst", [P, TOK], at=h_at + 18432)
    vst = sb("vst", [P, 6, HD], at=h_at + 21504)
    qst = sb("qst", [P, 2, LAT], at=h_at + 23040)
    pr = [sb(f"pr{b}", [P, TOK], at=h_at + 27136 + b * 3072) for b in range(2)]
    prt = sb("prt", [P, 6, LAT], at=h_at + 33280)
    stat = sb("stat", [P, 8], at=e_at + 5 * TOK * 4)
    rope = sb("rope", [P, 2, LAT], at=e_at + 16384)
    gu = sb("gu", [P, 4, LAT], at=u_at)
    gv = sb("gv", [P, NB_L, 4 * P], at=u_at + 8192)
    q2 = sb("q2", [P, 4, LAT], at=u_at + 16384)
    sg = sb("sg", [P, 16, LAT], at=h_at)
    kd2 = sb("kd2", [P, 2, P + LAT], at=h_at + 32768)
    v2 = sb("v2", [P, 5, P], at=h_at + 37888)
    k2f = sb("k2f", [P, LAT], at=h_at + 40448)
    bias2 = x[:, :, 0:CTX]
    sc2 = [sb(f"sc2_{b}", [P, 4, 2 * P], at=e_at + 4096 * b) for b in range(2)]
    pt2 = sb("pt2", [P, 4, 2, P], at=e_at + 8192)
    wst = sb("wst", [P, 8, P], at=e_at + 12288)
    bsp = sb("bsp", [P, 4, P], at=e_at + 16384)
    gvn = sb("gvn", [P, LAT], at=e_at + 6144)
    st2 = sb("st2", [P, 2, 32], at=e_at + 18432)
    sinks = sb("sinks", [P, 8], at=e_at + 18688)
    gst = sb("gst", [P, 16], at=e_at + 18720)
    bias_rev = sb("bias_rev", [P, 8, 2 * P], at=u_at)
    ws_in = sb("ws_in", [P, 8, P], at=u_at + 8192)
    rel = sb("rel", [BUCKETS + 1, 8], at=u_at + 12288)
    one_hot = sb("one_hot", [BUCKETS + 1, 3 * P], at=u_at + 12320)
    rel_line = sb("rel_line", [8, 3 * P], at=u_at + 13856)
    bs_rows = sb("bs_rows", [8, P], at=u_at + 15392)
    group = sb("group", [8, 4 * P], at=u_at + 15904)
    mh = sb("mh", [P, KT, LAT], F32R, u_at)
    ml = sb("ml", [P, KT, LAT], F32R, e_at)
    wg = sb("wg", [P, KT, E_FF], at=ah_at)
    wu = sb("wu", [P, KT, E_FF], at=ah_at + 16384)
    wd = sb("wd", [P, 4, D], at=ah_at + 32768)
    ht = sb("ht", [P, NB_L, D], at=raw_at)
    fgain = sb("fgain", [P, D], at=whi_at)
    hn = sb("hn", [P, NB_L, D], at=h_at)
    xg = sb("xg", [P, D], at=h_at + 16384)
    xgt = sb("xgt", [P, KT, P], at=h_at + 20480)
    gate_s = sb("gate_s", [P, E_FF], at=h_at + 24576)
    hidt = sb("hidt", [P, E_FF], at=h_at + 26624)
    hidT = sb("hidT", [P, 4, P], at=h_at + 28672)
    yo = sb("yo", [P, D], at=h_at + 30720)
    rw = sb("rw", [P, KT, 20], at=h_at + 34816)
    rb = sb("rb", [P, 20], at=h_at + 35456)
    ramp = sb("ramp", [P, 64], at=h_at + 35552)
    ids = sb("ids", [P, 4], I32, h_at + 35808)
    lg = sb("lg", [P, 4, 20], at=h_at + 35840)
    rt = sb("rt", [P, 24, 64], at=h_at + 36160)
    pos_i = sb("pos_i", [P, 8], U32, h_at + 42304)
    idx_all = sb("idx_all", [P, LIST], I32, h_at + 42336)
    idx1 = sb("idx1", [P, 1], U32, h_at + 42464)
    meta = sb("meta", [P, 32], I32, h_at + 42496)
    zero_i = sb("zero_i", [P, LIST], I32, h_at + 42624)
    wk = sb("wk", [P, 2, NB_L], at=h_at + 42752)
    fin_s = sb("fin_s", [P, 8], at=h_at + 42784)
    ga = [sb(f"ga{n}", [P, D], at=ah_at + 4096 * n) for n in range(8)]
    osum = [sb(f"osum{n}", [P, D], at=ah_at + 4096 * (8 + n)) for n in range(4)]

    def pb(name):
        return ctx.enter_context(nc.psum_tensor(name, [P, 1024], F32))

    acc = [pb("acc0"), pb("acc1")]
    pa, pbk = pb("pa"), pb("pb")

    rel_t = nc.dram_tensor("rel_line_dram", [8, 3 * P], F32, kind="Internal")
    hn_d = nc.dram_tensor("normed_rows_dram", [LAT, D], F32, kind="Internal").ap()
    list_d = nc.dram_tensor("slot_list_dram", [LIST * P, 1], I32, kind="Internal").ap()
    yo_d = nc.dram_tensor("expert_rows_dram", [LIST * P, D], F32, kind="Internal").ap()


    FULL = [(0, CTX, 1), (CTX, TOK, 0)]
    LATENT = [(CTX, TOK, 0)]

    def token_cols(bank, c0=0):
        return bank[:, CTX + c0:CTX + TOK]

    def slots(e, n, one, units=1, steps=0):
        def slot(i):
            one(i)
            e.n["g"] += 1
            e.n["q"] += 1

        turns = n // RING
        if turns > 1:
            with e.loop(turns, g=RING, q=RING, u=RING * units, c=RING * steps) as i:
                for j in range(RING):
                    slot(i * RING + j)
        else:
            turns = 0
        for j in range(turns * RING, n):
            slot(j)

    def split_only(e, n, one):
        with e.loop(n // RING, g=RING, q=RING) as i:
            for _ in range(RING):
                one()
                e.n["g"] += 1
                e.n["q"] += 1

    def qk_units(e, unit, steps=0):
        with e.loop(KT, c=steps) as i:
            unit(i, tile_of(qf, i, slice(0, LAT)), LAT)
        for j in range(2):
            unit(KT + j, kf[:, j, CTX:TOK], LAT)
        for j in range(2):
            unit(KT + 2 + j, kf[:, j, 0:CTX], CTX)

    def feed_forward(e, up, down, up_steps=0):
        def four(one, chunk, b):
            for j in range(4):
                one(chunk, j, b)
                e.n["g"] += 1
                e.n["q"] += 1

        four(up, 0, 0)
        with e.loop(3, g=16, q=16, u=24, c=8 * up_steps) as i:
            four(up, i * 2 + 1, 1)
            four(down, i * 2, 0)
            four(up, i * 2 + 2, 0)
            four(down, i * 2 + 1, 1)
        four(up, 7, 1)
        four(down, 6, 0)
        four(down, 7, 1)

    def load_slot(e, src, k):
        r = e.n["g"] % RING
        e.eng.wait_ge(S["lo_ready"], e.at("q", 1 - RING))
        e.eng.dma_start(raw[r][:, :].rearrange("p (k n) -> p k n", k=k),
                        src.rearrange("(k p) n -> p k n", p=P)).then_inc(S[f"raw_in{r}"], 16)

    def split_high(e):
        r = e.n["g"] % RING
        e.eng.wait_ge(S[f"raw_in{r}"], 16 * e.laps() if isinstance(e.laps(), int) else e.laps() * 16)
        e.eng.wait_ge(S["split_started"], e.at("q", 1))
        e.eng.activation(whi[e.n["q"] % 2][:, :], raw[r][:, :], ACT.Copy).then_inc(S["hi_ready"], 1)

    def split_low(e):
        b = e.n["q"] % 2
        e.eng.wait_ge(S["hi_ready"], e.at("q", 1))
        e.eng.tensor_tensor(wlo[b][:, :], raw[e.n["g"] % RING][:, :], whi[b][:, :].bitcast(F32),
                            ALU.subtract).then_inc(S["lo_ready"], 1)

    def run_group(e, group, first=None, last=None):
        keys = [g[0] for g in group]
        ins = None
        for n, (key, o, w, m) in enumerate(group):
            ins = e.eng.matmul(o, w, m, start=keys.index(key) == n,
                               stop=len(keys) - 1 - keys[::-1].index(key) == n)
            if n == 0 and first:
                ins.then_inc(S[first], 1)
        if last:
            ins.then_inc(S[last], 1)

    def product(e, act_hi, act_lo, segs, k=KT, shift=0, out0=CTX):
        h, l = whi[e.n["q"] % 2], wlo[e.n["q"] % 2]
        e.eng.wait_ge(S["lo_ready"], e.at("q", 1))
        wide = D // k
        for j in range(KT // k):
            bank = acc[e.n["u"] % 2]
            group = []
            for t in range(k):
                c = t * wide + j * P
                for w, a in ((h, act_hi), (h, act_lo), (l, act_hi)):
                    for s0, s1, _ in segs:
                        group.append((s0, bank[:, out0 + s0:out0 + s1], w[:, c:c + P], a[:, t + shift, s0:s1]))
            e.eng.wait_ge(S["acc_free"], e.at("u", 1))
            run_group(e, group, "split_started" if j == 0 else None, "acc_ready")
            e.n["u"] += 1

    def product_rows(e, blocks):
        h, l = whi[e.n["q"] % 2], wlo[e.n["q"] % 2]
        e.eng.wait_ge(S["lo_ready"], e.at("q", 1))
        e.eng.wait_ge(S["acc_free"], e.at("u", 1))
        bank = acc[e.n["u"] % 2]
        group = [(b, bank[:, CTX + b * P:CTX + b * P + P], a[:, t, b * P:b * P + P], w[:, t * P:t * P + P])
                 for b in blocks for t in range(KT) for a, w in ((ah, h), (ah, l), (al, h))]
        run_group(e, group, "split_started", "acc_ready")
        e.n["u"] += 1

    def sum_over_channels(e, src, segs, ready, done0):
        for t in range(KT):
            for sem in ready:
                e.eng.wait_ge(S[sem], done0 + t + 1)
            for s0, s1, _ in segs:
                ins = e.eng.matmul(pa[:, CTX + s0:CTX + s1], mats[:, M_MEAN, :], src[:, t, s0:s1],
                                   start=t == 0, stop=t == KT - 1)
        ins.then_inc(S["stat_ready"], 1)

    def take_unit(e):
        e.eng.wait_ge(S["acc_ready"], e.at("u", 1))
        return acc[e.n["u"] % 2]

    def free_unit(e, ins, then_read=False):
        ins.then_inc(S["acc_free"], 1)
        e.n["u"] += 1
        if then_read:
            e.eng.wait_ge(S["acc_free"], e.at("u", 2))

    def add_to_stream(e, tile_at, gate, segs):
        bank = take_unit(e)
        for s0, s1, v in segs:
            ins = e.eng.scalar_tensor_tensor(
                out=x[:, tile_at, s0:s1], in0=bank[:, CTX + s0:CTX + s1], scalar=mod[:, gate, v:v + 1],
                in1=x[:, tile_at, s0:s1], op0=ALU.mult, op1=ALU.add)
        free_unit(e, ins)

    def column(i):
        return bass.ds(i, 1)

    def tile_of(ap, i, *rest):
        return ap[(slice(None), bass.ds(i, 1)) + rest].rearrange("p a t -> p (a t)")

    def norm_act(e, k, segs, k_root, split=True):
        c0 = segs[0][0]
        e.eng.wait_ge(S["acc_free"], e.at("u", 2))
        with e.loop(KT) as i:
            e.eng.activation(tile_of(sq, i, slice(c0, TOK)), tile_of(x, i, slice(c0, TOK)),
                             ACT.Square).then_inc(S["sq_ready"], 1)
        root(e, k_root, rstd[:, c0:TOK])
        if split:
            with e.loop(KT) as i:
                e.eng.wait_ge(S["y_ready"], i + (KT * max(k - 1, 0) + 1))
                e.eng.activation(tile_of(ah, i, slice(c0, TOK)), tile_of(y, i, slice(c0, TOK)),
                                 ACT.Copy).then_inc(S["ah_ready"], 1)

    def low_pool(e, k, segs):
        c0 = segs[0][0]
        with e.loop(KT) as i:
            e.eng.wait_ge(S["ah_ready"], i + (KT * k + 1))
            e.eng.tensor_tensor(tile_of(al, i, slice(c0, TOK)), tile_of(y, i, slice(c0, TOK)),
                                tile_of(ah, i, slice(c0, TOK)).bitcast(F32),
                                ALU.subtract).then_inc(S["al_ready"], 1)

    def reciprocal_for_root(e, ap):
        e.eng.reciprocal(ap, ap).then_inc(S["root_in"], 1)

    def root(e, k, ap):
        e.eng.wait_ge(S["root_in"], k)
        e.eng.activation(ap, ap, ACT.Sqrt).then_inc(S["root_out"], 1)

    def inverse_root(e, stats, segs, k_root):
        c0 = segs[0][0]
        e.eng.wait_ge(S["stat_ready"], stats)
        e.step(e.eng.tensor_scalar(rstd[:, c0:TOK], token_cols(pa, c0), EPS, None, ALU.add))
        reciprocal_for_root(e, rstd[:, c0:TOK])
        e.eng.wait_ge(S["root_out"], k_root)

    def norm_dve(e, stats, segs, k_root, y0, scale=None, shift=None, gain=None):
        c0 = segs[0][0]
        inverse_root(e, stats, segs, k_root)
        if gain is not None:
            with e.loop(KT) as i:
                e.eng.scalar_tensor_tensor(
                    out=tile_of(y, i, slice(c0, TOK)), in0=tile_of(x, i, slice(c0, TOK)),
                    scalar=cols[:, column(i + gain)], in1=rstd[:, c0:TOK],
                    op0=ALU.mult, op1=ALU.mult).then_inc(S["y_ready"], 1)
            return
        with e.loop(KT, c=1) as i:
            e.step(e.eng.tensor_tensor(tmp[:, c0:TOK], tile_of(x, i, slice(c0, TOK)), rstd[:, c0:TOK],
                                       ALU.mult))
            for s0, s1, v in segs:
                ins = e.eng.tensor_scalar(
                    tile_of(y, i, slice(s0, s1)), tmp[:, s0:s1], msc[:, scale, column(i), v],
                    mod[:, column(i + shift), v], ALU.mult, ALU.add)
            ins.then_inc(S["y_ready"], 1)
            e.eng.wait_ge(S["y_ready"], i + (y0 + 1))


    U_TOTAL = 6 + 16 + 8 + 96 + 12 + 8 + 96 + 30 + 16 + 8
    ctx.enter_context(nc.allow_non_contiguous_dma(reason="short rows of constants"))
    block = ctx.enter_context(nc.Block())

    @block.sync
    def _(sp):
        e = Program(sp, counts="gq")
        sp.dma_start(xin[:, 0:NB_C, :], A["ctx"][0].rearrange("(b p) d -> p b d", p=P)).then_inc(S["x_in"], 16)
        sp.dma_start(xin[:, NB_C:, :], A["x"][0].rearrange("(b p) d -> p b d", p=P)).then_inc(S["x_in"], 16)

        def load_direct(m, layer, wait):
            if wait is not None:
                sp.wait_ge(S["direct_done"], wait)
            r = e.n["g"] % RING
            sp.dma_start(raw[r][:, :].rearrange("p (k n) -> p k n", k=KT),
                         A["w_mod"][layer, :, bass.ds(m * P, P)].rearrange("(k p) n -> p k n", p=P)
                         ).then_inc(S[f"raw_in{r}"], 16)
            e.n["g"] += 1

        for m in range(RING):
            load_direct(m, 0, None)
        with e.loop(4, start=1, g=RING) as i:
            for j in range(RING):
                load_direct(i * 4 + j, 0, i * 4 + (j - 3))
        pw1 = A["conv_w_pw1"][0]
        with e.loop(KT, g=12, q=2) as i:
            for j in range(2):
                sp.wait_ge(S["direct_done"], i * 10 + (13 + j))
                r = e.n["g"] % RING
                sp.dma_start(raw[r][:, :].rearrange("p (k n) -> p k n", k=KT),
                             pw1[:, bass.ds(i * P + j * D, P)].rearrange("(k p) n -> p k n", p=P)
                             ).then_inc(S[f"raw_in{r}"], 16)
                e.n["g"] += 1
                e.n["q"] += 1
            for j in range(10):
                if j in (2, 3):
                    sp.wait_ge(S["lo_ready"], i * 2 + (j - 1))
                    wait = None
                elif j < 2:
                    wait = i * 10 + (15 + j)
                else:
                    wait = i * 10 + (16 + j - 3)
                if j < 4:
                    load_direct(i * 4 + (16 + j), 0, wait)
                else:
                    load_direct(i * 6 + (j - 4), 1, wait)
        sp.wait_ge(S["direct_done"], 96)
        slots(e, KT, lambda i: load_slot(e, A["conv_w_pw2"][0][:, bass.ds(i * P, P)], KT))

        def load_ff(layer):
            up = A["w_ff1"][layer]
            down = A["w_ff2"][layer]
            feed_forward(
                e, lambda c, j, b: load_slot(e, up[:, bass.ds(c * 512 + j * P, P)], KT),
                lambda c, j, b: load_slot(e, down[bass.ds(c * 512, 512), j * 256:j * 256 + 256], 4))

        load_ff(0)
        slots(e, 12, lambda i: load_slot(e, A["gqa_w_qkv"][0][:, bass.ds(i * P, P)], KT))
        slots(e, KT, lambda i: load_slot(e, A["gqa_w_o"][0][:, bass.ds(i * P, P)], KT))
        load_ff(1)
        sp.wait_ge(S["al_ready"], KT * 5)
        sp.wait_ge(S["mask_row"], 1)
        for dst, src in ((rel[0:BUCKETS, :], A["rel_bias_2"]), (one_hot[:, :], A["one_hot"]),
                         (ws_in[:, :, :], A["gm_w_spatial_2"][0].rearrange("g t s -> t g s")),
                         (bs_rows[:, :], A["gm_b_spatial_2"][0]), (group[:, :], A["group"])):
            sp.dma_start(dst, src).then_inc(S["prep_in"], 16)
        sp.wait_ge(S["line_ready"], 1)
        sp.dma_start(rel_t.ap(), rel_line[:, :]).then_inc(S["line_out"], 16)
        sp.wait_ge(S["line_out"], 16)
        sp.dma_start(bias_rev[:, :, :], bass.AP(rel_t, 0, [[1, P], [3 * P, 8], [1, 2 * P]])).then_inc(S["rev_in"], 16)
        sp.dma_start(gvn[:, :], A["gm_v_norm_g_2"].to_broadcast([P, LAT])).then_inc(S["gains_in"], 16)
        sp.dma_start(sinks[:, :], A["attn_sinks_2"].to_broadcast([P, 8])).then_inc(S["gains_in"], 16)
        slots(e, 30, lambda i: load_slot(e, A["w_in_2"][0][:, bass.ds(i * P, P)], KT))

        def load_pair(i):
            pass
        with e.loop(2, g=4, q=4) as i:
            for s in range(2):
                for w in ("w_proj_a_2", "w_proj_b_2"):
                    load_slot(e, A[w][0][:, bass.ds(i * 512 + s * 256, 256)], 4)
                    e.n["g"] += 1
                    e.n["q"] += 1
        slots(e, KT, lambda i: load_slot(e, A["w_out_2"][0][:, bass.ds(i * P, P)], KT))
        sp.wait_ge(S["acc_ready"], U_TOTAL)
        sp.dma_start(rw[:, :, 0:4], A["router_group_w_2"][0].rearrange("(k p) n -> p k n", p=P)).then_inc(S["route_in"], 16)
        for g in range(4):
            sp.dma_start(rw[:, :, 4 + 4 * g:8 + 4 * g],
                         A["router_expert_w_2"][0, g].rearrange("(k p) n -> p k n", p=P)).then_inc(S["route_in"], 16)
        sp.dma_start(rb[:, 0:4], A["router_group_b_2"].to_broadcast([P, 4])).then_inc(S["route_in"], 16)
        sp.dma_start(rb[:, 4:20], A["router_expert_b_2"].rearrange("l g e -> l (g e)").to_broadcast([P, 16])
                     ).then_inc(S["route_in"], 16)
        sp.dma_start(ramp[:, :], A["ramp"]).then_inc(S["route_in"], 16)
        sp.dma_start(ids[:, :], A["ids"]).then_inc(S["route_in"], 16)
        sp.dma_start(fgain[:, :], A["final_norm_g_2"].rearrange("(a d) -> a d", a=1).to_broadcast([P, D])
                     ).then_inc(S["route_in"], 16)
        sp.wait_ge(S["hn_ready"], NB_L)
        sp.dma_start(hn_d.rearrange("(b p) d -> p b d", p=P), hn[:, :, :]).then_inc(S["hn_out"], 16)
        sp.wait_ge(S["meta_ready"], 1)
        n_blocks = sp.value_load(meta[0:1, LIST:LIST + 1], min_val=2 * LAT // P, max_val=SLOTS_MAX)
        with sp.Fori(0, n_blocks) as i:
            ex = sp.value_load(meta[0:1, bass.ds(i, 1)], min_val=0, max_val=N_EXP - 1)
            sp.wait_ge(S["gate_done"], i + 1)
            sp.dma_start(wg[:, :, :], A["expert_w_gate_2"][0, bass.ds(ex, 1)].rearrange(
                "e (p k) n -> p (e k) n", k=KT)).then_inc(S["wg_in"], 16)
            sp.wait_ge(S["up_done"], i + 1)
            sp.dma_start(wu[:, :, :], A["expert_w_up_2"][0, bass.ds(ex, 1)].rearrange(
                "e (p k) n -> p (e k) n", k=KT)).then_inc(S["wu_in"], 16)
            sp.wait_ge(S["down_done"], i + 1)
            sp.dma_start(wd[:, :, :], A["expert_w_down_2"][0, bass.ds(ex, 1)].rearrange(
                "e (p k) n -> p (e k) n", k=4)).then_inc(S["wd_in"], 16)
        for b in range(NB_L):
            sp.wait_ge(S["final_ready"], b + 1)
            sp.dma_start(out[0, b * P:b * P + P, :], osum[b][:, :]).then_inc(S["stored"], 16)
        sp.wait_ge(S["stored"], 16 * NB_L)

    @block.scalar
    def _(act):
        e = Program(act, S["act_chain"])
        vectors = [("norm1_g", 2), ("norm2_g", 2), ("conv_b_dw", 1), ("conv_ln_g", 1), ("conv_ln_b", 1),
                   ("c", 1), ("c_ctx", 1), ("attn_norm_g_2", 1), ("ffn_norm_g_2", 1)]
        act.dma_start(mats[:, :, :], A["mats"][0:N_MATS - 1].rearrange("n p q -> p n q")).then_inc(S["consts_in"], 16)
        act.dma_start(vec_rows[0:96, 0, :], A["b_mod"].rearrange("l (m p) -> (l m) p", p=P)).then_inc(S["consts_in"], 16)
        row = 0
        for name, count in vectors:
            src = A[name].rearrange("(c p) -> c p", p=P) if name == "c_ctx" else \
                A[name].rearrange("l (c p) -> (l c) p", p=P)
            act.dma_start(vec_rows[row:row + 8 * count, 1, :], src).then_inc(S["consts_in"], 16)
            row += 8 * count
        dw = A["conv_w_dw"][0].rearrange("t (c p) -> (t c) p", p=P)
        act.dma_start(vec_rows[0:120, 2, :], dw[0:120, :]).then_inc(S["consts_in"], 16)
        act.dma_start(vec_rows[0:128, 3, :], dw[120:248, :]).then_inc(S["consts_in"], 16)
        act.dma_start(rope[:, :, :], A["rope"].rearrange("n p t -> p n t")).then_inc(S["consts_in"], 16)
        for n, name in enumerate(("gqa_q_norm", "gqa_k_norm")):
            for h in range(2):
                act.dma_start(qk_gain[HD * h:HD * h + HD, n:n + 1],
                              A[name].rearrange("l (d o) -> (l d) o", o=1)).then_inc(S["consts_in"], 16)
        act.wait_ge(S["cols_ready"], 1)
        for v, c in enumerate((V_C, V_CC)):
            act.activation(silu_c[:, :, v], cols[:, C_VEC + 8 * c:C_VEC + 8 * c + 8], ACT.Silu
                           ).then_inc(S["silu_ready"], 1)
        e.n["g"] += 16
        e.n["u"] += NB_C + NB_L
        norm_act(e, 0, FULL, 1)
        with e.loop(KT, g=12, q=2, u=2) as i:
            for _ in range(2):
                split_high(e)
                e.n["g"] += 1
                e.n["q"] += 1
            e.n["g"] += 10
            e.n["u"] += 1
            act.wait_ge(S["acc_ready"], e.at("u", 1))
            act.activation(sig[:, :], token_cols(acc[e.n["u"] % 2]), ACT.Sigmoid).then_inc(S["sig_ready"], 1)
            e.n["u"] += 1
        with e.loop(KT) as i:
            act.wait_ge(S["centred"], i + 1)
            act.activation(tile_of(sq, i, slice(0, TOK)), tile_of(cv, i, slice(0, TOK)), ACT.Square
                           ).then_inc(S["sq_ready"], 1)
        root(e, 2, rstd[:, :])
        with e.loop(KT, c=1) as i:
            act.wait_ge(S["ln_ready"], i + 1)
            e.step(act.activation(tile_of(y, i, slice(0, TOK)), tile_of(cv, i, slice(0, TOK)), ACT.Silu,
                                  bias=cols[:, column(i + (C_VEC + 8 * V_LB))],
                                  scale=cols[:, column(i + (C_VEC + 8 * V_LG))]))
            act.activation(tile_of(ah, i, slice(0, TOK)), tile_of(y, i, slice(0, TOK)), ACT.Copy
                           ).then_inc(S["ah_ready"], 1)

        def high(*_):
            split_high(e)

        slots(e, KT, high, units=0)
        e.n["u"] += KT
        norm_act(e, 2, FULL, 3)

        def high_ff():
            u0 = e.n["u"]
            split_only(e, 64, high)
            e.n["u"] = u0 + 96

        high_ff()
        norm_act(e, 3, FULL, 4)
        slots(e, 12, high, units=0)
        e.n["u"] += 12
        act.wait_ge(S["acc_free"], e.at("u", 2))

        def squares(r, src, cols_n):
            act.wait_ge(S["qk_stat"], r + 1)
            act.activation(tmp2[:, 0:cols_n], src, ACT.Square).then_inc(S["qk_sq"], 1)
            root(e, r + 5, rstd[:, 0:cols_n])

        qk_units(e, squares)
        with e.loop(4) as i:
            def exps(m):
                act.wait_ge(S["nmax_ready"], i * 16 + (m + 1))
                if m >= 2:
                    act.wait_ge(S["turned"], i * 16 + (m - 1))
                b = m % 2
                act.activation(pr[b][:, :], acc[b][:, 0:TOK], ACT.Exp, bias=stat[:, 4 * b + 1:4 * b + 2],
                               scale=HD ** -0.5, accum_out=stat[:, 4 * b + 2:4 * b + 3]).then_inc(S["exp_done"], 1)

            exps(0)
            for m in range(16):
                if m + 1 < 16:
                    exps(m + 1)
                act.wait_ge(S["turned"], i * 16 + (m + 1))
                qb = m % 4
                act.activation(prt[:, :, qb * P:qb * P + P],
                               pa[:, 0:TOK].rearrange("p (k q) -> p k q", q=P), ACT.Copy).then_inc(S["prt_ready"], 1)
        slots(e, KT, high, units=0)
        e.n["u"] += KT
        norm_act(e, 4, LATENT, 17)
        high_ff()
        norm_act(e, 5, LATENT, 18)
        for _ in range(14):
            high()
            e.n["g"] += 1
            e.n["q"] += 1
            e.n["u"] += 1
        act.wait_ge(S["acc_free"], e.at("u", -6 + 2))
        for j in range(4):
            act.activation(gv[:, j, :], gv[:, j, :], ACT.Gelu_apprx_tanh).then_inc(S["gelu_done"], 1)
        for j in range(4):
            act.activation(gu[:, j, :], gu[:, j, :], ACT.Gelu_apprx_tanh).then_inc(S["gelu_done"], 1)
        with e.loop(4, g=4, q=4, u=4) as i:
            for j in range(4):
                high()
                e.n["g"] += 1
                e.n["q"] += 1
                e.n["u"] += 1
        root(e, 19, gst[:, 12:16])
        act.wait_ge(S["acc_free"], e.at("u", 2))
        with e.loop(16) as i:
            act.activation(tile_of(sg, i, slice(0, LAT)), tile_of(sg, i, slice(0, LAT)), ACT.Sigmoid
                           ).then_inc(S["gates_ready"], 1)
        for h in range(8):
            b = h % 2
            act.wait_ge(S["nm2_ready"], h + 1)
            for blk in range(4):
                act.activation(sc2[b][:, blk, :], sc2[b][:, blk, :], ACT.Exp, bias=st2[:, b, 4 + blk:5 + blk],
                               accum_out=st2[:, b, 8 + blk:9 + blk])
            act.activation(st2[:, b, 12:16], st2[:, b, 4:8], ACT.Exp, bias=sinks[:, h:h + 1]
                           ).then_inc(S["exp2_done"], 1)
            act.wait_ge(S["turned2"], h + 1)
            act.activation(pt2[:, :, :, :].rearrange("p a b q -> p (a b q)"), pa[:, :], ACT.Copy
                           ).then_inc(S["pt2_ready"], 1)
        with e.loop(2, g=4, q=4, u=8) as i:
            for j in range(4):
                high()
                e.n["g"] += 1
                e.n["q"] += 1
                e.n["u"] += 2
        slots(e, KT, high, units=0)
        e.n["u"] += KT
        norm_act(e, 6, LATENT, 20, split=False)
        act.wait_ge(S["route_args"], 1)
        act.activation(rt[:, 1, 0:20], rt[:, 0, 0:20], ACT.Exp).then_inc(S["route_exp"], 1)
        act.sem_inc(S["yo_out"], 16)
        act.wait_ge(S["meta_ready"], 1)
        n_blocks = act.value_load(meta[0:1, LIST:LIST + 1], min_val=2 * LAT // P, max_val=SLOTS_MAX)
        with act.Fori(0, n_blocks) as i:
            act.wait_ge(S["gate_done"], i + 2)
            act.activation(gate_s[:, :], acc[0][:, 0:E_FF], ACT.Silu).then_inc(S["silu_gate"], 1)
            act.wait_ge(S["down_done"], i + 2)
            act.wait_ge(S["yo_out"], i * 16 + 16)
            act.activation(yo[:, 0:512], pbk[:, 0:512], ACT.Copy).then_inc(S["yo_act"], 1)
            act.wait_ge(S["yo_act"], i + 1)
            act.wait_ge(S["yo_dve"], i + 2)
            act.dma_start(yo_d[bass.ds(i * P, P), :], yo[:, :]).then_inc(S["yo_out"], 16)
        for b in range(NB_L):
            act.wait_ge(S["osum_ready"], b + 1)
            act.activation(ga[2 * b][:, :], osum[b][:, :], ACT.Square, accum_out=fin_s[:, b:b + 1]
                           ).then_inc(S["fin_sq"], 1)
            root(e, 21 + b, fin_s[:, 4 + b:5 + b])

    @block.gpsimd
    def _(pool):
        e = Program(pool, S["pool_chain"], "cgq")
        low_pool(e, 0, FULL)
        e.n["g"] += 16
        with e.loop(KT, g=12, q=2) as i:
            for _ in range(2):
                split_low(e)
                e.n["g"] += 1
                e.n["q"] += 1
            e.n["g"] += 10
        low_pool(e, 1, FULL)

        def low(*_):
            split_low(e)

        slots(e, KT, low, units=0)
        low_pool(e, 2, FULL)
        pool.wait_ge(S["zero_rows_ready"], 1)
        pool.dma_start(yo_d.rearrange("(j p) d -> p j d", p=P),
                       zero_rows[:, :].unsqueeze(1).to_broadcast([P, LIST, D])).then_inc(S["rows_zeroed"], 16)
        split_only(e, 64, low)
        low_pool(e, 3, FULL)
        slots(e, 12, low, units=0)
        slots(e, KT, low, units=0)
        low_pool(e, 4, LATENT)
        split_only(e, 64, low)
        pool.wait_ge(S["wst_ready"], 1)
        pool.affine_select(out=wst[:, :, :], in_=wst[:, :, :], compare_op=ALU.is_ge, fill=0.0, base=0,
                           pattern=[[0, 8], [1, P]], channel_multiplier=-1).then_inc(S["wst_masked"], 1)
        low_pool(e, 5, LATENT)
        split_only(e, 28, low)
        for _ in range(2):
            low()
            e.n["g"] += 1
            e.n["q"] += 1
        slots(e, KT, low, units=0)
        slots(e, KT, low, units=0)
        pool.wait_ge(S["acc_free"], U_TOTAL + 2)
        pool.memset(zero_i[:, :], 0).then_inc(S["zeroed"], 1)
        pool.wait_ge(S["zeroed"], 1)
        pool.dma_start(list_d.rearrange("(p j) o -> p (j o)", p=P), zero_i[:, :]).then_inc(S["list_zero"], 16)
        pool.wait_ge(S["list_zero"], 16)
        pool.wait_ge(S["pos_ready"], 1)
        pool.wait_ge(S["route_in"], 160)
        for n in range(2 * NB_L):
            pool.indirect_dma_start(
                out=list_d, out_offset=bass.IndirectOffsetOnAxis(ap=pos_i[:, n:n + 1], axis=0),
                in_=ids[:, n % NB_L:n % NB_L + 1], in_offset=None).then_inc(S["scattered"], 16)
            pool.wait_ge(S["scattered"], 16 * (n + 1))
        pool.dma_start(idx_all[:, :], list_d.rearrange("(j p) o -> p (j o)", p=P)).then_inc(S["idx_in"], 16)
        pool.wait_ge(S["idx_in"], 16)
        pool.wait_ge(S["hn_out"], 16)
        pool.wait_ge(S["meta_ready"], 1)
        n_blocks = pool.value_load(meta[0:1, LIST:LIST + 1], min_val=2 * LAT // P, max_val=SLOTS_MAX)
        with pool.Fori(0, n_blocks + 1) as i:
            pool.tensor_copy(idx1[:, :], idx_all[:, column(i)].bitcast(U32)).then_inc(S["idx_ready"], 1)
            pool.wait_ge(S["idx_ready"], i + 1)
            pool.wait_ge(S["xg_turned"], i + 1)
            pool.sem_inc(S["gathers"], 1)
            pool.indirect_dma_start(
                out=xg[:, :], out_offset=None, in_=hn_d,
                in_offset=bass.IndirectOffsetOnAxis(ap=idx1[:, 0:1], axis=0)).then_inc(S["xg_in"], 16)
            pool.wait_ge(S["xg_in"], i * 16 + 16)
        pool.wait_ge(S["yo_out"], (n_blocks + 1) * 16)
        pool.sem_inc(S["gathers"], 1)
        for n in range(NB_L):
            for k in range(2):
                pool.indirect_dma_start(
                    out=ga[2 * n + k][:, :], out_offset=None, in_=yo_d,
                    in_offset=bass.IndirectOffsetOnAxis(ap=pos_i[:, k * NB_L + n:k * NB_L + n + 1], axis=0)
                ).then_inc(S[f"rows_in{n}"], 16)

    @block.vector
    def _(dve):
        e = Program(dve, S["dve_chain"], "cu")
        TT, TS, STT = dve.tensor_tensor, dve.tensor_scalar, dve.scalar_tensor_tensor
        dve.sem_inc(S["acc_free"], 2)
        dve.sem_inc(S["mod_free"], 1)
        dve.sem_inc(S["yo_dve"], 1)
        dve.wait_ge(S["vec_turned"], 1)
        for n, rows in enumerate((96, 88, 120, 128)):
            ins = dve.tensor_copy(cols[:, P * n:P * n + rows], pbk[:, P * n:P * n + rows])
        ins.then_inc(S["cols_ready"], 1)
        dve.wait_ge(S["cols_ready"], 1)
        for b in range(NB_C + NB_L):
            bank = take_unit(e)
            free_unit(e, dve.tensor_copy(x[:, :, b * P:b * P + P], bank[:, :].rearrange("p (k t) -> p k t", t=P)))

        def modulation(at, ps, n, index):
            return TT(mod[:, bass.ds(at, n), :], pbk[:, ps:ps + 2 * n].rearrange("p (n v) -> p n v", v=2),
                      cols[:, bass.ds(at, n)].unsqueeze(2).to_broadcast([P, n, 2]), ALU.add)

        def scales(n, layer, chunk, gain):
            return STT(out=msc[:, n, :, :], in0=mod[:, layer * 48 + chunk * 8:layer * 48 + chunk * 8 + 8, :],
                       scalar=1.0, in1=cols[:, C_VEC + 8 * gain:C_VEC + 8 * gain + 8].unsqueeze(2).to_broadcast([P, KT, 2]),
                       op0=ALU.add, op1=ALU.mult)

        with e.loop(4) as i:
            dve.wait_ge(S["direct_done"], i * 4 + 4)
            modulation(i * 4, 0, 4, None).then_inc(S["mod_free"], 1)
        dve.wait_ge(S["mod_free"], 5)
        e.step(scales(0, 0, 1, V_N1))
        norm_dve(e, 1, FULL, 1, 0, scale=0, shift=0)
        e.step(dve.memset(upb[:, :], 0.0))
        tap_a = cols[:, C_TAP_A:C_TAP_A + 8 * TAP_SPLIT].rearrange("p (t c) -> p t c", c=8)
        tap_b = cols[:, C_TAP_B:C_TAP_B + 8 * (TAPS - TAP_SPLIT)].rearrange("p (t c) -> p t c", c=8)
        wide = CTX + PAD + LAT
        with e.loop(KT, u=2, c=1 + TAPS) as i:
            dve.tensor_copy(taps[:, 0:TAP_SPLIT], tap_a[:, :, column(i)].rearrange("p t c -> p (t c)"))
            dve.tensor_copy(taps[:, TAP_SPLIT:TAPS], tap_b[:, :, column(i)].rearrange("p t c -> p (t c)"))
            e.step(dve.tensor_copy(taps[:, TAPS:TAPS + 1], cols[:, column(i + (C_VEC + 8 * V_CB))]))
            bank = take_unit(e)
            dve.wait_ge(S["sig_ready"], i + 1)
            TT(upb[:, PAD:PAD + CTX], bank[:, CTX:2 * CTX], sig[:, 0:CTX], ALU.mult)
            free_unit(e, TT(upb[:, 2 * PAD + CTX:2 * PAD + TOK], bank[:, 2 * CTX:], sig[:, CTX:TOK], ALU.mult),
                      then_read=True)
            free_unit(e, TS(csum[0][:, :], upb[:, 0:wide], taps[:, 0:1], taps[:, TAPS:TAPS + 1], ALU.mult, ALU.add))
            TS(csum[1][:, :], upb[:, 1:1 + wide], taps[:, 1:2], None, ALU.mult).then_inc(S["dve_chain"], 1)
            e.n["c"] += 1
            for t in range(2, TAPS):
                if t == 2:
                    dve.wait_ge(S["acc_free"], e.at("u", 2))
                else:
                    dve.wait_ge(S["dve_chain"], e.at("c", -1))
                part = csum[t % 2][:, :]
                STT(out=part, in0=upb[:, t:t + wide], scalar=taps[:, t:t + 1], in1=part,
                    op0=ALU.mult, op1=ALU.add).then_inc(S["dve_chain"], 1)
                e.n["c"] += 1
            dve.wait_ge(S["dve_chain"], e.at("c"))
            TT(tile_of(cv, i, slice(0, CTX)), csum[0][:, 0:CTX], csum[1][:, 0:CTX], ALU.add)
            e.step(TT(tile_of(cv, i, slice(CTX, TOK)), csum[0][:, CTX + PAD:], csum[1][:, CTX + PAD:], ALU.add))
            dve.wait_ge(S["direct_done"], i * 10 + 26)
            modulation(i * 4 + 16, 0, 4, None)
            modulation(i * 6 + 48, 8, 6, None).then_inc(S["mod_free"], 1)
        dve.wait_ge(S["mod_free"], 5 + KT)
        scales(1, 0, 4, V_N2)
        scales(2, 1, 1, V_N1B)
        e.step(scales(3, 1, 4, V_N2B))
        dve.sem_inc(S["conv_done"], 1)
        dve.wait_ge(S["stat_ready"], 2)
        e.step(dve.tensor_copy(mu[:, :], token_cols(pa)))
        with e.loop(KT) as i:
            TT(tile_of(cv, i, slice(0, TOK)), tile_of(cv, i, slice(0, TOK)), mu[:, :], ALU.subtract
               ).then_inc(S["centred"], 1)
        inverse_root(e, 3, FULL, 2)
        with e.loop(KT) as i:
            TT(tile_of(cv, i, slice(0, TOK)), tile_of(cv, i, slice(0, TOK)), rstd[:, :], ALU.mult
               ).then_inc(S["ln_ready"], 1)
        def to_stream(gate, segs):
            def one(i):
                bank = take_unit(e)
                for s0, s1, v in segs:
                    xs = tile_of(x, i, slice(s0, s1))
                    ins = STT(out=xs, in0=bank[:, CTX + s0:CTX + s1], scalar=mod[:, column(i + gate), v], in1=xs,
                              op0=ALU.mult, op1=ALU.add)
                free_unit(e, ins)
            return one

        def mlp(layer, segs):
            c0 = segs[0][0]

            def up(chunk, j, b):
                bank = take_unit(e)
                free_unit(e, TS(tmp[:, c0:TOK], token_cols(bank, c0), 0.0, None, ALU.max), then_read=True)
                e.step(TT(tmp2[:, c0:TOK], tmp[:, c0:TOK], tmp[:, c0:TOK], ALU.mult))
                e.step(dve.tensor_copy(hid_hi[b][:, j, c0:TOK], tmp2[:, c0:TOK]))
                TT(hid_lo[b][:, j, c0:TOK], tmp2[:, c0:TOK], hid_hi[b][:, j, c0:TOK].bitcast(F32), ALU.subtract
                   ).then_inc(S["hid_ready"], 1)

            def down(chunk, j, b):
                for n in (2 * j, 2 * j + 1):
                    bank = take_unit(e)
                    for s0, s1, v in segs:
                        g = layer * 48 + 40 + n
                        ins = STT(out=x[:, n, s0:s1], in0=bank[:, CTX + s0:CTX + s1], scalar=mod[:, g, v:v + 1],
                                  in1=x[:, n, s0:s1], op0=ALU.mult, op1=ALU.add)
                    free_unit(e, ins)

            feed_forward(e, up, down, up_steps=2)

        slots(e, KT, to_stream(16, FULL))
        norm_dve(e, 4, FULL, 3, 8, scale=1, shift=24)
        dve.wait_ge(S["al_ready"], KT * 3)
        dve.memset(zero_rows[:, :], 0.0).then_inc(S["zero_rows_ready"], 1)
        mlp(0, FULL)
        dve.wait_ge(S["rows_zeroed"], 16)
        norm_dve(e, 5, FULL, 4, 16, scale=2, shift=48)

        def to_q(i):
            bank = take_unit(e)
            free_unit(e, dve.tensor_copy(tile_of(qf, i, slice(0, LAT)), bank[:, 512:1024]))

        slots(e, KT, to_q)
        for j in range(2):
            bank = take_unit(e)
            free_unit(e, dve.tensor_copy(kf[:, j, :], token_cols(bank)))
            e.n["g"] += 1
            e.n["q"] += 1
        for j in range(2):
            bank = take_unit(e)
            free_unit(e, dve.tensor_copy(vt[:, :, j * P:j * P + P],
                                         token_cols(bank).rearrange("p (b n) -> p b n", n=P)))
            e.n["g"] += 1
            e.n["q"] += 1
        dve.wait_ge(S["acc_free"], e.at("u", 2))

        def norm_rope(r, src, n):
            is_q = not isinstance(r, int)
            turns = is_q or r < KT + 2
            gain = qk_gain[:, 0:1] if is_q else qk_gain[:, 1:2]
            dve.wait_ge(S["qk_stat"], r + 2)
            e.step(TS(rstd[:, 0:n], pa[:, 0:n], EPS, None, ALU.add))
            reciprocal_for_root(e, rstd[:, 0:n])
            dve.wait_ge(S["root_out"], r + 5)
            if not turns:
                STT(out=src, in0=src, scalar=gain, in1=rstd[:, 0:n], op0=ALU.mult, op1=ALU.mult
                    ).then_inc(S["qk_normed"], 1)
                dve.wait_ge(S["qk_normed"], r + 1)
                return
            STT(out=tmp[:, 0:n], in0=src, scalar=gain, in1=rstd[:, 0:n], op0=ALU.mult, op1=ALU.mult
                ).then_inc(S["qk_normed"], 1)
            dve.wait_ge(S["qk_normed"], r + 1)
            TT(tmp3[:, 0:n], tmp[:, 0:n], rope[:, 0, :], ALU.mult)
            dve.wait_ge(S["qk_rotated"], r + 1)
            e.step(TT(src, pbk[:, 0:n], rope[:, 1, :], ALU.mult))
            e.step(TT(src, src, tmp3[:, 0:n], ALU.add))

        qk_units(e, norm_rope, steps=3)
        dve.wait_ge(S["qk_normed"], KT + 4)
        dve.sem_inc(S["k_ready"], 1)
        for kv in range(4):
            dve.wait_ge(S["k_doubled"], kv + 1)
            dve.tensor_copy(kdup[:, kv, :], token_cols((pa, pbk)[kv % 2])).then_inc(S["kdup_ready"], 1)
        dve.wait_ge(S["kdup_ready"], 4)
        with e.loop(4, c=2 * 16 + 4) as i:
            dve.tensor_copy(kst[:, :], tile_of(kdup, i, slice(0, TOK)))
            dve.tensor_copy(vst[:, :, :], vt[:, :, bass.ds(i * HD, HD)])
            dve.tensor_copy(qst[:, 0, :], tile_of(qf, i * 2, slice(0, LAT)))
            dve.tensor_copy(qst[:, 1, :], tile_of(qf, i * 2 + 1, slice(0, LAT))).then_inc(S["staged"], 1)

            def maxima(m):
                s = 4 * (m % 2)
                dve.wait_ge(S["scores_ready"], i * 16 + (m + 1))
                e.step(dve.tensor_reduce(stat[:, s:s + 1], acc[m % 2][:, 0:TOK], AX.X, ALU.max))
                TS(stat[:, s + 1:s + 2], stat[:, s:s + 1], -HD ** -0.5, None, ALU.mult).then_inc(S["nmax_ready"], 1)

            maxima(0)
            for m in range(16):
                if m + 1 < 16:
                    maxima(m + 1)
                s = 4 * (m % 2)
                dve.wait_ge(S["exp_done"], i * 16 + (m + 1))
                e.step(dve.reciprocal(stat[:, s + 3:s + 4], stat[:, s + 2:s + 3]))
                TS(pr[m % 2][:, :], pr[m % 2][:, :], stat[:, s + 3:s + 4], None, ALU.mult
                   ).then_inc(S["probs_ready"], 1)
                if m % 8 == 7:
                    t = m // 8
                    dve.wait_ge(S["heads_done"], i * 4 + (2 * t + 2))
                    o = pbk[:, 512 * t:512 * t + LAT]
                    e.step(dve.tensor_copy(tile_of(ah, i * 2 + t, slice(CTX, TOK)), o))
                    e.step(TT(tile_of(al, i * 2 + t, slice(CTX, TOK)), o,
                              tile_of(ah, i * 2 + t, slice(CTX, TOK)).bitcast(F32), ALU.subtract))
        dve.sem_inc(S["attended"], 1)
        slots(e, KT, to_stream(48 + 16, LATENT))
        norm_dve(e, 6, LATENT, 17, 24, scale=3, shift=72)
        dve.wait_ge(S["al_ready"], KT * 5)
        dve.memset(rel[:, :], NEG).then_inc(S["mask_row"], 1)
        mlp(1, LATENT)

        dve.wait_ge(S["rel_ready"], 1)
        dve.tensor_copy(rel_line[:, :], pbk[0:8, 0:3 * P]).then_inc(S["line_ready"], 1)
        dve.wait_ge(S["rev_turned"], 2)
        for n, bank in enumerate((pa, pbk)):
            dve.tensor_copy(bias2[:, 4 * n:4 * n + 4, :], bank[:, :].rearrange("p (h s) -> p h s", h=4)
                            ).then_inc(S["bias_done"], 1)
        dve.wait_ge(S["ws_turned"], 1)
        dve.tensor_copy(wst[:, :, :], pa[:, :].rearrange("p (g t) -> p g t", g=8)).then_inc(S["wst_ready"], 1)
        dve.wait_ge(S["bs_spread"], 1)
        e.step(dve.tensor_copy(bsp[:, :, :], pbk[:, 0:512].rearrange("p (t q) -> p t q", t=4)))
        norm_dve(e, 7, LATENT, 18, 32, gain=C_VEC + 8 * V_AN)

        def keep(dst, n=None):
            bank = take_unit(e)
            src = bank[:, 512:1024]
            free_unit(e, dve.tensor_copy(dst, src if n is None else src.rearrange("p (b n) -> p b n", n=n)))
            e.n["g"] += 1
            e.n["q"] += 1

        for j in range(4):
            keep(gu[:, j, :])
        for j in range(4):
            keep(gv[:, :, j * P:j * P + P], P)
        for j in range(4):
            keep(q2[:, j, :])
        keep(k2f[:, :])
        keep(v2[:, 1:5, :], P)
        with e.loop(4, g=4, q=4, u=4) as i:
            for j in range(4):
                keep(tile_of(sg, i * 4 + j, slice(0, LAT)))
        dve.wait_ge(S["acc_free"], e.at("u", 2))

        dve.memset(v2[:, 0, :], 0.0)
        dve.memset(kd2[:, :, 0:P], 0.0)
        for kv in range(2):
            dve.wait_ge(S["k2_doubled"], kv + 1)
            dve.tensor_copy(kd2[:, kv, P:], (pa, pbk)[kv][:, 0:LAT]).then_inc(S["kd2_ready"], 1)

        dve.wait_ge(S["gelu_done"], 8)
        dve.wait_ge(S["gains_in"], 32)
        e.step(dve.tensor_reduce(gst[:, 0:4], gv[:, :, :], AX.X, ALU.add))
        e.step(TS(gst[:, 4:8], gst[:, 0:4], 1.0 / 512, None, ALU.mult))
        for b in range(4):
            e.step(TS(gv[:, b, :], gv[:, b, :], gst[:, 4 + b:5 + b], None, ALU.subtract))
            e.step(STT(out=tmp[:, 0:LAT], in0=gv[:, b, :], scalar=1.0, in1=gv[:, b, :], op0=ALU.mult, op1=ALU.mult,
                       accum_out=gst[:, 8 + b:9 + b]))
        e.step(TS(gst[:, 12:16], gst[:, 8:12], 1.0 / 512, EPS, ALU.mult, ALU.add))
        reciprocal_for_root(e, gst[:, 12:16])
        dve.wait_ge(S["root_out"], 19)
        for b in range(4):
            STT(out=gv[:, b, :], in0=gv[:, b, :], scalar=gst[:, 12 + b:13 + b], in1=gvn[:, :], op0=ALU.mult,
                op1=ALU.mult).then_inc(S["gv_ready"], 1)
        dve.wait_ge(S["gv_ready"], 4)
        for t in range(4):
            dve.wait_ge(S["spatial_done"], t + 1)
            s = (pa, pbk)[t // 2][:, (t % 2) * 512:(t % 2) * 512 + 512].rearrange("p (c q) -> p c q", q=P)
            t4 = tmp[:, 0:LAT].rearrange("p (c q) -> p c q", q=P)
            e.step(TT(t4, s, bsp[:, t, :].unsqueeze(1).to_broadcast([P, 4, P]), ALU.add))
            e.step(TT(tmp[:, 0:LAT], tmp[:, 0:LAT], gu[:, t, :], ALU.mult))
            e.step(dve.tensor_copy(ah[:, t, CTX:TOK], tmp[:, 0:LAT]))
            e.step(TT(al[:, t, CTX:TOK], tmp[:, 0:LAT], ah[:, t, CTX:TOK].bitcast(F32), ALU.subtract))

        def logits(h):
            b = h % 2
            dve.wait_ge(S["scores2"], h + 1)
            e.step(STT(out=sc2[b][:, :, :], in0=acc[b][:, :].rearrange("p (c s) -> p c s", c=4), scalar=HD ** -0.5,
                       in1=bias2[:, h, :].unsqueeze(1).to_broadcast([P, 4, 2 * P]), op0=ALU.mult, op1=ALU.add))
            e.step(dve.memset(sc2[b][:, 0, 0:P], NEG))
            e.step(dve.tensor_reduce(st2[:, b, 0:4], sc2[b][:, :, :], AX.X, ALU.max))
            TS(st2[:, b, 4:8], st2[:, b, 0:4], sinks[:, h:h + 1], -1.0, ALU.max, ALU.mult
               ).then_inc(S["nm2_ready"], 1)

        logits(0)
        for h in range(8):
            b = h % 2
            if h + 1 < 8:
                logits(h + 1)
            dve.wait_ge(S["exp2_done"], h + 1)
            e.step(TT(st2[:, b, 16:20], st2[:, b, 8:12], st2[:, b, 12:16], ALU.add))
            e.step(dve.reciprocal(st2[:, b, 20:24], st2[:, b, 16:20]))
            TT(sc2[b][:, :, :], sc2[b][:, :, :], st2[:, b, 20:24].unsqueeze(2).to_broadcast([P, 4, 2 * P]), ALU.mult
               ).then_inc(S["probs2"], 1)
            if h % 2 == 1:
                t = h // 2
                dve.wait_ge(S["heads2"], h + 1)
                o = pbk[:, (t % 2) * 512:(t % 2) * 512 + 512]
                e.step(dve.tensor_copy(ah[:, 4 + t, CTX:TOK], o))
                TT(al[:, 4 + t, CTX:TOK], o, ah[:, 4 + t, CTX:TOK].bitcast(F32), ALU.subtract
                   ).then_inc(S["branches_ready"], 1)

        dve.wait_ge(S["gates_ready"], 16)
        with e.loop(2, g=4, q=4, u=8, c=8) as i:
            for s in range(2):
                for branch in range(2):
                    for j in range(2):
                        n = i * 4 + (2 * s + j)
                        bank = take_unit(e)
                        g = tile_of(sg, n + 8 * branch, slice(0, LAT))
                        free_unit(e, TT(g, bank[:, 512:1024], g, ALU.mult), then_read=True)
                    e.n["g"] += 1
                    e.n["q"] += 1
                for j in range(2):
                    n = i * 4 + (2 * s + j)
                    g0, g1 = tile_of(sg, n, slice(0, LAT)), tile_of(sg, n + 8, slice(0, LAT))
                    e.step(TT(g0, g0, g1, ALU.add))
                    e.step(dve.tensor_copy(tile_of(mh, n, slice(0, LAT)), g0))
                    TT(tile_of(ml, n, slice(0, LAT)), g0, tile_of(mh, n, slice(0, LAT)).bitcast(F32), ALU.subtract
                       ).then_inc(S["merged"], 1)

        def plain(i):
            bank = take_unit(e)
            xs = tile_of(x, i, slice(CTX, TOK))
            free_unit(e, TT(xs, bank[:, 512:1024], xs, ALU.add))

        slots(e, KT, plain)
        norm_dve(e, 8, LATENT, 20, 40, gain=C_VEC + 8 * V_FN)

        for b in range(NB_L):
            bank = take_unit(e)
            free_unit(e, dve.tensor_copy(hn[:, b, :], bank[:, :]), then_read=True)
            dve.sem_inc(S["hn_ready"], 1)
        dve.wait_ge(S["logits_done"], 1)
        dve.wait_ge(S["route_in"], 160)

        def line(n, a=4, b=4):
            return rt[:, n, 0:a * b].rearrange("p (a b) -> p a b", a=a)

        def spread(ap, n):
            return ap.unsqueeze(2).to_broadcast([P, ap.shape[1], n])

        from16 = ramp[:, 0:4].unsqueeze(1).to_broadcast([P, 4, 4])

        def first_of_max(dst, src, most, s1, s2):
            e.step(dve.tensor_reduce(most, src, AX.X, ALU.max))
            e.step(TT(s1, src, spread(most, 4), ALU.is_equal))
            e.step(TT(s1, s1, from16, ALU.mult))
            e.step(dve.tensor_reduce(s2, s1, AX.X, ALU.min))
            e.step(TT(dst, from16, spread(s2, 4), ALU.is_equal))

        e.step(TT(lg[:, :, :], pbk[:, 0:80].rearrange("p (b n) -> p b n", b=4),
                  rb[:, :].unsqueeze(1).to_broadcast([P, 4, 20]), ALU.add))
        oh_g, oh_1, oh_2 = line(2), line(3), line(4)
        gm, m1, m2 = rt[:, 5, 0:4], rt[:, 5, 4:8], rt[:, 5, 8:12]
        first_of_max(oh_g, lg[:, :, 0:4], gm, line(6), rt[:, 7, 0:4])
        e.step(TT(line(0), lg[:, :, 0:4], spread(gm, 4), ALU.subtract))
        four = rt[:, 8, 0:64].rearrange("p (b g e) -> p b g e", b=4, g=4)
        e.step(TT(four, lg[:, :, 4:20].rearrange("p b (g e) -> p b g e", g=4),
                  oh_g.unsqueeze(3).to_broadcast([P, 4, 4, 4]), ALU.mult))
        el = line(9)
        e.step(dve.tensor_reduce(el, four.rearrange("p b g e -> p b e g"), AX.X, ALU.add))
        first_of_max(oh_1, el, m1, line(6), rt[:, 7, 0:4])
        el2 = line(10)
        e.step(STT(out=el2, in0=oh_1, scalar=NEG, in1=el, op0=ALU.mult, op1=ALU.add))
        first_of_max(oh_2, el2, m2, line(6), rt[:, 7, 0:4])
        TT(rt[:, 0, 16:20], m2, m1, ALU.subtract).then_inc(S["route_args"], 1)
        pick = [rt[:, 11 + k, 0:64].rearrange("p (b n) -> p b n", b=4) for k in range(3)]
        for k, oh in enumerate((oh_1, oh_2)):
            e.step(TT(pick[k].rearrange("p b (g e) -> p b g e", g=4), oh_g.unsqueeze(3).to_broadcast([P, 4, 4, 4]),
                      oh.unsqueeze(2).to_broadcast([P, 4, 4, 4]), ALU.mult))
        TT(pick[2], pick[0], pick[1], ALU.add).then_inc(S["picks_ready"], 1)
        dve.wait_ge(S["route_exp"], 1)
        e.step(dve.tensor_reduce(rt[:, 7, 4:8], line(1), AX.X, ALU.add))
        e.step(TS(rt[:, 7, 8:12], rt[:, 1, 16:20], 1.0, None, ALU.add))
        e.step(dve.reciprocal(rt[:, 7, 12:16], rt[:, 7, 4:8]))
        e.step(dve.reciprocal(rt[:, 7, 16:20], rt[:, 7, 8:12]))
        e.step(TT(wk[:, 0, :], rt[:, 7, 12:16], rt[:, 7, 16:20], ALU.mult))
        e.step(TT(wk[:, 1, :], wk[:, 0, :], rt[:, 1, 16:20], ALU.mult))
        dve.wait_ge(S["ranks_done"], 1)
        n16 = rt[:, 14, 0:16]
        e.step(dve.tensor_copy(n16, pbk[:, 576:592]))
        e.step(TT(rt[:, 15, 0:64].rearrange("p (n k) -> p n k", k=4), spread(n16, 4),
                  ramp[:, 48:52].unsqueeze(1).to_broadcast([P, 16, 4]), ALU.is_gt))
        nb, even, odd = rt[:, 16, 0:16], rt[:, 16, 16:32], rt[:, 16, 32:48]
        e.step(dve.tensor_reduce(nb, rt[:, 15, 0:64].rearrange("p (n k) -> p n k", k=4), AX.X, ALU.add))
        src, dst = nb, even
        for shift in (1, 2, 4, 8):
            e.step(dve.tensor_copy(dst[:, 0:shift], src[:, 0:shift]))
            e.step(TT(dst[:, shift:16], src[:, shift:16], src[:, 0:16 - shift], ALU.add))
            src, dst = dst, (odd if dst is even else even)
        upto = src
        base = rt[:, 17, 0:16]
        e.step(TT(base, upto, nb, ALU.subtract))
        e.step(TS(base, base, float(P), None, ALU.mult))
        where = rt[:, 18, 0:64].rearrange("p (b n) -> p b n", b=4)
        e.step(TT(where, pbk[:, 512:576].rearrange("p (b n) -> p b n", b=4),
                  base.unsqueeze(1).to_broadcast([P, 4, 16]), ALU.add))
        prod = rt[:, 19, 0:64].rearrange("p (b n) -> p b n", b=4)
        for k in range(2):
            e.step(TT(prod, pick[k], where, ALU.mult))
            e.step(dve.tensor_reduce(rt[:, 20, 4 * k:4 * k + 4], prod, AX.X, ALU.add))
        dve.tensor_copy(pos_i[:, :], rt[:, 20, 0:8]).then_inc(S["pos_ready"], 1)
        table = rt[:, 0:6, :].rearrange("p a b -> p (a b)").rearrange("p (j n) -> p j n", n=16)
        e.step(TT(table, upto.unsqueeze(1).to_broadcast([P, LIST, 16]), spread(ramp[:, 16:16 + LIST], 16), ALU.is_le))
        e.step(dve.tensor_reduce(rt[:, 21, 0:LIST], table, AX.X, ALU.add))
        e.step(TS(rt[:, 21, 0:LIST], rt[:, 21, 0:LIST], float(N_EXP - 1), None, ALU.min))
        e.step(dve.tensor_copy(rt[:, 21, LIST:LIST + 1], upto[:, 15:16]))
        dve.tensor_copy(meta[:, 0:LIST + 1], rt[:, 21, 0:LIST + 1]).then_inc(S["meta_ready"], 1)
        for b in range(NB_L):
            bank = take_unit(e)
            free_unit(e, dve.tensor_copy(ht[:, b, :], bank[:, :]))
        dve.wait_ge(S["meta_ready"], 1)
        n_blocks = dve.value_load(meta[0:1, LIST:LIST + 1], min_val=2 * LAT // P, max_val=SLOTS_MAX)

        def take_rows(v):
            dve.wait_ge(S["xg_turned"], v)
            dve.tensor_copy(xgt[:, :, :], pa[:, :].rearrange("p (k q) -> p k q", q=P)).then_inc(S["xgt_ready"], 1)

        take_rows(2)
        with dve.Fori(0, n_blocks) as i:
            dve.wait_ge(S["silu_gate"], i + 1)
            dve.wait_ge(S["up_done"], i + 2)
            TT(hidt[:, :], gate_s[:, :], acc[0][:, 512:1024], ALU.mult).then_inc(S["hidt_ready"], 1)
            take_rows(i + 3)
            dve.wait_ge(S["hid_turned"], i + 1)
            dve.tensor_copy(hidT[:, :, :], acc[1][:, 0:E_FF].rearrange("p (k q) -> p k q", q=P)
                            ).then_inc(S["hidT_ready"], 1)
            dve.wait_ge(S["down_done"], i + 2)
            dve.wait_ge(S["yo_out"], i * 16 + 16)
            dve.tensor_copy(yo[:, 512:1024], pbk[:, 512:1024]).then_inc(S["yo_dve"], 1)
        for b in range(NB_L):
            dve.wait_ge(S[f"rows_in{b}"], 32)
            e.step(STT(out=osum[b][:, :], in0=ga[2 * b][:, :], scalar=wk[:, 0, b:b + 1], in1=ht[:, b, :],
                       op0=ALU.mult, op1=ALU.add))
            STT(out=osum[b][:, :], in0=ga[2 * b + 1][:, :], scalar=wk[:, 1, b:b + 1], in1=osum[b][:, :],
                op0=ALU.mult, op1=ALU.add).then_inc(S["osum_ready"], 1)
            dve.wait_ge(S["fin_sq"], b + 1)
            e.step(TS(fin_s[:, 4 + b:5 + b], fin_s[:, b:b + 1], 1.0 / D, EPS, ALU.mult, ALU.add))
            reciprocal_for_root(e, fin_s[:, 4 + b:5 + b])
            dve.wait_ge(S["root_out"], 21 + b)
            STT(out=osum[b][:, :], in0=osum[b][:, :], scalar=fin_s[:, 4 + b:5 + b], in1=fgain[:, :],
                op0=ALU.mult, op1=ALU.mult).then_inc(S["final_ready"], 1)

    @block.tensor
    def _(pe):
        e = Program(pe, counts="gqu")
        ident = mats[:, M_ID, :]
        pe.sem_inc(S["split_started"], 1)
        pe.sem_inc(S["qk_stat"], 1)
        for name in ("gate_done", "up_done", "down_done", "xg_turned"):
            pe.sem_inc(S[name], 1)
        pe.wait_ge(S["consts_in"], 16 * 18)
        for n, rows in enumerate((96, 88, 120, 128)):
            ins = pe.transpose(pbk[:, P * n:P * n + rows], vec_rows[0:rows, n, :], ident[0:rows, 0:rows])
        ins.then_inc(S["vec_turned"], 1)
        pe.wait_ge(S["x_in"], 32)

        def turn_unit(rows):
            pe.wait_ge(S["acc_free"], e.at("u", 1))
            for k in range(KT):
                ins = pe.transpose(acc[e.n["u"] % 2][:, k * P:k * P + P], rows(k), ident)
            ins.then_inc(S["acc_ready"], 1)
            e.n["u"] += 1

        for b in range(NB_C + NB_L):
            turn_unit(lambda k: xin[:, b, k * P:k * P + P])

        def direct(at):
            r = e.n["g"] % RING
            pe.wait_ge(S[f"raw_in{r}"], 16 * e.laps() if isinstance(e.laps(), int) else e.laps() * 16)
            for k in range(KT):
                ins = pe.matmul(pbk[:, at:at + 2], raw[r][:, k * P:k * P + P], silu_c[:, k, :],
                                start=k == 0, stop=k == KT - 1)
            ins.then_inc(S["direct_done"], 1)
            e.n["g"] += 1

        pe.wait_ge(S["silu_ready"], 2)
        with e.loop(4, g=4) as i:
            pe.wait_ge(S["mod_free"], i + 1)
            for j in range(4):
                direct(2 * j)
        sum_over_channels(e, sq, FULL, ["sq_ready"], 0)
        pe.wait_ge(S["al_ready"], KT)
        with e.loop(KT, g=12, q=2, u=2) as i:
            for _ in range(2):
                product(e, ah, al, FULL)
                e.n["g"] += 1
                e.n["q"] += 1
            pe.wait_ge(S["mod_free"], i + 5)
            for j in range(10):
                direct(2 * j)
        pe.wait_ge(S["conv_done"], 1)
        sum_over_channels(e, cv, FULL, [], 0)
        sum_over_channels(e, sq, FULL, ["sq_ready"], 8)
        pe.wait_ge(S["al_ready"], 2 * KT)

        def tile(segs, hi=ah, lo=al, **kw):
            return lambda i: product(e, hi, lo, segs, **kw)

        slots(e, KT, tile(FULL))

        def mlp(segs, hidden0, layers):
            def down(chunk, j, b):
                if j == 0:
                    pe.wait_ge(S["hid_ready"], chunk * 4 + (hidden0 + 4))
                product(e, hid_hi[b], hid_lo[b], segs, k=4)

            feed_forward(e, lambda chunk, j, b: product(e, ah, al, segs), down)

        sum_over_channels(e, sq, FULL, ["sq_ready"], 16)
        pe.wait_ge(S["al_ready"], 3 * KT)
        mlp(FULL, 0, 0)
        sum_over_channels(e, sq, FULL, ["sq_ready"], 24)
        pe.wait_ge(S["al_ready"], 4 * KT)
        slots(e, KT, tile(LATENT))
        for _ in range(2):
            product(e, ah, al, FULL)
            e.n["g"] += 1
            e.n["q"] += 1
        for _ in range(2):
            product_rows(e, range(NB_C + NB_L))
            e.n["g"] += 1
            e.n["q"] += 1

        def head_sums(r, src, n):
            turns = not isinstance(r, int) or r < KT + 2
            pe.wait_ge(S["qk_sq"], r + 1)
            pe.matmul(pa[:, 0:n], mats[:, M_HEAD, :], tmp2[:, 0:n], start=True, stop=True).then_inc(S["qk_stat"], 1)
            pe.wait_ge(S["qk_normed"], r + 1)
            if turns:
                pe.matmul(pbk[:, 0:n], mats[:, M_ROT, :], tmp[:, 0:n], start=True, stop=True
                          ).then_inc(S["qk_rotated"], 1)

        qk_units(e, head_sums)
        pe.wait_ge(S["k_ready"], 1)
        for kv in range(4):
            if kv >= 2:
                pe.wait_ge(S["kdup_ready"], kv - 1)
            for s0, s1, _ in FULL:
                ins = pe.matmul((pa, pbk)[kv % 2][:, CTX + s0:CTX + s1], mats[:, M_DUP0 + kv % 2, :],
                                kf[:, kv // 2, s0:s1], start=True, stop=True)
            ins.then_inc(S["k_doubled"], 1)
        with e.loop(4) as i:
            def scores(m):
                t, h, qb = m // 8, (m // 4) % 2, m % 4
                if m >= 2:
                    pe.wait_ge(S["exp_done"], i * 16 + (m - 1))
                rows = slice(HD * h, HD * h + HD)
                for k0, k1 in ((0, 512), (512, TOK)):
                    ins = pe.matmul(acc[m % 2][:, k0:k1], qst[rows, t, qb * P:qb * P + P], kst[rows, k0:k1],
                                    start=True, stop=True)
                ins.then_inc(S["scores_ready"], 1)

            pe.wait_ge(S["staged"], i + 1)
            scores(0)
            for m in range(16):
                if m + 1 < 16:
                    scores(m + 1)
                t, h = m // 8, (m // 4) % 2
                pe.wait_ge(S["probs_ready"], i * 16 + (m + 1))
                if m >= 1:
                    pe.wait_ge(S["prt_ready"], i * 16 + m)
                for k in range(6):
                    ins = pe.transpose(pa[:, k * P:k * P + P], pr[m % 2][:, k * P:k * P + P], ident)
                ins.then_inc(S["turned"], 1)
                if m % 4 == 3:
                    pe.wait_ge(S["prt_ready"], i * 16 + (m + 1))
                    for k in range(6):
                        ins = pe.matmul(pbk[HD * h:HD * h + HD, 512 * t:512 * t + LAT], vst[:, k, :], prt[:, k, :],
                                        start=k == 0, stop=k == 5)
                    ins.then_inc(S["heads_done"], 1)
        pe.wait_ge(S["attended"], 1)
        slots(e, KT, tile(LATENT))
        sum_over_channels(e, sq, LATENT, ["sq_ready"], 32)
        pe.wait_ge(S["al_ready"], 5 * KT)
        mlp(LATENT, 32, 0)
        pe.wait_ge(S["prep_in"], 80)
        pe.wait_ge(S["mask_row"], 1)
        pe.matmul(pbk[0:8, 0:3 * P], rel[:, :], one_hot[:, :], start=True, stop=True).then_inc(S["rel_ready"], 1)
        pe.wait_ge(S["rev_in"], 16)
        for n, bank in enumerate((pa, pbk)):
            for j in range(2):
                ins = pe.matmul(bank[:, 512 * j:512 * j + 512], mats[:, M_FLIP, :],
                                bias_rev[:, 4 * n + 2 * j:4 * n + 2 * j + 2, :].rearrange("p h s -> p (h s)"),
                                start=True, stop=True)
            ins.then_inc(S["rev_turned"], 1)
        pe.wait_ge(S["bias_done"], 2)
        for g in range(8):
            ins = pe.transpose(pa[:, g * P:g * P + P], ws_in[:, g, :], ident)
        ins.then_inc(S["ws_turned"], 1)
        for t in range(4):
            ins = pe.matmul(pbk[:, t * P:t * P + P], group[:, t * P:t * P + P], bs_rows[:, :], start=True, stop=True)
        ins.then_inc(S["bs_spread"], 1)
        pe.wait_ge(S["wst_ready"], 1)
        sum_over_channels(e, sq, LATENT, ["sq_ready"], 40)
        pe.wait_ge(S["al_ready"], 6 * KT)

        def used():
            e.n["g"] += 1
            e.n["q"] += 1

        for n in range(14):
            if n in (4, 5, 6, 7, 13):
                product_rows(e, range(NB_C, NB_C + NB_L))
            else:
                product(e, ah, al, LATENT)
            used()
        with e.loop(4, g=4, q=4, u=4) as i:
            for j in range(4):
                product(e, ah, al, LATENT)
                used()
        pe.wait_ge(S["acc_free"], e.at("u", 2))
        for kv in range(2):
            pe.matmul((pa, pbk)[kv][:, 0:LAT], mats[:, M_DUP0 + kv, :], k2f[:, :], start=True, stop=True
                      ).then_inc(S["k2_doubled"], 1)
        pe.wait_ge(S["kd2_ready"], 2)
        pe.wait_ge(S["gv_ready"], 4)
        pe.wait_ge(S["wst_masked"], 1)
        for t in range(4):
            for h in range(2):
                g = 2 * t + h
                for c in range(4):
                    at = (t % 2) * 512 + c * P
                    ins = pe.matmul((pa, pbk)[t // 2][HD * h:HD * h + HD, at:at + P], gv[:, c, g * HD:g * HD + HD],
                                    wst[:, g, :], start=True, stop=True)
            ins.then_inc(S["spatial_done"], 1)

        def scores2(h):
            rows = slice(HD * (h % 2), HD * (h % 2) + HD)
            for blk in range(4):
                ins = pe.matmul(acc[h % 2][:, blk * 2 * P:blk * 2 * P + 2 * P],
                                q2[rows, h // 2, blk * P:blk * P + P], kd2[rows, h // 4, blk * P:blk * P + 2 * P],
                                start=True, stop=True)
            ins.then_inc(S["scores2"], 1)

        scores2(0)
        for h in range(8):
            if h + 1 < 8:
                if h >= 1:
                    pe.wait_ge(S["nm2_ready"], h)
                scores2(h + 1)
            pe.wait_ge(S["probs2"], h + 1)
            if h >= 1:
                pe.wait_ge(S["pt2_ready"], h)
            for blk in range(4):
                for kk in range(2):
                    at = (2 * blk + kk) * P
                    ins = pe.transpose(pa[:, at:at + P], sc2[h % 2][:, blk, kk * P:kk * P + P], ident)
            ins.then_inc(S["turned2"], 1)
            pe.wait_ge(S["pt2_ready"], h + 1)
            t = h // 2
            if h in (4, 6):
                pe.wait_ge(S["branches_ready"], t - 1)
            for blk in range(4):
                at = (t % 2) * 512 + blk * P
                for kk in range(2):
                    ins = pe.matmul(pbk[HD * (h % 2):HD * (h % 2) + HD, at:at + P],
                                    v2[:, blk + kk, HD * (h // 4):HD * (h // 4) + HD], pt2[:, blk, kk, :],
                                    start=kk == 0, stop=kk == 1)
            ins.then_inc(S["heads2"], 1)
        pe.wait_ge(S["branches_ready"], 4)
        with e.loop(2, g=4, q=4, u=8) as i:
            for s in range(2):
                for branch in range(2):
                    product(e, ah, al, LATENT, k=4, shift=4 * branch)
                    used()
        pe.wait_ge(S["merged"], 8)
        slots(e, KT, tile([(0, LAT, 0)], mh, ml, out0=512))
        sum_over_channels(e, sq, LATENT, ["sq_ready"], 48)
        pe.wait_ge(S["y_ready"], KT * 6)
        for b in range(NB_L):
            turn_unit(lambda k: y[:, k, CTX + b * P:CTX + b * P + P])
        pe.wait_ge(S["route_in"], 160)
        for b in range(NB_L):
            for k in range(KT):
                ins = pe.matmul(pbk[:, 20 * b:20 * b + 20], y[:, k, CTX + b * P:CTX + b * P + P], rw[:, k, :],
                                start=k == 0, stop=k == KT - 1)
        ins.then_inc(S["logits_done"], 1)
        pe.wait_ge(S["picks_ready"], 1)
        both = rt[:, 13, 0:64].rearrange("p (b n) -> p b n", b=4)
        for b in range(NB_L):
            for c in range(b + 1):
                pe.matmul(pbk[:, 512 + 16 * b:528 + 16 * b], mats[:, M_TRI if c == b else M_ONE, :], both[:, c, :],
                          start=c == 0, stop=c == b)
        for c in range(NB_L):
            ins = pe.matmul(pbk[:, 576:592], mats[:, M_ONE, :], both[:, c, :], start=c == 0, stop=c == NB_L - 1)
        ins.then_inc(S["ranks_done"], 1)
        for b in range(NB_L):
            turn_unit(lambda k: x[:, k, CTX + b * P:CTX + b * P + P])
        pe.wait_ge(S["meta_ready"], 1)
        n_blocks = pe.value_load(meta[0:1, LIST:LIST + 1], min_val=2 * LAT // P, max_val=SLOTS_MAX)

        def turn_rows(v):
            pe.wait_ge(S["xg_in"], v)
            for k in range(KT):
                ins = pe.transpose(pa[:, k * P:k * P + P], xg[:, :].rearrange("q (p k) -> q k p", k=KT)[:, k, :], ident)
            ins.then_inc(S["xg_turned"], 1)

        pe.wait_ge(S["acc_free"], e.at("u", 2))
        turn_rows(16)
        with pe.Fori(0, n_blocks) as i:
            pe.wait_ge(S["xgt_ready"], i + 1)
            for name, w, c0 in (("wg_in", wg, 0), ("wu_in", wu, 512)):
                pe.wait_ge(S[name], i * 16 + 16)
                for k in range(KT):
                    ins = pe.matmul(acc[0][:, c0:c0 + E_FF], xgt[:, k, :], w[:, k, :], start=k == 0, stop=k == KT - 1)
                ins.then_inc(S["gate_done" if c0 == 0 else "up_done"], 1)
            turn_rows(i * 16 + 32)
            pe.wait_ge(S["hidt_ready"], i + 1)
            for k in range(4):
                ins = pe.transpose(acc[1][:, k * P:k * P + P],
                                   hidt[:, :].rearrange("q (p k) -> q k p", k=4)[:, k, :], ident)
            ins.then_inc(S["hid_turned"], 1)
            pe.wait_ge(S["hidT_ready"], i + 1)
            pe.wait_ge(S["wd_in"], i * 16 + 16)
            pe.wait_ge(S["yo_dve"], i + 1)
            for half in range(2):
                for k in range(4):
                    ins = pe.matmul(pbk[:, 512 * half:512 * half + 512], hidT[:, k, :],
                                    wd[:, k, 512 * half:512 * half + 512], start=k == 0, stop=k == 3)
            ins.then_inc(S["down_done"], 1)


_USED = ['x', 'c', 'ctx', 'c_ctx', 'norm1_g', 'norm2_g', 'w_mod', 'b_mod', 'w_ff1', 'w_ff2', 'conv_w_pw1',
         'conv_w_dw', 'conv_b_dw', 'conv_ln_g', 'conv_ln_b', 'conv_w_pw2', 'gqa_w_qkv', 'gqa_q_norm',
         'gqa_k_norm', 'gqa_w_o', 'attn_norm_g_2', 'w_in_2', 'gm_v_norm_g_2', 'gm_w_spatial_2',
         'gm_b_spatial_2', 'attn_sinks_2', 'rel_bias_2', 'w_proj_a_2', 'w_proj_b_2', 'w_out_2',
         'ffn_norm_g_2', 'router_group_w_2', 'router_group_b_2', 'router_expert_w_2', 'router_expert_b_2',
         'expert_w_gate_2', 'expert_w_up_2', 'expert_w_down_2', 'final_norm_g_2']


def kernel(**inputs):
    import concourse.bacc as bacc
    from concourse.bass_utils import run_bass_kernel_spmd

    nc = bacc.Bacc("TRN2", target_bir_lowering=False, num_devices=1)
    arrays = {name: np.ascontiguousarray(inputs[name]) for name in _USED}
    arrays.update(shape_constants())
    aps = {name: nc.dram_tensor(f"in_{name}", a.shape, mybir.dt.from_np(a.dtype), kind="ExternalInput").ap()
           for name, a in arrays.items()}
    out = nc.dram_tensor("out", (1, LAT, D), F32, kind="ExternalOutput").ap()
    build(nc, aps, out)
    r = run_bass_kernel_spmd(nc, [{f"in_{name}": a for name, a in arrays.items()}], core_ids=[0])
    return r.results[0]["out"]
```

```python
from contextlib import ExitStack, contextmanager

import numpy as np

import concourse.bass as bass
from concourse import mybir

F32 = mybir.dt.float32
F32R = mybir.dt.float32r
I32 = mybir.dt.int32
U32 = mybir.dt.uint32
ALU = mybir.AluOpType
ACT = mybir.ActivationFunctionType
AX = mybir.AxisListType

P = 128
D = 1024
KT = D // P
CTX, LAT = 256, 512
TOK = CTX + LAT
NB_C, NB_L = CTX // P, LAT // P
EPS = 1e-6
TAPS = 31
PAD = TAPS // 2
DFF = 4 * D
HD = 64
NEG = -1e30
N_EXP, E_FF = 16, 512
SLOTS_MAX = N_EXP + (2 * LAT - N_EXP) // P
LIST = SLOTS_MAX + 1
NORMS = 6
RING = 4
BUCKETS = 32
WIN = 128

C_BMOD, C_VEC, C_TAP_A, C_TAP_B = 0, 128, 256, 384
(V_N1, V_N1B, V_N2, V_N2B, V_CB, V_LG, V_LB, V_C, V_CC, V_AN, V_FN) = range(11)
TAP_SPLIT = 15
ACT_TAPS = 10

(M_ID, M_MEAN, M_HEAD, M_ROT, M_DUP0, M_DUP1, M_TRI, M_ONE, M_FLIP, M_SEL) = range(10)
N_MATS = 10


def shape_constants():
    m = np.zeros((N_MATS, P, P), np.float32)
    i = np.arange(P)
    m[M_ID] = np.eye(P)
    m[M_MEAN] = 1.0 / D
    m[M_HEAD] = (i[:, None] // HD == i[None, :] // HD) / float(HD)
    for d in range(P):
        if d % 32 < 16:
            m[M_ROT, d + 16, d] = -1.0
        else:
            m[M_ROT, d - 16, d] = 1.0
        m[M_DUP0, d % HD, d] = 1.0
        m[M_DUP1, HD + d % HD, d] = 1.0
    m[M_TRI] = i[:, None] < i[None, :]
    m[M_ONE] = 1.0
    m[M_FLIP] = (i[:, None] + i[None, :]) == P - 1
    quarter = 16
    inv = (np.float32(10000.0) ** (-np.arange(quarter, dtype=np.float32) / np.float32(quarter))).astype(np.float32)
    t = np.arange(LAT)
    row, col = (t // 64).astype(np.float32), (t % 64).astype(np.float32)
    ang = np.zeros((P, LAT), np.float32)
    for d in range(P):
        ang[d] = (row if (d % HD) < 32 else col) * inv[d % 16]
    rope = np.stack([np.cos(ang), np.sin(ang)]).astype(np.float32)
    one_hot = np.zeros((BUCKETS + 1, 3 * P), np.float32)
    half = BUCKETS // 2
    for c in range(3 * P):
        dist = 2 * WIN - 1 - c
        if 0 <= dist < WIN:
            if dist < half:
                b = dist
            else:
                b = half + int(np.float32(np.log(np.float32(dist) / np.float32(half))
                                          / np.float32(np.log(128 / half)) * np.float32(BUCKETS - half)))
                b = min(b, BUCKETS - 1)
            one_hot[b, c] = 1.0
        else:
            one_hot[BUCKETS, c] = 1.0
    group = np.zeros((8, 4, P), np.float32)
    for g in range(8):
        group[g, g // 2, (g % 2) * HD:(g % 2) * HD + HD] = 1.0
    ramp = np.zeros((P, 64), np.float32)
    ramp[:, 0:16] = np.arange(16) - 16.0
    ramp[:, 16:16 + LIST] = np.arange(LIST)
    ramp[:, 48:52] = np.arange(4) * 128.0
    ids = (i[:, None] + P * np.arange(4)[None, :]).astype(np.int32)
    return {"mats": m, "rope": rope, "one_hot": one_hot, "group": group.reshape(8, 4 * P),
            "ramp": ramp, "ids": ids}


class Program:

    def __init__(self, eng, chain=None, counts="cgqu"):
        self.eng, self.chain, self.counts = eng, chain, counts
        self.n = {"c": 0, "g": 0, "q": 0, "u": 0}
        self.r = {"c": 0, "g": 0, "q": 0, "u": 0}

    def at(self, key, more=0):
        return self.n[key] + more + self.r[key]

    def step(self, ins):
        ins.then_inc(self.chain, 1)
        self.n["c"] += 1
        self.eng.wait_ge(self.chain, self.at("c"))

    def laps(self):
        return self.n["g"] // RING + 1 + self.r["g"]

    @contextmanager
    def loop(self, count, start=0, **per):
        assert per.get("g", 0) % RING == 0
        per = {k: v for k, v in per.items() if k in self.counts}
        n0, r0 = dict(self.n), dict(self.r)
        with self.eng.Fori(start, count) as i:
            for k, v in per.items():
                if v:
                    self.r[k] = r0[k] + (i - start if start else i) * (v // RING if k == "g" else v)
            yield i
            for k in self.counts:
                assert self.n[k] - n0[k] == per.get(k, 0), (k, self.n[k] - n0[k], per)
        self.r = r0
        self.n = {k: n0[k] + (count - start) * per.get(k, 0) for k in self.n}


def build(nc, A, out):
    with ExitStack() as ctx:
        _build(nc, ctx, A, out)


def _build(nc, ctx, A, out):
    place = [16512]

    def region(nbytes):
        at = place[0]
        place[0] += nbytes
        assert place[0] <= 229344, place[0]
        return at

    def sb(name, shape, dt=F32, at=None):
        size = int(np.prod(shape[1:])) * 4
        size += -size % 32
        return nc.alloc_sbuf_tensor_at(name, shape, dt, offset=region(size) if at is None else at)

    class Sems(dict):
        def __missing__(self, name):
            self[name] = ctx.enter_context(nc.semaphore(name))
            return self[name]

    S = Sems()

    x = sb("x", [P, KT, TOK])
    ah_at = region(KT * TOK * 4)
    al_at = region(KT * TOK * 4)
    ah = sb("ah", [P, KT, TOK], F32R, ah_at)
    al = sb("al", [P, KT, TOK], F32R, al_at)
    h_at = region(4 * 4 * TOK * 4)
    u_at = region(KT * TOK * 4)
    raw_at = region(RING * D * 4)
    raw = [sb(f"raw{r}", [P, D], at=raw_at + 4 * D * r) for r in range(RING)]
    whi_at = region(2 * D * 4)
    whi = [sb(f"whi{r}", [P, D], F32R, whi_at + 4 * D * r) for r in range(2)]
    wlo = [sb(f"wlo{r}", [P, D], F32R) for r in range(2)]
    mats = sb("mats", [P, N_MATS - 1, P])
    cols = sb("cols", [P, 512])
    mod = sb("mod", [P, 96, 2])
    msc = sb("msc", [P, 4, KT, 2])
    qk_gain = sb("qk_gain", [P, 2])
    e_at = region(20480)

    hid_hi = [sb(f"hid_hi{b}", [P, 4, TOK], F32R, h_at + b * 4 * TOK * 4) for b in range(2)]
    hid_lo = [sb(f"hid_lo{b}", [P, 4, TOK], F32R, h_at + (2 + b) * 4 * TOK * 4) for b in range(2)]
    sq = sb("sq", [P, KT, TOK], at=h_at)
    squares = [sb(f"squares{b}", [P, TOK], at=u_at + 18432 + 3072 * b) for b in range(2)]
    square_sum = [sb("square_sum", [P, TOK], at=e_at + 9216),
                  sb("square_sum_last", [P, TOK], at=h_at)]
    cv_sum = sb("cv_sum", [P, TOK], at=h_at + 36864)
    y = sb("y", [P, KT, TOK], at=u_at)
    rstd = sb("rstd", [P, TOK], at=e_at)
    tmp = sb("tmp", [P, TOK], at=e_at + TOK * 4)
    tmp2 = sb("tmp2", [P, TOK], at=e_at + 2 * TOK * 4)
    tmp3 = sb("tmp3", [P, TOK], at=e_at + 3 * TOK * 4)
    xin = sb("xin", [P, NB_C + NB_L, D], at=u_at)
    vec_rows = sb("vec_rows", [P, 4, P], at=h_at)
    silu_c = sb("silu_c", [P, KT, P], at=h_at + 28672)
    mod_row = [sb(f"mod_row{b}", [P, 512], at=h_at + 32768 + 2048 * b) for b in range(2)]
    cv = sb("cv", [P, KT, TOK], at=u_at)
    sig = sb("sig", [P, TOK], at=h_at)
    upb = sb("upb", [P, PAD + CTX + PAD + LAT + PAD], at=h_at + 3072)
    csum = [sb(f"csum{b}", [P, CTX + PAD + LAT], at=h_at + 6400 + 3200 * b) for b in range(2)]
    taps = sb("taps", [P, 32], at=h_at + 12800)
    prod = [sb(f"prod{b}", [P, CTX + PAD + LAT], at=h_at + 13056 + 3200 * b) for b in range(3)]
    tap_sum = sb("tap_sum", [P, CTX + PAD + LAT], at=h_at + 22656)
    mu = sb("mu", [P, TOK], at=e_at + 4 * TOK * 4)
    zero_rows = sb("zero_rows", [P, D], at=u_at)
    qf = sb("qf", [P, KT, LAT], at=u_at)
    kf = sb("kf", [P, 2, TOK], at=u_at + KT * LAT * 4)
    vt = sb("vt", [P, 6, 256], at=h_at)
    kdup = sb("kdup", [P, 4, TOK], at=h_at + 6144)
    kst = [sb("kst0", [P, TOK], at=h_at + 18432), sb("kst1", [P, TOK], at=e_at + 3072)]
    vst = sb("vst", [P, 6, 2, HD], at=e_at)
    qst = sb("qst", [P, 2, LAT], at=h_at + 23040)
    pr = [sb(f"pr{b}", [P, TOK], at=h_at + 27136 + b * 3072) for b in range(2)]
    prt = sb("prt", [P, 6, LAT], at=h_at + 33280)
    stat = sb("stat", [P, 8], at=e_at + 5 * TOK * 4)
    rope = sb("rope", [P, 2, LAT], at=e_at + 16384)
    gu = sb("gu", [P, 4, LAT], at=u_at)
    gv = sb("gv", [P, NB_L, 4 * P], at=u_at + 8192)
    q2 = sb("q2", [P, 4, LAT], at=u_at + 16384)
    sg = sb("sg", [P, 16, LAT], at=h_at)
    kd2 = sb("kd2", [P, 4, P + LAT], at=h_at + 32768)
    v2 = sb("v2", [P, 5, 2, 2, HD], at=h_at + 43008)
    k2f = sb("k2f", [P, LAT], at=e_at)
    bias2 = x[:, :, 0:CTX]
    sc2 = [sb(f"sc2_{b}", [P, 4, 2 * P], at=e_at + 4096 * b) for b in range(2)]
    pt2 = sb("pt2", [P, 4, 2, P], at=e_at + 8192)
    wst = sb("wst", [P, 8, P], at=e_at + 12288)
    bsp = sb("bsp", [P, 4, P], at=e_at + 16384)
    gvn = sb("gvn", [P, LAT], at=e_at + 6144)
    st2 = sb("st2", [P, 2, 32], at=e_at + 18432)
    sinks = sb("sinks", [P, 8], at=e_at + 18688)
    gst = sb("gst", [P, 16], at=e_at + 18720)
    bias_rev = sb("bias_rev", [P, 8, 2 * P], at=u_at)
    ws_in = sb("ws_in", [P, 8, P], at=u_at + 8192)
    rel = sb("rel", [BUCKETS + 1, 8], at=u_at + 12288)
    one_hot = sb("one_hot", [BUCKETS + 1, 3 * P], at=u_at + 12320)
    rel_line = sb("rel_line", [8, 3 * P], at=u_at + 13856)
    bs_rows = sb("bs_rows", [8, P], at=u_at + 15392)
    group = sb("group", [8, 4 * P], at=u_at + 15904)
    mh = sb("mh", [P, KT, LAT], F32R, u_at)
    ml = sb("ml", [P, KT, LAT], F32R, e_at)
    wg = sb("wg", [P, KT, E_FF], at=ah_at)
    wu = sb("wu", [P, KT, E_FF], at=ah_at + 16384)
    wd = sb("wd", [P, 4, D], at=ah_at + 32768)
    ht = sb("ht", [P, NB_L, D], at=raw_at)
    fgain = sb("fgain", [P, D], at=whi_at)
    hn = sb("hn", [P, NB_L, D], at=h_at)
    xg = sb("xg", [P, D], at=h_at + 16384)
    xgt = sb("xgt", [P, KT, P], at=h_at + 20480)
    gate_s = sb("gate_s", [P, E_FF], at=h_at + 24576)
    hidt = sb("hidt", [P, E_FF], at=h_at + 26624)
    hidT = sb("hidT", [P, 4, P], at=h_at + 28672)
    yo = sb("yo", [P, D], at=h_at + 30720)
    rw = sb("rw", [P, KT, 20], at=h_at + 34816)
    rb = sb("rb", [P, 20], at=h_at + 35456)
    ramp = sb("ramp", [P, 64], at=h_at + 35552)
    ids = sb("ids", [P, 4], I32, h_at + 35808)
    lg = sb("lg", [P, 4, 20], at=h_at + 35840)
    rt = sb("rt", [P, 24, 64], at=h_at + 36160)
    pos_i = sb("pos_i", [P, 8], U32, h_at + 42304)
    idx_all = sb("idx_all", [P, LIST], I32, h_at + 42336)
    idx1 = sb("idx1", [P, 1], U32, h_at + 42464)
    meta = sb("meta", [P, 32], I32, h_at + 42496)
    zero_i = sb("zero_i", [P, LIST], I32, h_at + 42624)
    wk = sb("wk", [P, 2, NB_L], at=h_at + 42752)
    fin_s = sb("fin_s", [P, 8], at=h_at + 42784)
    ga = [sb(f"ga{n}", [P, D], at=ah_at + 4096 * n) for n in range(8)]
    osum = [sb(f"osum{n}", [P, D], at=ah_at + 4096 * (8 + n)) for n in range(4)]

    def pb(name):
        return ctx.enter_context(nc.psum_tensor(name, [P, 1024], F32))

    acc = [pb("acc0"), pb("acc1")]
    pa, pbk = pb("pa"), pb("pb")

    rel_t = nc.dram_tensor("rel_line_dram", [8, 3 * P], F32, kind="Internal")
    hn_d = nc.dram_tensor("normed_rows_dram", [LAT, D], F32, kind="Internal").ap()
    list_d = nc.dram_tensor("slot_list_dram", [LIST * P, 1], I32, kind="Internal").ap()
    yo_d = nc.dram_tensor("expert_rows_dram", [LIST * P, D], F32, kind="Internal").ap()


    FULL = [(0, CTX, 1), (CTX, TOK, 0)]
    LATENT = [(CTX, TOK, 0)]

    def token_cols(bank, c0=0):
        return bank[:, CTX + c0:CTX + TOK]

    def slots(e, n, one, units=1, steps=0):
        def slot(i):
            one(i)
            e.n["g"] += 1
            e.n["q"] += 1

        turns = n // RING
        if turns > 1 and n % RING == 0:
            with e.loop(turns, g=RING, q=RING, u=RING * units, c=RING * steps) as i:
                for j in range(RING):
                    slot(i * RING + j)
        else:
            turns = 0
        for j in range(turns * RING, n):
            slot(j)

    def split_only(e, n, one):
        def four(count):
            for _ in range(count):
                one()
                e.n["g"] += 1
                e.n["q"] += 1

        with e.loop(n // RING, g=RING, q=RING) as i:
            four(RING)
        four(n % RING)

    def qk_units(e, unit, steps=0):
        with e.loop(KT, c=steps) as i:
            unit(i, tile_of(qf, i, slice(0, LAT)), LAT)
        for j in range(2):
            unit(KT + j, kf[:, j, CTX:TOK], LAT)
        for j in range(2):
            unit(KT + 2 + j, kf[:, j, 0:CTX], CTX)

    def feed_forward(e, up, down, up_steps=0):
        def four(one, chunk, b):
            for j in range(4):
                one(chunk, j, b)
                e.n["g"] += 1
                e.n["q"] += 1

        four(up, 0, 0)
        with e.loop(3, g=16, q=16, u=24, c=8 * up_steps) as i:
            four(up, i * 2 + 1, 1)
            four(down, i * 2, 0)
            four(up, i * 2 + 2, 0)
            four(down, i * 2 + 1, 1)
        four(up, 7, 1)
        four(down, 6, 0)
        four(down, 7, 1)

    wide = CTX + PAD + LAT

    def load_slot(e, src, k):
        r = e.n["g"] % RING
        e.eng.wait_ge(S["lo_ready"], e.at("q", 1 - RING))
        e.eng.dma_start(raw[r][:, :].rearrange("p (k n) -> p k n", k=k),
                        src.rearrange("(k p) n -> p k n", p=P)).then_inc(S[f"raw_in{r}"], 16)

    def split_high(e):
        r = e.n["g"] % RING
        e.eng.wait_ge(S[f"raw_in{r}"], 16 * e.laps() if isinstance(e.laps(), int) else e.laps() * 16)
        e.eng.wait_ge(S["split_started"], e.at("q", 1))
        e.eng.activation(whi[e.n["q"] % 2][:, :], raw[r][:, :], ACT.Copy).then_inc(S["hi_ready"], 1)

    def split_first(e, split):
        split(e)
        e.n["g"] += 1
        e.n["q"] += 1

    def split_low(e):
        b = e.n["q"] % 2
        e.eng.wait_ge(S["hi_ready"], e.at("q", 1))
        e.eng.tensor_tensor(wlo[b][:, :], raw[e.n["g"] % RING][:, :], whi[b][:, :].bitcast(F32),
                            ALU.subtract).then_inc(S["lo_ready"], 1)

    def run_group(e, group, first=None, last=None, operand=None, per_tile=1):
        keys = [g[0] for g in group]
        ins = None
        for n, (key, o, w, m) in enumerate(group):
            if operand is not None and n % per_tile == 0:
                e.eng.wait_ge(S["al_ready"], KT * operand + n // per_tile + 1)
            ins = e.eng.matmul(o, w, m, start=keys.index(key) == n,
                               stop=len(keys) - 1 - keys[::-1].index(key) == n)
            if n == 0 and first:
                ins.then_inc(S[first], 1)
        if last:
            ins.then_inc(S[last], 1)

    def product(e, act_hi, act_lo, segs, k=KT, shift=0, out0=CTX, first="split_started",
                operand=None):
        h, l = whi[e.n["q"] % 2], wlo[e.n["q"] % 2]
        e.eng.wait_ge(S["lo_ready"], e.at("q", 1))
        wide = D // k
        for j in range(KT // k):
            bank = acc[e.n["u"] % 2]
            group = []
            for t in range(k):
                c = t * wide + j * P
                for w, a in ((h, act_hi), (h, act_lo), (l, act_hi)):
                    for s0, s1, _ in segs:
                        group.append((s0, bank[:, out0 + s0:out0 + s1], w[:, c:c + P], a[:, t + shift, s0:s1]))
            e.eng.wait_ge(S["acc_free"], e.at("u", 1))
            run_group(e, group, first if j == 0 else None, "acc_ready", operand, 3 * len(segs))
            e.n["u"] += 1

    def product_rows(e, blocks):
        h, l = whi[e.n["q"] % 2], wlo[e.n["q"] % 2]
        e.eng.wait_ge(S["lo_ready"], e.at("q", 1))
        e.eng.wait_ge(S["acc_free"], e.at("u", 1))
        bank = acc[e.n["u"] % 2]
        group = [(b, bank[:, CTX + b * P:CTX + b * P + P], a[:, t, b * P:b * P + P], w[:, t * P:t * P + P])
                 for b in blocks for t in range(KT) for a, w in ((ah, h), (ah, l), (al, h))]
        run_group(e, group, "split_started", "acc_ready")
        e.n["u"] += 1

    def sum_over_channels(e, src, segs, ready, done0):
        for t in range(KT):
            for sem in ready:
                e.eng.wait_ge(S[sem], done0 + t + 1)
            for s0, s1, _ in segs:
                ins = e.eng.matmul(pa[:, CTX + s0:CTX + s1], mats[:, M_MEAN, :], src[:, t, s0:s1],
                                   start=t == 0, stop=t == KT - 1)
        ins.then_inc(S["stat_ready"], 1)

    def take_unit(e):
        e.eng.wait_ge(S["acc_ready"], e.at("u", 1))
        return acc[e.n["u"] % 2]

    def free_unit(e, ins, then_read=False):
        ins.then_inc(S["acc_free"], 1)
        e.n["u"] += 1
        if then_read:
            e.eng.wait_ge(S["acc_free"], e.at("u", 2))

    def add_to_stream(e, tile_at, gate, segs):
        bank = take_unit(e)
        for s0, s1, v in segs:
            ins = e.eng.scalar_tensor_tensor(
                out=x[:, tile_at, s0:s1], in0=bank[:, CTX + s0:CTX + s1], scalar=mod[:, gate, v:v + 1],
                in1=x[:, tile_at, s0:s1], op0=ALU.mult, op1=ALU.add)
        free_unit(e, ins)

    def column(i):
        return bass.ds(i, 1)

    def tile_of(ap, i, *rest):
        return ap[(slice(None), bass.ds(i, 1)) + rest].rearrange("p a t -> p (a t)")

    def norm_act(e, n, k, segs, k_root, split=True, early=None):
        c0 = segs[0][0]
        total = square_sum[n == NORMS - 1]
        for i in range(KT):
            e.eng.wait_ge(S["acc_free"], e.at("u", 2 if n == 0 else 3 - KT + i))
            if i >= 3:
                e.eng.wait_ge(S["sq_added"], (KT - 1) * n + i - 2)
            e.eng.activation((squares[(i - 1) % 2] if i else total)[:, c0:TOK], x[:, i, c0:TOK],
                             ACT.Square).then_inc(S["sq_ready"], 1)
        if early:
            early()
        root(e, k_root, rstd[:, c0:TOK])
        if split:
            with e.loop(KT) as i:
                e.eng.wait_ge(S["y_ready"], i + (KT * max(k - 1, 0) + 1))
                e.eng.activation(tile_of(ah, i, slice(c0, TOK)), tile_of(y, i, slice(c0, TOK)),
                                 ACT.Copy).then_inc(S["ah_ready"], 1)

    def add_squares(e, n, segs):
        c0 = segs[0][0]
        total = square_sum[n == NORMS - 1][:, c0:TOK]
        for i in range(1, KT):
            e.eng.wait_ge(S["sq_ready"], KT * n + i + 1)
            if i >= 2:
                e.eng.wait_ge(S["sq_added"], (KT - 1) * n + i - 1)
            e.eng.tensor_tensor(total, total, squares[(i - 1) % 2][:, c0:TOK], ALU.add).then_inc(S["sq_added"], 1)

    def spread_mean(e, n, segs):
        e.eng.wait_ge(S["sq_added"], (KT - 1) * (n + 1))
        for s0, s1, _ in segs:
            ins = e.eng.matmul(pa[:, CTX + s0:CTX + s1], mats[:, M_MEAN, :], square_sum[n == NORMS - 1][:, s0:s1],
                               start=True, stop=True)
        ins.then_inc(S["stat_ready"], 1)

    def low_pool(e, k, segs):
        c0 = segs[0][0]
        with e.loop(KT) as i:
            e.eng.wait_ge(S["ah_ready"], i + (KT * k + 1))
            e.eng.tensor_tensor(tile_of(al, i, slice(c0, TOK)), tile_of(y, i, slice(c0, TOK)),
                                tile_of(ah, i, slice(c0, TOK)).bitcast(F32),
                                ALU.subtract).then_inc(S["al_ready"], 1)

    def reciprocal_for_root(e, ap):
        e.eng.reciprocal(ap, ap).then_inc(S["root_in"], 1)

    def root(e, k, ap):
        e.eng.wait_ge(S["root_in"], k)
        e.eng.activation(ap, ap, ACT.Sqrt).then_inc(S["root_out"], 1)

    def inverse_root(e, stats, segs, k_root):
        c0 = segs[0][0]
        e.eng.wait_ge(S["stat_ready"], stats)
        e.step(e.eng.tensor_scalar(rstd[:, c0:TOK], token_cols(pa, c0), EPS, None, ALU.add))
        reciprocal_for_root(e, rstd[:, c0:TOK])
        e.eng.wait_ge(S["root_out"], k_root)

    def norm_dve(e, stats, segs, k_root, y0, scale=None, shift=None, gain=None):
        c0 = segs[0][0]
        inverse_root(e, stats, segs, k_root)
        if gain is not None:
            with e.loop(KT) as i:
                e.eng.scalar_tensor_tensor(
                    out=tile_of(y, i, slice(c0, TOK)), in0=tile_of(x, i, slice(c0, TOK)),
                    scalar=cols[:, column(i + gain)], in1=rstd[:, c0:TOK],
                    op0=ALU.mult, op1=ALU.mult).then_inc(S["y_ready"], 1)
            return
        scaled = (tmp, tmp2)

        def by_root(i):
            if i >= 2:
                e.eng.wait_ge(S["y_ready"], y0 + i - 1)
            e.eng.tensor_tensor(scaled[i % 2][:, c0:TOK], x[:, i, c0:TOK], rstd[:, c0:TOK], ALU.mult
                                ).then_inc(e.chain, 1)
            e.n["c"] += 1

        by_root(0)
        for i in range(KT):
            if i + 1 < KT:
                by_root(i + 1)
            e.eng.wait_ge(e.chain, e.at("c", -1 if i + 1 < KT else 0))
            for s0, s1, v in segs:
                ins = e.eng.tensor_scalar(
                    y[:, i, s0:s1], scaled[i % 2][:, s0:s1], msc[:, scale, i:i + 1, v],
                    mod[:, i + shift:i + shift + 1, v], ALU.mult, ALU.add)
            ins.then_inc(S["y_ready"], 1)

    U_TOTAL = 6 + 16 + 8 + 96 + 12 + 8 + 96 + 30 + 16 + 8
    ctx.enter_context(nc.allow_non_contiguous_dma(reason="short rows of constants"))
    block = ctx.enter_context(nc.Block())

    @block.sync
    def _(sp):
        e = Program(sp, counts="gq")
        sp.dma_start(xin[:, 0:NB_C, :], A["ctx"][0].rearrange("(b p) d -> p b d", p=P)).then_inc(S["x_in"], 16)
        sp.dma_start(xin[:, NB_C:, :], A["x"][0].rearrange("(b p) d -> p b d", p=P)).then_inc(S["x_in"], 16)

        def load_direct(layer, chunk, k):
            r = e.n["g"] % RING
            sp.dma_start(raw[r][:, :].rearrange("p (k n) -> p k n", k=2),
                         A["w_mod"][layer, 256 * k:256 * k + 256, bass.ds(chunk * 512, 512)].rearrange(
                             "(k p) n -> p k n", p=P)).then_inc(S[f"raw_in{r}"], 16)
            e.n["g"] += 1

        for k in range(RING):
            load_direct(0, 0, k)
        with e.loop(4, start=1, g=RING) as i:
            for k in range(RING):
                sp.wait_ge(S["direct_done"], i * 4 + (k - 3))
                load_direct(0, i, k)
        pw1 = A["conv_w_pw1"][0]
        order = ["P"] * 2 + ["D"] * 8 + ["P"] * 2 + ["D"] * 12
        with e.loop(KT // 2, g=24, q=4) as i:
            for n, kind in enumerate(order):
                before = (order * 2)[24 + n - RING]
                at = order[:n - RING if n >= RING else 24 + n - RING].count(before) - (0 if n >= RING else order.count(before))
                if before == "D":
                    sp.wait_ge(S["direct_done"], i * 20 + (16 + at + 1))
                else:
                    sp.wait_ge(S["lo_ready"], i * 4 + (at + 1))
                here = order[:n].count(kind)
                if kind == "D":
                    if here < 8:
                        load_direct(0, i * 2 + (4 + here // 4), here % 4)
                    else:
                        load_direct(1, i * 3 + (here - 8) // 4, here % 4)
                else:
                    r = e.n["g"] % RING
                    sp.dma_start(raw[r][:, :].rearrange("p (k n) -> p k n", k=KT),
                                 pw1[:, bass.ds(i * 256 + (here // 2 * P + here % 2 * D), P)].rearrange(
                                     "(k p) n -> p k n", p=P)).then_inc(S[f"raw_in{r}"], 16)
                    e.n["g"] += 1
                    e.n["q"] += 1
        sp.wait_ge(S["direct_done"], 96)
        slots(e, KT, lambda i: load_slot(e, A["conv_w_pw2"][0][:, bass.ds(i * P, P)], KT))

        def load_ff(layer):
            up = A["w_ff1"][layer]
            down = A["w_ff2"][layer]
            feed_forward(
                e, lambda c, j, b: load_slot(e, up[:, bass.ds(c * 512 + j * P, P)], KT),
                lambda c, j, b: load_slot(e, down[bass.ds(c * 512, 512), j * 256:j * 256 + 256], 4))

        load_ff(0)
        slots(e, 12, lambda i: load_slot(e, A["gqa_w_qkv"][0][:, bass.ds(i * P, P)], KT))
        slots(e, KT, lambda i: load_slot(e, A["gqa_w_o"][0][:, bass.ds(i * P, P)], KT))
        load_ff(1)
        sp.wait_ge(S["al_ready"], KT * 5)
        sp.wait_ge(S["mask_row"], 1)
        for dst, src in ((rel[0:BUCKETS, :], A["rel_bias_2"]), (one_hot[:, :], A["one_hot"]),
                         (ws_in[:, :, :], A["gm_w_spatial_2"][0].rearrange("g t s -> t g s")),
                         (bs_rows[:, :], A["gm_b_spatial_2"][0]), (group[:, :], A["group"])):
            sp.dma_start(dst, src).then_inc(S["prep_in"], 16)
        sp.wait_ge(S["line_ready"], 1)
        sp.dma_start(rel_t.ap(), rel_line[:, :]).then_inc(S["line_out"], 16)
        sp.wait_ge(S["line_out"], 16)
        sp.dma_start(bias_rev[:, :, :], bass.AP(rel_t, 0, [[1, P], [3 * P, 8], [1, 2 * P]])).then_inc(S["rev_in"], 16)
        sp.dma_start(gvn[:, :], A["gm_v_norm_g_2"].to_broadcast([P, LAT])).then_inc(S["gains_in"], 16)
        sp.dma_start(sinks[:, :], A["attn_sinks_2"].to_broadcast([P, 8])).then_inc(S["gains_in"], 16)
        slots(e, 30, lambda i: load_slot(e, A["w_in_2"][0][:, bass.ds(i * P, P)], KT))

        def load_pair(i):
            pass
        with e.loop(2, g=4, q=4) as i:
            for s in range(2):
                for w in ("w_proj_a_2", "w_proj_b_2"):
                    load_slot(e, A[w][0][:, bass.ds(i * 512 + s * 256, 256)], 4)
                    e.n["g"] += 1
                    e.n["q"] += 1
        slots(e, KT, lambda i: load_slot(e, A["w_out_2"][0][:, bass.ds(i * P, P)], KT))
        sp.wait_ge(S["acc_ready"], U_TOTAL)
        sp.dma_start(rw[:, :, 0:4], A["router_group_w_2"][0].rearrange("(k p) n -> p k n", p=P)).then_inc(S["route_in"], 16)
        for g in range(4):
            sp.dma_start(rw[:, :, 4 + 4 * g:8 + 4 * g],
                         A["router_expert_w_2"][0, g].rearrange("(k p) n -> p k n", p=P)).then_inc(S["route_in"], 16)
        sp.dma_start(rb[:, 0:4], A["router_group_b_2"].to_broadcast([P, 4])).then_inc(S["route_in"], 16)
        sp.dma_start(rb[:, 4:20], A["router_expert_b_2"].rearrange("l g e -> l (g e)").to_broadcast([P, 16])
                     ).then_inc(S["route_in"], 16)
        sp.dma_start(ramp[:, :], A["ramp"]).then_inc(S["route_in"], 16)
        sp.dma_start(ids[:, :], A["ids"]).then_inc(S["route_in"], 16)
        sp.dma_start(fgain[:, :], A["final_norm_g_2"].rearrange("(a d) -> a d", a=1).to_broadcast([P, D])
                     ).then_inc(S["route_in"], 16)
        sp.wait_ge(S["hn_ready"], NB_L)
        sp.dma_start(hn_d.rearrange("(b p) d -> p b d", p=P), hn[:, :, :]).then_inc(S["hn_out"], 16)
        sp.wait_ge(S["meta_ready"], 1)
        n_blocks = sp.value_load(meta[0:1, LIST:LIST + 1], min_val=2 * LAT // P, max_val=SLOTS_MAX)
        with sp.Fori(0, n_blocks) as i:
            ex = sp.value_load(meta[0:1, bass.ds(i, 1)], min_val=0, max_val=N_EXP - 1)
            sp.wait_ge(S["gate_done"], i + 1)
            sp.dma_start(wg[:, :, :], A["expert_w_gate_2"][0, bass.ds(ex, 1)].rearrange(
                "e (p k) n -> p (e k) n", k=KT)).then_inc(S["wg_in"], 16)
            sp.wait_ge(S["up_done"], i + 1)
            sp.dma_start(wu[:, :, :], A["expert_w_up_2"][0, bass.ds(ex, 1)].rearrange(
                "e (p k) n -> p (e k) n", k=KT)).then_inc(S["wu_in"], 16)
            sp.wait_ge(S["down_done"], i + 1)
            sp.dma_start(wd[:, :, :], A["expert_w_down_2"][0, bass.ds(ex, 1)].rearrange(
                "e (p k) n -> p (e k) n", k=4)).then_inc(S["wd_in"], 16)
        for b in range(NB_L):
            sp.wait_ge(S["final_ready"], b + 1)
            sp.dma_start(out[0, b * P:b * P + P, :], osum[b][:, :]).then_inc(S["stored"], 16)
        sp.wait_ge(S["stored"], 16 * NB_L)

    @block.scalar
    def _(act):
        e = Program(act, S["act_chain"])
        vectors = [("norm1_g", 2), ("norm2_g", 2), ("conv_b_dw", 1), ("conv_ln_g", 1), ("conv_ln_b", 1),
                   ("c", 1), ("c_ctx", 1), ("attn_norm_g_2", 1), ("ffn_norm_g_2", 1)]
        act.dma_start(mats[:, :, :], A["mats"][0:N_MATS - 1].rearrange("n p q -> p n q")).then_inc(S["consts_in"], 16)
        act.dma_start(vec_rows[0:96, 0, :], A["b_mod"].rearrange("l (m p) -> (l m) p", p=P)).then_inc(S["consts_in"], 16)
        row = 0
        for name, count in vectors:
            src = A[name].rearrange("(c p) -> c p", p=P) if name == "c_ctx" else \
                A[name].rearrange("l (c p) -> (l c) p", p=P)
            act.dma_start(vec_rows[row:row + 8 * count, 1, :], src).then_inc(S["consts_in"], 16)
            row += 8 * count
        dw = A["conv_w_dw"][0].rearrange("t (c p) -> (t c) p", p=P)
        act.dma_start(vec_rows[0:120, 2, :], dw[0:120, :]).then_inc(S["consts_in"], 16)
        act.dma_start(vec_rows[0:128, 3, :], dw[120:248, :]).then_inc(S["consts_in"], 16)
        act.dma_start(rope[:, :, :], A["rope"].rearrange("n p t -> p n t")).then_inc(S["consts_in"], 16)
        for n, name in enumerate(("gqa_q_norm", "gqa_k_norm")):
            for h in range(2):
                act.dma_start(qk_gain[HD * h:HD * h + HD, n:n + 1],
                              A[name].rearrange("l (d o) -> (l d) o", o=1)).then_inc(S["consts_in"], 16)
        act.wait_ge(S["cols_ready"], 1)
        act.wait_ge(S["pad_zeroed"], 1)
        act.sem_inc(S["mod_copied"], 2)
        for v, c in enumerate((V_C, V_CC)):
            act.activation(silu_c[:, :, v], cols[:, C_VEC + 8 * c:C_VEC + 8 * c + 8], ACT.Silu
                           ).then_inc(S["silu_ready"], 1)

        def copy_row(n, b):
            act.wait_ge(S["direct_done"], n * 4 + 4)
            act.activation(mod_row[b][0:2, :], pa[0:2, 512 * b:512 * b + 512], ACT.Copy).then_inc(S["mod_copied"], 1)

        with e.loop(2) as i:
            for b in range(2):
                copy_row(i * 2 + b, b)
        e.n["g"] += 16
        e.n["u"] += NB_C + NB_L
        norm_act(e, 0, 0, FULL, 1)
        def projection_split():
            split_high(e)
            e.n["g"] += 1
            e.n["q"] += 1

        def tap_products(i, first, last):
            for j in range(first, last):
                t = TAPS - ACT_TAPS + j
                if j:
                    act.wait_ge(S["conv_added"], i * (ACT_TAPS - 1) + j)
                act.activation((prod[(j - 1) % 3] if j else tap_sum)[:, :], upb[:, t:t + wide], ACT.Copy,
                               scale=taps[:, t:t + 1]).then_inc(S["tap_product"], 1)

        def before_sigmoid(chunk0, chunks, i=None):
            projection_split()
            projection_split()
            if i is not None:
                act.wait_ge(S["acc_free"], e.at("u", 1))
                tap_products(i, 0, 4)
            copy_row(chunk0, 0)
            if i is not None:
                tap_products(i, 4, ACT_TAPS)
            for j in range(1, chunks):
                copy_row(chunk0 + j, j % 2)
            e.n["g"] += 4 * chunks
            e.n["u"] += 1
            act.wait_ge(S["acc_ready"], e.at("u", 1))
            act.activation(sig[:, :], token_cols(acc[e.n["u"] % 2]), ACT.Sigmoid).then_inc(S["sig_ready"], 1)
            e.n["u"] += 1

        before_sigmoid(4, 2)
        with e.loop(KT // 2 - 1, g=24, q=4, u=4) as i:
            before_sigmoid(i * 5 + 6, 3, i * 2)
            before_sigmoid(i * 5 + 9, 2, i * 2 + 1)
        before_sigmoid(21, 3, KT - 2)
        act.wait_ge(S["acc_free"], e.at("u", 1))
        tap_products(KT - 1, 0, ACT_TAPS)
        def high(*_):
            split_high(e)

        def early():
            split_first(e, split_high)

        with e.loop(KT) as i:
            act.wait_ge(S["centred"], i + 1)
            act.activation(tile_of(sq, i, slice(0, TOK)), tile_of(cv, i, slice(0, TOK)), ACT.Square
                           ).then_inc(S["ln_sq_ready"], 1)
        early()
        root(e, 2, rstd[:, :])
        with e.loop(KT, c=1) as i:
            act.wait_ge(S["ln_ready"], i + 1)
            e.step(act.activation(tile_of(y, i, slice(0, TOK)), tile_of(cv, i, slice(0, TOK)), ACT.Silu,
                                  bias=cols[:, column(i + (C_VEC + 8 * V_LB))],
                                  scale=cols[:, column(i + (C_VEC + 8 * V_LG))]))
            act.activation(tile_of(ah, i, slice(0, TOK)), tile_of(y, i, slice(0, TOK)), ACT.Copy
                           ).then_inc(S["ah_ready"], 1)

        slots(e, KT - 1, high, units=0)
        e.n["u"] += KT
        norm_act(e, 1, 2, FULL, 3, early=early)

        def high_ff():
            u0 = e.n["u"]
            split_only(e, 63, high)
            e.n["u"] = u0 + 96

        high_ff()
        norm_act(e, 2, 3, FULL, 4, early=early)
        slots(e, 11, high, units=0)
        e.n["u"] += 12
        act.wait_ge(S["acc_free"], e.at("u", 2))

        def squares(r, src, cols_n):
            act.wait_ge(S["qk_stat"], r + 1)
            act.activation(tmp2[:, 0:cols_n], src, ACT.Square).then_inc(S["qk_sq"], 1)
            root(e, r + 5, rstd[:, 0:cols_n])

        qk_units(e, squares)
        with e.loop(4) as i:
            def exps(m):
                act.wait_ge(S["nmax_ready"], i * 16 + (m + 1))
                if m >= 2:
                    act.wait_ge(S["turned"], i * 16 + (m - 1))
                b = m % 2
                act.activation(pr[b][:, :], acc[b][:, 0:TOK], ACT.Exp, bias=stat[:, 4 * b + 1:4 * b + 2],
                               scale=HD ** -0.5, accum_out=stat[:, 4 * b + 2:4 * b + 3]).then_inc(S["exp_done"], 1)

            exps(0)
            for m in range(16):
                if m + 1 < 16:
                    exps(m + 1)
                act.wait_ge(S["turned"], i * 16 + (m + 1))
                qb = m % 4
                act.activation(prt[:, :, qb * P:qb * P + P],
                               pa[:, 0:TOK].rearrange("p (k q) -> p k q", q=P), ACT.Copy).then_inc(S["prt_ready"], 1)
        slots(e, KT, high, units=0)
        e.n["u"] += KT
        norm_act(e, 3, 4, LATENT, 17, early=early)
        high_ff()
        norm_act(e, 4, 5, LATENT, 18, early=early)
        e.n["u"] += 1
        for _ in range(13):
            high()
            e.n["g"] += 1
            e.n["q"] += 1
            e.n["u"] += 1
        act.wait_ge(S["acc_free"], e.at("u", -6 + 2))
        for j in range(4):
            act.activation(gv[:, j, :], gv[:, j, :], ACT.Gelu_apprx_tanh).then_inc(S["gelu_done"], 1)
        for j in range(4):
            act.activation(gu[:, j, :], gu[:, j, :], ACT.Gelu_apprx_tanh).then_inc(S["gelu_done"], 1)
        with e.loop(4, g=4, q=4, u=4) as i:
            for j in range(4):
                high()
                e.n["g"] += 1
                e.n["q"] += 1
                e.n["u"] += 1
        root(e, 19, gst[:, 12:16])
        act.wait_ge(S["acc_free"], e.at("u", 2))
        with e.loop(16) as i:
            act.activation(tile_of(sg, i, slice(0, LAT)), tile_of(sg, i, slice(0, LAT)), ACT.Sigmoid
                           ).then_inc(S["gates_ready"], 1)
        for h in range(8):
            b = h % 2
            act.wait_ge(S["nm2_ready"], h + 1)
            for blk in range(4):
                act.activation(sc2[b][:, blk, :], sc2[b][:, blk, :], ACT.Exp, bias=st2[:, b, 4 + blk:5 + blk],
                               accum_out=st2[:, b, 8 + blk:9 + blk])
            act.activation(st2[:, b, 12:16], st2[:, b, 4:8], ACT.Exp, bias=sinks[:, h:h + 1]
                           ).then_inc(S["exp2_done"], 1)
            act.wait_ge(S["turned2"], h + 1)
            act.activation(pt2[:, :, :, :].rearrange("p a b q -> p (a b q)"), pa[:, :], ACT.Copy
                           ).then_inc(S["pt2_ready"], 1)
        with e.loop(2, g=4, q=4, u=8) as i:
            for j in range(4):
                high()
                e.n["g"] += 1
                e.n["q"] += 1
                e.n["u"] += 2
        slots(e, KT, high, units=0)
        e.n["u"] += KT
        norm_act(e, 5, 6, LATENT, 20, split=False)
        act.wait_ge(S["route_args"], 1)
        act.activation(rt[:, 1, 0:20], rt[:, 0, 0:20], ACT.Exp).then_inc(S["route_exp"], 1)
        act.sem_inc(S["yo_out"], 16)
        act.wait_ge(S["meta_ready"], 1)
        n_blocks = act.value_load(meta[0:1, LIST:LIST + 1], min_val=2 * LAT // P, max_val=SLOTS_MAX)
        with act.Fori(0, n_blocks) as i:
            act.wait_ge(S["gate_done"], i + 2)
            act.activation(gate_s[:, :], acc[0][:, 0:E_FF], ACT.Silu).then_inc(S["silu_gate"], 1)
            act.wait_ge(S["down_done"], i + 2)
            act.wait_ge(S["yo_out"], i * 16 + 16)
            act.activation(yo[:, 0:512], pbk[:, 0:512], ACT.Copy).then_inc(S["yo_act"], 1)
            act.wait_ge(S["yo_act"], i + 1)
            act.wait_ge(S["yo_dve"], i + 2)
            act.dma_start(yo_d[bass.ds(i * P, P), :], yo[:, :]).then_inc(S["yo_out"], 16)
        for b in range(NB_L):
            act.wait_ge(S["osum_ready"], b + 1)
            act.activation(ga[2 * b][:, :], osum[b][:, :], ACT.Square, accum_out=fin_s[:, b:b + 1]
                           ).then_inc(S["fin_sq"], 1)
            root(e, 21 + b, fin_s[:, 4 + b:5 + b])

    @block.gpsimd
    def _(pool):
        e = Program(pool, S["pool_chain"], "cgq")
        add_squares(e, 0, FULL)
        low_pool(e, 0, FULL)
        e.n["g"] += 16
        pool.sem_inc(S["conv_added"], 3)

        def projection_split():
            split_low(e)
            e.n["g"] += 1
            e.n["q"] += 1

        def add_products(i, first, last):
            for j in range(max(first, 1), last):
                pool.wait_ge(S["tap_product"], i * ACT_TAPS + (j + 1))
                pool.wait_ge(S["conv_added"], i * (ACT_TAPS - 1) + (j + 2))
                pool.tensor_tensor(tap_sum[:, :], tap_sum[:, :], prod[(j - 1) % 3][:, :], ALU.add
                                   ).then_inc(S["conv_added"], 1)

        def splits(chunks, i=None):
            projection_split()
            projection_split()
            if i is not None:
                add_products(i, 0, ACT_TAPS)
            e.n["g"] += 4 * chunks

        def add_tile(i):
            pool.wait_ge(S["cv_ready"], i + 1)
            if isinstance(i, int) and i == 0:
                pool.tensor_copy(cv_sum[:, :], cv[:, 0, :]).then_inc(S["cv_added"], 1)
                return
            pool.wait_ge(S["cv_added"], i)
            pool.tensor_tensor(cv_sum[:, :], cv_sum[:, :], tile_of(cv, i, slice(0, TOK)), ALU.add
                               ).then_inc(S["cv_added"], 1)

        splits(2)
        splits(3, 0)
        add_tile(0)
        splits(2, 1)
        with e.loop(KT // 2 - 2, g=24, q=4) as i:
            add_tile(i * 2 + 1)
            splits(3, i * 2 + 2)
            add_tile(i * 2 + 2)
            splits(2, i * 2 + 3)
        add_tile(KT - 3)
        splits(3, KT - 2)
        add_tile(KT - 2)
        add_products(KT - 1, 0, ACT_TAPS)
        add_tile(KT - 1)
        split_first(e, split_low)
        low_pool(e, 1, FULL)

        def low(*_):
            split_low(e)

        slots(e, KT - 1, low, units=0)
        add_squares(e, 1, FULL)
        split_first(e, split_low)
        low_pool(e, 2, FULL)
        pool.wait_ge(S["zero_rows_ready"], 1)
        pool.dma_start(yo_d.rearrange("(j p) d -> p j d", p=P),
                       zero_rows[:, :].unsqueeze(1).to_broadcast([P, LIST, D])).then_inc(S["rows_zeroed"], 16)
        split_only(e, 63, low)
        add_squares(e, 2, FULL)
        split_first(e, split_low)
        low_pool(e, 3, FULL)
        slots(e, 11, low, units=0)
        slots(e, KT, low, units=0)
        add_squares(e, 3, LATENT)
        split_first(e, split_low)
        low_pool(e, 4, LATENT)
        split_only(e, 63, low)
        pool.wait_ge(S["wst_ready"], 1)
        pool.affine_select(out=wst[:, :, :], in_=wst[:, :, :], compare_op=ALU.is_ge, fill=0.0, base=0,
                           pattern=[[0, 8], [1, P]], channel_multiplier=-1).then_inc(S["wst_masked"], 1)
        add_squares(e, 4, LATENT)
        split_first(e, split_low)
        low_pool(e, 5, LATENT)
        split_only(e, 27, low)
        for _ in range(2):
            low()
            e.n["g"] += 1
            e.n["q"] += 1
        slots(e, KT, low, units=0)
        slots(e, KT, low, units=0)
        add_squares(e, 5, LATENT)
        pool.wait_ge(S["acc_free"], U_TOTAL + 2)
        pool.memset(zero_i[:, :], 0).then_inc(S["zeroed"], 1)
        pool.wait_ge(S["zeroed"], 1)
        pool.dma_start(list_d.rearrange("(p j) o -> p (j o)", p=P), zero_i[:, :]).then_inc(S["list_zero"], 16)
        pool.wait_ge(S["list_zero"], 16)
        pool.wait_ge(S["pos_ready"], 1)
        pool.wait_ge(S["route_in"], 160)
        for n in range(2 * NB_L):
            pool.indirect_dma_start(
                out=list_d, out_offset=bass.IndirectOffsetOnAxis(ap=pos_i[:, n:n + 1], axis=0),
                in_=ids[:, n % NB_L:n % NB_L + 1], in_offset=None).then_inc(S["scattered"], 16)
            pool.wait_ge(S["scattered"], 16 * (n + 1))
        pool.dma_start(idx_all[:, :], list_d.rearrange("(j p) o -> p (j o)", p=P)).then_inc(S["idx_in"], 16)
        pool.wait_ge(S["idx_in"], 16)
        pool.wait_ge(S["hn_out"], 16)
        pool.wait_ge(S["meta_ready"], 1)
        n_blocks = pool.value_load(meta[0:1, LIST:LIST + 1], min_val=2 * LAT // P, max_val=SLOTS_MAX)
        with pool.Fori(0, n_blocks + 1) as i:
            pool.tensor_copy(idx1[:, :], idx_all[:, column(i)].bitcast(U32)).then_inc(S["idx_ready"], 1)
            pool.wait_ge(S["idx_ready"], i + 1)
            pool.wait_ge(S["xg_turned"], i + 1)
            pool.sem_inc(S["gathers"], 1)
            pool.indirect_dma_start(
                out=xg[:, :], out_offset=None, in_=hn_d,
                in_offset=bass.IndirectOffsetOnAxis(ap=idx1[:, 0:1], axis=0)).then_inc(S["xg_in"], 16)
            pool.wait_ge(S["xg_in"], i * 16 + 16)
        pool.wait_ge(S["yo_out"], (n_blocks + 1) * 16)
        pool.sem_inc(S["gathers"], 1)
        for n in range(NB_L):
            for k in range(2):
                pool.indirect_dma_start(
                    out=ga[2 * n + k][:, :], out_offset=None, in_=yo_d,
                    in_offset=bass.IndirectOffsetOnAxis(ap=pos_i[:, k * NB_L + n:k * NB_L + n + 1], axis=0)
                ).then_inc(S[f"rows_in{n}"], 16)

    @block.vector
    def _(dve):
        e = Program(dve, S["dve_chain"], "cu")
        TT, TS, STT = dve.tensor_tensor, dve.tensor_scalar, dve.scalar_tensor_tensor
        dve.sem_inc(S["acc_free"], 2)
        dve.sem_inc(S["mod_free"], 2)
        dve.memset(silu_c[:, :, :], 0.0).then_inc(S["pad_zeroed"], 1)
        dve.sem_inc(S["yo_dve"], 1)
        dve.sem_inc(S["heads_taken"], 2)
        dve.sem_inc(S["heads2_taken"], 2)
        dve.wait_ge(S["vec_turned"], 1)
        for n, rows in enumerate((96, 88, 120, 128)):
            ins = dve.tensor_copy(cols[:, P * n:P * n + rows], pbk[:, P * n:P * n + rows])
        ins.then_inc(S["cols_ready"], 1)
        dve.wait_ge(S["cols_ready"], 1)
        for b in range(NB_C + NB_L):
            bank = take_unit(e)
            free_unit(e, dve.tensor_copy(x[:, :, b * P:b * P + P], bank[:, :].rearrange("p (k t) -> p k t", t=P)))

        def modulation(at, ps, n):
            return TT(mod[:, bass.ds(at, n), :], pbk[:, ps:ps + 2 * n].rearrange("p (n v) -> p n v", v=2),
                      cols[:, bass.ds(at, n)].unsqueeze(2).to_broadcast([P, n, 2]), ALU.add)

        def scales(n, layer, chunk, gain):
            return STT(out=msc[:, n, :, :], in0=mod[:, layer * 48 + chunk * 8:layer * 48 + chunk * 8 + 8, :],
                       scalar=1.0, in1=cols[:, C_VEC + 8 * gain:C_VEC + 8 * gain + 8].unsqueeze(2).to_broadcast([P, KT, 2]),
                       op0=ALU.add, op1=ALU.mult)

        with e.loop(2) as i:
            for b in range(2):
                dve.wait_ge(S["mod_turned"], i * 2 + (b + 1))
                modulation(i * 8 + 4 * b, 512 * b, 4).then_inc(S["mod_free"], 1)
        dve.wait_ge(S["mod_free"], 2 + 4)
        e.step(scales(0, 0, 1, V_N1))
        norm_dve(e, 1, FULL, 1, 0, scale=0, shift=0)
        e.step(dve.memset(upb[:, :], 0.0))
        tap_a = cols[:, C_TAP_A:C_TAP_A + 8 * TAP_SPLIT].rearrange("p (t c) -> p t c", c=8)
        tap_b = cols[:, C_TAP_B:C_TAP_B + 8 * (TAPS - TAP_SPLIT)].rearrange("p (t c) -> p t c", c=8)
        def conv_tile(i, turned, at, n, base):
            dve.tensor_copy(taps[:, 0:TAP_SPLIT], tap_a[:, :, column(i)].rearrange("p t c -> p (t c)"))
            dve.tensor_copy(taps[:, TAP_SPLIT:TAPS], tap_b[:, :, column(i)].rearrange("p t c -> p (t c)"))
            e.step(dve.tensor_copy(taps[:, TAPS:TAPS + 1], cols[:, column(i + (C_VEC + 8 * V_CB))]))
            bank = take_unit(e)
            dve.wait_ge(S["sig_ready"], i + 1)
            TT(upb[:, PAD:PAD + CTX], bank[:, CTX:2 * CTX], sig[:, 0:CTX], ALU.mult)
            free_unit(e, TT(upb[:, 2 * PAD + CTX:2 * PAD + TOK], bank[:, 2 * CTX:], sig[:, CTX:TOK], ALU.mult),
                      then_read=True)
            free_unit(e, TS(csum[0][:, :], upb[:, 0:wide], taps[:, 0:1], taps[:, TAPS:TAPS + 1], ALU.mult, ALU.add))
            TS(csum[1][:, :], upb[:, 1:1 + wide], taps[:, 1:2], None, ALU.mult).then_inc(S["dve_chain"], 1)
            e.n["c"] += 1
            for t in range(2, TAPS - ACT_TAPS):
                if t == 2:
                    dve.wait_ge(S["acc_free"], e.at("u", 2))
                else:
                    dve.wait_ge(S["dve_chain"], e.at("c", -1))
                part = csum[t % 2][:, :]
                STT(out=part, in0=upb[:, t:t + wide], scalar=taps[:, t:t + 1], in1=part,
                    op0=ALU.mult, op1=ALU.add).then_inc(S["dve_chain"], 1)
                e.n["c"] += 1
            dve.wait_ge(S["dve_chain"], e.at("c"))
            e.step(TT(csum[0][:, :], csum[0][:, :], csum[1][:, :], ALU.add))
            dve.wait_ge(S["conv_added"], i * (ACT_TAPS - 1) + (ACT_TAPS + 2))
            TT(tile_of(cv, i, slice(0, CTX)), csum[0][:, 0:CTX], tap_sum[:, 0:CTX], ALU.add)
            e.step(TT(tile_of(cv, i, slice(CTX, TOK)), csum[0][:, CTX + PAD:], tap_sum[:, CTX + PAD:], ALU.add))
            dve.sem_inc(S["cv_ready"], 1)
            dve.wait_ge(S["mod_turned"], turned)
            modulation(at, base, n).then_inc(S["mod_free"], 1)

        with e.loop(KT // 2, u=4, c=2 * (2 + TAPS - ACT_TAPS)) as i:
            conv_tile(i * 2, i * 5 + 6, i * 8 + 16, 8, 512)
            conv_tile(i * 2 + 1, i * 5 + 9, i * 12 + 48, 12, 0)
        dve.wait_ge(S["mod_free"], 2 + 4 + KT)
        scales(1, 0, 4, V_N2)
        scales(2, 1, 1, V_N1B)
        e.step(scales(3, 1, 4, V_N2B))
        dve.wait_ge(S["stat_ready"], 2)
        e.step(dve.tensor_copy(mu[:, :], token_cols(pa)))
        with e.loop(KT) as i:
            TT(tile_of(cv, i, slice(0, TOK)), tile_of(cv, i, slice(0, TOK)), mu[:, :], ALU.subtract
               ).then_inc(S["centred"], 1)
        inverse_root(e, 3, FULL, 2)
        with e.loop(KT) as i:
            TT(tile_of(cv, i, slice(0, TOK)), tile_of(cv, i, slice(0, TOK)), rstd[:, :], ALU.mult
               ).then_inc(S["ln_ready"], 1)
        def to_stream(gate, segs):
            def one(i):
                bank = take_unit(e)
                for s0, s1, v in segs:
                    xs = tile_of(x, i, slice(s0, s1))
                    ins = STT(out=xs, in0=bank[:, CTX + s0:CTX + s1], scalar=mod[:, column(i + gate), v], in1=xs,
                              op0=ALU.mult, op1=ALU.add)
                free_unit(e, ins)
            return one

        def mlp(layer, segs):
            c0 = segs[0][0]

            def up(chunk, j, b):
                bank = take_unit(e)
                free_unit(e, TS(tmp[:, c0:TOK], token_cols(bank, c0), 0.0, None, ALU.max), then_read=True)
                e.step(TT(tmp2[:, c0:TOK], tmp[:, c0:TOK], tmp[:, c0:TOK], ALU.mult))
                e.step(dve.tensor_copy(hid_hi[b][:, j, c0:TOK], tmp2[:, c0:TOK]))
                TT(hid_lo[b][:, j, c0:TOK], tmp2[:, c0:TOK], hid_hi[b][:, j, c0:TOK].bitcast(F32), ALU.subtract
                   ).then_inc(S["hid_ready"], 1)

            def down(chunk, j, b):
                for n in (2 * j, 2 * j + 1):
                    bank = take_unit(e)
                    for s0, s1, v in segs:
                        g = layer * 48 + 40 + n
                        ins = STT(out=x[:, n, s0:s1], in0=bank[:, CTX + s0:CTX + s1], scalar=mod[:, g, v:v + 1],
                                  in1=x[:, n, s0:s1], op0=ALU.mult, op1=ALU.add)
                    free_unit(e, ins)

            feed_forward(e, up, down, up_steps=2)

        slots(e, KT, to_stream(16, FULL))
        norm_dve(e, 4, FULL, 3, 8, scale=1, shift=24)
        dve.wait_ge(S["al_ready"], KT * 3)
        dve.memset(zero_rows[:, :], 0.0).then_inc(S["zero_rows_ready"], 1)
        mlp(0, FULL)
        dve.wait_ge(S["rows_zeroed"], 16)
        norm_dve(e, 5, FULL, 4, 16, scale=2, shift=48)

        def to_q(i):
            bank = take_unit(e)
            free_unit(e, dve.tensor_copy(tile_of(qf, i, slice(0, LAT)), bank[:, 512:1024]))

        slots(e, KT, to_q)
        for j in range(2):
            bank = take_unit(e)
            free_unit(e, dve.tensor_copy(kf[:, j, :], token_cols(bank)))
            e.n["g"] += 1
            e.n["q"] += 1
        for j in range(2):
            bank = take_unit(e)
            free_unit(e, dve.tensor_copy(vt[:, :, j * P:j * P + P],
                                         token_cols(bank).rearrange("p (b n) -> p b n", n=P)))
            e.n["g"] += 1
            e.n["q"] += 1
        dve.wait_ge(S["acc_free"], e.at("u", 2))

        def norm_rope(r, src, n):
            is_q = not isinstance(r, int)
            turns = is_q or r < KT + 2
            gain = qk_gain[:, 0:1] if is_q else qk_gain[:, 1:2]
            dve.wait_ge(S["qk_stat"], r + 2)
            e.step(TS(rstd[:, 0:n], pa[:, 0:n], EPS, None, ALU.add))
            reciprocal_for_root(e, rstd[:, 0:n])
            dve.wait_ge(S["root_out"], r + 5)
            if not turns:
                STT(out=src, in0=src, scalar=gain, in1=rstd[:, 0:n], op0=ALU.mult, op1=ALU.mult
                    ).then_inc(S["qk_normed"], 1)
                dve.wait_ge(S["qk_normed"], r + 1)
                return
            STT(out=tmp[:, 0:n], in0=src, scalar=gain, in1=rstd[:, 0:n], op0=ALU.mult, op1=ALU.mult
                ).then_inc(S["qk_normed"], 1)
            dve.wait_ge(S["qk_normed"], r + 1)
            TT(tmp3[:, 0:n], tmp[:, 0:n], rope[:, 0, :], ALU.mult)
            dve.wait_ge(S["qk_rotated"], r + 1)
            e.step(TT(src, pbk[:, 0:n], rope[:, 1, :], ALU.mult))
            e.step(TT(src, src, tmp3[:, 0:n], ALU.add))

        qk_units(e, norm_rope, steps=3)
        dve.wait_ge(S["qk_normed"], KT + 4)
        dve.sem_inc(S["k_ready"], 1)
        for kv in range(4):
            dve.wait_ge(S["k_doubled"], kv + 1)
            dve.tensor_copy(kdup[:, kv, :], token_cols((pa, pbk)[kv % 2])).then_inc(S["kdup_ready"], 1)
        dve.wait_ge(S["kdup_ready"], 4)
        dve.memset(kst[0][HD:P, :], 0.0)
        dve.memset(kst[1][0:HD, :], 0.0)
        with e.loop(4, c=2 * 16 + 4) as i:
            keys = tile_of(kdup, i, slice(0, TOK))
            dve.tensor_copy(kst[0][0:HD, :], keys[0:HD, :])
            dve.tensor_copy(kst[1][HD:P, :], keys[HD:P, :])
            for twice in range(2):
                dve.tensor_copy(vst[:, :, twice, :], vt[:, :, bass.ds(i * HD, HD)])
            dve.tensor_copy(qst[:, 0, :], tile_of(qf, i * 2, slice(0, LAT)))
            dve.tensor_copy(qst[:, 1, :], tile_of(qf, i * 2 + 1, slice(0, LAT))).then_inc(S["staged"], 1)

            def maxima(m):
                s = 4 * (m % 2)
                dve.wait_ge(S["scores_ready"], i * 16 + (m + 1))
                e.step(dve.tensor_reduce(stat[:, s:s + 1], acc[m % 2][:, 0:TOK], AX.X, ALU.max))
                TS(stat[:, s + 1:s + 2], stat[:, s:s + 1], -HD ** -0.5, None, ALU.mult).then_inc(S["nmax_ready"], 1)

            def normalise(m):
                s = 4 * (m % 2)
                dve.wait_ge(S["exp_done"], i * 16 + (m + 1))
                e.step(dve.reciprocal(stat[:, s + 3:s + 4], stat[:, s + 2:s + 3]))
                TS(pr[m % 2][:, :], pr[m % 2][:, :], stat[:, s + 3:s + 4], None, ALU.mult
                   ).then_inc(S["probs_ready"], 1)

            def take_head(n):
                t, h = n // 2, n % 2
                rows = slice(HD * h, HD * h + HD)
                dve.wait_ge(S["heads_done"], i * 4 + (n + 1))
                o = pbk[rows, 512 * h:512 * h + LAT]
                hi, lo = (tile_of(part, i * 2 + t, slice(CTX, TOK))[rows, :] for part in (ah, al))
                e.step(dve.tensor_copy(hi, o))
                TT(lo, o, hi.bitcast(F32), ALU.subtract).then_inc(S["heads_taken"], 1)

            maxima(0)
            maxima(1)
            for m in range(16):
                normalise(m)
                if m + 2 < 16:
                    maxima(m + 2)
                if m % 4 == 0 and m:
                    take_head(m // 4 - 1)
            take_head(3)
        dve.wait_ge(S["heads_taken"], 2 + 16)
        dve.sem_inc(S["attended"], 1)
        slots(e, KT, to_stream(48 + 16, LATENT))
        norm_dve(e, 6, LATENT, 17, 24, scale=3, shift=72)
        dve.wait_ge(S["al_ready"], KT * 5)
        dve.memset(rel[:, :], NEG).then_inc(S["mask_row"], 1)
        mlp(1, LATENT)

        dve.wait_ge(S["rel_ready"], 1)
        dve.tensor_copy(rel_line[:, :], pbk[0:8, 0:3 * P]).then_inc(S["line_ready"], 1)
        dve.wait_ge(S["rev_turned"], 2)
        for n, bank in enumerate((pa, pbk)):
            dve.tensor_copy(bias2[:, 4 * n:4 * n + 4, :], bank[:, :].rearrange("p (h s) -> p h s", h=4)
                            ).then_inc(S["bias_done"], 1)
        dve.wait_ge(S["ws_turned"], 1)
        dve.tensor_copy(wst[:, :, :], pa[:, :].rearrange("p (g t) -> p g t", g=8)).then_inc(S["wst_ready"], 1)
        dve.wait_ge(S["bs_spread"], 1)
        e.step(dve.tensor_copy(bsp[:, :, :], pbk[:, 0:512].rearrange("p (t q) -> p t q", t=4)))
        norm_dve(e, 7, LATENT, 18, 32, gain=C_VEC + 8 * V_AN)

        def keep(dst, n=None):
            bank = take_unit(e)
            src = bank[:, 512:1024]
            free_unit(e, dve.tensor_copy(dst, src if n is None else src.rearrange("p (b n) -> p b n", n=n)))
            e.n["g"] += 1
            e.n["q"] += 1

        for j in range(4):
            keep(gu[:, j, :])
        for j in range(4):
            keep(gv[:, :, j * P:j * P + P], P)
        for j in range(4):
            keep(q2[:, j, :])
        keep(k2f[:, :])
        bank = take_unit(e)
        for twice in range(2):
            ins = dve.tensor_copy(v2[:, 1:5, :, twice, :],
                                  bank[:, 512:1024].rearrange("p (b g d) -> p b g d", b=NB_L, g=2))
        free_unit(e, ins)
        e.n["g"] += 1
        e.n["q"] += 1
        with e.loop(4, g=4, q=4, u=4) as i:
            for j in range(4):
                keep(tile_of(sg, i * 4 + j, slice(0, LAT)))
        dve.wait_ge(S["acc_free"], e.at("u", 2))

        dve.memset(v2[:, 0, :, :, :], 0.0)
        dve.memset(kd2[:, :, 0:P], 0.0)
        for kv in range(2):
            dve.wait_ge(S["k2_doubled"], kv + 1)
            for j in range(2):
                rows, others = slice(HD * j, HD * j + HD), slice(HD - HD * j, P - HD * j)
                dve.memset(kd2[others, 2 * kv + j, P:], 0.0)
                ins = dve.tensor_copy(kd2[rows, 2 * kv + j, P:], (pa, pbk)[kv][rows, 0:LAT])
            ins.then_inc(S["kd2_ready"], 1)

        dve.wait_ge(S["gelu_done"], 8)
        dve.wait_ge(S["gains_in"], 32)
        e.step(dve.tensor_reduce(gst[:, 0:4], gv[:, :, :], AX.X, ALU.add))
        e.step(TS(gst[:, 4:8], gst[:, 0:4], 1.0 / 512, None, ALU.mult))
        for b in range(4):
            e.step(TS(gv[:, b, :], gv[:, b, :], gst[:, 4 + b:5 + b], None, ALU.subtract))
            e.step(STT(out=tmp[:, 0:LAT], in0=gv[:, b, :], scalar=1.0, in1=gv[:, b, :], op0=ALU.mult, op1=ALU.mult,
                       accum_out=gst[:, 8 + b:9 + b]))
        e.step(TS(gst[:, 12:16], gst[:, 8:12], 1.0 / 512, EPS, ALU.mult, ALU.add))
        reciprocal_for_root(e, gst[:, 12:16])
        dve.wait_ge(S["root_out"], 19)
        for b in range(4):
            STT(out=gv[:, b, :], in0=gv[:, b, :], scalar=gst[:, 12 + b:13 + b], in1=gvn[:, :], op0=ALU.mult,
                op1=ALU.mult).then_inc(S["gv_ready"], 1)
        dve.wait_ge(S["gv_ready"], 4)
        for t in range(4):
            dve.wait_ge(S["spatial_done"], t + 1)
            s = (pa, pbk)[t // 2][:, (t % 2) * 512:(t % 2) * 512 + 512].rearrange("p (c q) -> p c q", q=P)
            t4 = tmp[:, 0:LAT].rearrange("p (c q) -> p c q", q=P)
            e.step(TT(t4, s, bsp[:, t, :].unsqueeze(1).to_broadcast([P, 4, P]), ALU.add))
            e.step(TT(tmp[:, 0:LAT], tmp[:, 0:LAT], gu[:, t, :], ALU.mult))
            e.step(dve.tensor_copy(ah[:, t, CTX:TOK], tmp[:, 0:LAT]))
            e.step(TT(al[:, t, CTX:TOK], tmp[:, 0:LAT], ah[:, t, CTX:TOK].bitcast(F32), ALU.subtract))

        def logits(h):
            b = h % 2
            dve.wait_ge(S["scores2"], h + 1)
            if h >= 2:
                dve.wait_ge(S["turned2"], h - 1)
            e.step(STT(out=sc2[b][:, :, :], in0=acc[b][:, :].rearrange("p (c s) -> p c s", c=4), scalar=HD ** -0.5,
                       in1=bias2[:, h, :].unsqueeze(1).to_broadcast([P, 4, 2 * P]), op0=ALU.mult, op1=ALU.add))
            e.step(dve.memset(sc2[b][:, 0, 0:P], NEG))
            e.step(dve.tensor_reduce(st2[:, b, 0:4], sc2[b][:, :, :], AX.X, ALU.max))
            TS(st2[:, b, 4:8], st2[:, b, 0:4], sinks[:, h:h + 1], -1.0, ALU.max, ALU.mult
               ).then_inc(S["nm2_ready"], 1)

        def take_head2(h):
            rows = slice(HD * (h % 2), HD * (h % 2) + HD)
            dve.wait_ge(S["heads2"], h + 1)
            o = pbk[rows, (h % 2) * 512:(h % 2) * 512 + 512]
            hi, lo = ah[rows, 4 + h // 2, CTX:TOK], al[rows, 4 + h // 2, CTX:TOK]
            e.step(dve.tensor_copy(hi, o))
            TT(lo, o, hi.bitcast(F32), ALU.subtract).then_inc(S["heads2_taken"], 1)

        logits(0)
        for h in range(8):
            b = h % 2
            if h + 1 < 8:
                logits(h + 1)
            dve.wait_ge(S["exp2_done"], h + 1)
            e.step(TT(st2[:, b, 16:20], st2[:, b, 8:12], st2[:, b, 12:16], ALU.add))
            e.step(dve.reciprocal(st2[:, b, 20:24], st2[:, b, 16:20]))
            TT(sc2[b][:, :, :], sc2[b][:, :, :], st2[:, b, 20:24].unsqueeze(2).to_broadcast([P, 4, 2 * P]), ALU.mult
               ).then_inc(S["probs2"], 1)
            if h >= 1:
                take_head2(h - 1)
        take_head2(7)

        dve.wait_ge(S["gates_ready"], 16)
        with e.loop(2, g=4, q=4, u=8, c=8) as i:
            for s in range(2):
                for branch in range(2):
                    for j in range(2):
                        n = i * 4 + (2 * s + j)
                        bank = take_unit(e)
                        g = tile_of(sg, n + 8 * branch, slice(0, LAT))
                        free_unit(e, TT(g, bank[:, 512:1024], g, ALU.mult), then_read=True)
                    e.n["g"] += 1
                    e.n["q"] += 1
                for j in range(2):
                    n = i * 4 + (2 * s + j)
                    g0, g1 = tile_of(sg, n, slice(0, LAT)), tile_of(sg, n + 8, slice(0, LAT))
                    e.step(TT(g0, g0, g1, ALU.add))
                    e.step(dve.tensor_copy(tile_of(mh, n, slice(0, LAT)), g0))
                    TT(tile_of(ml, n, slice(0, LAT)), g0, tile_of(mh, n, slice(0, LAT)).bitcast(F32), ALU.subtract
                       ).then_inc(S["merged"], 1)

        def plain(i):
            bank = take_unit(e)
            xs = tile_of(x, i, slice(CTX, TOK))
            free_unit(e, TT(xs, bank[:, 512:1024], xs, ALU.add))

        slots(e, KT, plain)
        norm_dve(e, 8, LATENT, 20, 40, gain=C_VEC + 8 * V_FN)

        for b in range(NB_L):
            bank = take_unit(e)
            free_unit(e, dve.tensor_copy(hn[:, b, :], bank[:, :]), then_read=True)
            dve.sem_inc(S["hn_ready"], 1)
        dve.wait_ge(S["logits_done"], 1)
        dve.wait_ge(S["route_in"], 160)

        def line(n, a=4, b=4):
            return rt[:, n, 0:a * b].rearrange("p (a b) -> p a b", a=a)

        def spread(ap, n):
            return ap.unsqueeze(2).to_broadcast([P, ap.shape[1], n])

        from16 = ramp[:, 0:4].unsqueeze(1).to_broadcast([P, 4, 4])

        def first_of_max(dst, src, most, s1, s2):
            e.step(dve.tensor_reduce(most, src, AX.X, ALU.max))
            e.step(TT(s1, src, spread(most, 4), ALU.is_equal))
            e.step(TT(s1, s1, from16, ALU.mult))
            e.step(dve.tensor_reduce(s2, s1, AX.X, ALU.min))
            e.step(TT(dst, from16, spread(s2, 4), ALU.is_equal))

        e.step(TT(lg[:, :, :], pbk[:, 0:80].rearrange("p (b n) -> p b n", b=4),
                  rb[:, :].unsqueeze(1).to_broadcast([P, 4, 20]), ALU.add))
        oh_g, oh_1, oh_2 = line(2), line(3), line(4)
        gm, m1, m2 = rt[:, 5, 0:4], rt[:, 5, 4:8], rt[:, 5, 8:12]
        first_of_max(oh_g, lg[:, :, 0:4], gm, line(6), rt[:, 7, 0:4])
        e.step(TT(line(0), lg[:, :, 0:4], spread(gm, 4), ALU.subtract))
        four = rt[:, 8, 0:64].rearrange("p (b g e) -> p b g e", b=4, g=4)
        e.step(TT(four, lg[:, :, 4:20].rearrange("p b (g e) -> p b g e", g=4),
                  oh_g.unsqueeze(3).to_broadcast([P, 4, 4, 4]), ALU.mult))
        el = line(9)
        e.step(dve.tensor_reduce(el, four.rearrange("p b g e -> p b e g"), AX.X, ALU.add))
        first_of_max(oh_1, el, m1, line(6), rt[:, 7, 0:4])
        el2 = line(10)
        e.step(STT(out=el2, in0=oh_1, scalar=NEG, in1=el, op0=ALU.mult, op1=ALU.add))
        first_of_max(oh_2, el2, m2, line(6), rt[:, 7, 0:4])
        TT(rt[:, 0, 16:20], m2, m1, ALU.subtract).then_inc(S["route_args"], 1)
        pick = [rt[:, 11 + k, 0:64].rearrange("p (b n) -> p b n", b=4) for k in range(3)]
        for k, oh in enumerate((oh_1, oh_2)):
            e.step(TT(pick[k].rearrange("p b (g e) -> p b g e", g=4), oh_g.unsqueeze(3).to_broadcast([P, 4, 4, 4]),
                      oh.unsqueeze(2).to_broadcast([P, 4, 4, 4]), ALU.mult))
        TT(pick[2], pick[0], pick[1], ALU.add).then_inc(S["picks_ready"], 1)
        dve.wait_ge(S["route_exp"], 1)
        e.step(dve.tensor_reduce(rt[:, 7, 4:8], line(1), AX.X, ALU.add))
        e.step(TS(rt[:, 7, 8:12], rt[:, 1, 16:20], 1.0, None, ALU.add))
        e.step(dve.reciprocal(rt[:, 7, 12:16], rt[:, 7, 4:8]))
        e.step(dve.reciprocal(rt[:, 7, 16:20], rt[:, 7, 8:12]))
        e.step(TT(wk[:, 0, :], rt[:, 7, 12:16], rt[:, 7, 16:20], ALU.mult))
        e.step(TT(wk[:, 1, :], wk[:, 0, :], rt[:, 1, 16:20], ALU.mult))
        dve.wait_ge(S["ranks_done"], 1)
        n16 = rt[:, 14, 0:16]
        e.step(dve.tensor_copy(n16, pbk[:, 576:592]))
        e.step(TT(rt[:, 15, 0:64].rearrange("p (n k) -> p n k", k=4), spread(n16, 4),
                  ramp[:, 48:52].unsqueeze(1).to_broadcast([P, 16, 4]), ALU.is_gt))
        nb, even, odd = rt[:, 16, 0:16], rt[:, 16, 16:32], rt[:, 16, 32:48]
        e.step(dve.tensor_reduce(nb, rt[:, 15, 0:64].rearrange("p (n k) -> p n k", k=4), AX.X, ALU.add))
        src, dst = nb, even
        for shift in (1, 2, 4, 8):
            e.step(dve.tensor_copy(dst[:, 0:shift], src[:, 0:shift]))
            e.step(TT(dst[:, shift:16], src[:, shift:16], src[:, 0:16 - shift], ALU.add))
            src, dst = dst, (odd if dst is even else even)
        upto = src
        base = rt[:, 17, 0:16]
        e.step(TT(base, upto, nb, ALU.subtract))
        e.step(TS(base, base, float(P), None, ALU.mult))
        where = rt[:, 18, 0:64].rearrange("p (b n) -> p b n", b=4)
        e.step(TT(where, pbk[:, 512:576].rearrange("p (b n) -> p b n", b=4),
                  base.unsqueeze(1).to_broadcast([P, 4, 16]), ALU.add))
        prod = rt[:, 19, 0:64].rearrange("p (b n) -> p b n", b=4)
        for k in range(2):
            e.step(TT(prod, pick[k], where, ALU.mult))
            e.step(dve.tensor_reduce(rt[:, 20, 4 * k:4 * k + 4], prod, AX.X, ALU.add))
        dve.tensor_copy(pos_i[:, :], rt[:, 20, 0:8]).then_inc(S["pos_ready"], 1)
        table = rt[:, 0:6, :].rearrange("p a b -> p (a b)").rearrange("p (j n) -> p j n", n=16)
        e.step(TT(table, upto.unsqueeze(1).to_broadcast([P, LIST, 16]), spread(ramp[:, 16:16 + LIST], 16), ALU.is_le))
        e.step(dve.tensor_reduce(rt[:, 21, 0:LIST], table, AX.X, ALU.add))
        e.step(TS(rt[:, 21, 0:LIST], rt[:, 21, 0:LIST], float(N_EXP - 1), None, ALU.min))
        e.step(dve.tensor_copy(rt[:, 21, LIST:LIST + 1], upto[:, 15:16]))
        dve.tensor_copy(meta[:, 0:LIST + 1], rt[:, 21, 0:LIST + 1]).then_inc(S["meta_ready"], 1)
        for b in range(NB_L):
            bank = take_unit(e)
            free_unit(e, dve.tensor_copy(ht[:, b, :], bank[:, :]))
        dve.wait_ge(S["meta_ready"], 1)
        n_blocks = dve.value_load(meta[0:1, LIST:LIST + 1], min_val=2 * LAT // P, max_val=SLOTS_MAX)

        def take_rows(v):
            dve.wait_ge(S["xg_turned"], v)
            dve.tensor_copy(xgt[:, :, :], pa[:, :].rearrange("p (k q) -> p k q", q=P)).then_inc(S["xgt_ready"], 1)

        take_rows(2)
        with dve.Fori(0, n_blocks) as i:
            dve.wait_ge(S["silu_gate"], i + 1)
            dve.wait_ge(S["up_done"], i + 2)
            TT(hidt[:, :], gate_s[:, :], acc[0][:, 512:1024], ALU.mult).then_inc(S["hidt_ready"], 1)
            take_rows(i + 3)
            dve.wait_ge(S["hid_turned"], i + 1)
            dve.tensor_copy(hidT[:, :, :], acc[1][:, 0:E_FF].rearrange("p (k q) -> p k q", q=P)
                            ).then_inc(S["hidT_ready"], 1)
            dve.wait_ge(S["down_done"], i + 2)
            dve.wait_ge(S["yo_out"], i * 16 + 16)
            dve.tensor_copy(yo[:, 512:1024], pbk[:, 512:1024]).then_inc(S["yo_dve"], 1)
        for b in range(NB_L):
            dve.wait_ge(S[f"rows_in{b}"], 32)
            e.step(STT(out=osum[b][:, :], in0=ga[2 * b][:, :], scalar=wk[:, 0, b:b + 1], in1=ht[:, b, :],
                       op0=ALU.mult, op1=ALU.add))
            STT(out=osum[b][:, :], in0=ga[2 * b + 1][:, :], scalar=wk[:, 1, b:b + 1], in1=osum[b][:, :],
                op0=ALU.mult, op1=ALU.add).then_inc(S["osum_ready"], 1)
            dve.wait_ge(S["fin_sq"], b + 1)
            e.step(TS(fin_s[:, 4 + b:5 + b], fin_s[:, b:b + 1], 1.0 / D, EPS, ALU.mult, ALU.add))
            reciprocal_for_root(e, fin_s[:, 4 + b:5 + b])
            dve.wait_ge(S["root_out"], 21 + b)
            STT(out=osum[b][:, :], in0=osum[b][:, :], scalar=fin_s[:, 4 + b:5 + b], in1=fgain[:, :],
                op0=ALU.mult, op1=ALU.mult).then_inc(S["final_ready"], 1)

    @block.tensor
    def _(pe):
        e = Program(pe, counts="gqu")
        ident = mats[:, M_ID, :]
        pe.sem_inc(S["split_started"], 1)
        pe.sem_inc(S["qk_stat"], 1)
        for name in ("gate_done", "up_done", "down_done", "xg_turned"):
            pe.sem_inc(S[name], 1)
        pe.wait_ge(S["consts_in"], 16 * 18)
        for n, rows in enumerate((96, 88, 120, 128)):
            ins = pe.transpose(pbk[:, P * n:P * n + rows], vec_rows[0:rows, n, :], ident[0:rows, 0:rows])
        ins.then_inc(S["vec_turned"], 1)
        pe.wait_ge(S["x_in"], 32)

        def turn_unit(rows):
            pe.wait_ge(S["acc_free"], e.at("u", 1))
            for k in range(KT):
                ins = pe.transpose(acc[e.n["u"] % 2][:, k * P:k * P + P], rows(k), ident)
            ins.then_inc(S["acc_ready"], 1)
            e.n["u"] += 1

        for b in range(NB_C + NB_L):
            turn_unit(lambda k: xin[:, b, k * P:k * P + P])

        def mod_chunk(n, b, after_product=False, last_copied=0):
            pe.wait_ge(S["mod_copied"], n + (1 + last_copied))
            for s in range(4):
                r = e.n["g"] % RING
                pe.wait_ge(S[f"raw_in{r}"], 16 * e.laps() if isinstance(e.laps(), int) else e.laps() * 16)
                for k in range(2):
                    ins = pe.matmul(pa[:, 512 * b:512 * b + 512], silu_c[:, 2 * s + k, :],
                                    raw[r][:, 512 * k:512 * k + 512], start=s == 0 and k == 0, stop=s == 3 and k == 1)
                    if after_product and s == 0 and k == 0:
                        ins.then_inc(S["split_started"], 1)
                ins.then_inc(S["direct_done"], 1)
                e.n["g"] += 1

        def turn_mod(n, b, at):
            pe.wait_ge(S["mod_copied"], n + 3)
            pe.sem_inc(S["rows_to_turn"], 1)
            for j in range(4):
                ins = pe.transpose(pbk[:, at + 2 * j:at + 2 * j + 2], mod_row[b][0:2, P * j:P * j + P],
                                   ident[0:2, 0:2])
            ins.then_inc(S["mod_turned"], 1)

        pe.wait_ge(S["silu_ready"], 2)
        with e.loop(2, g=8) as i:
            for b in range(2):
                mod_chunk(i * 2 + b, b)
                pe.wait_ge(S["mod_free"], i * 2 + (b + 1))
                turn_mod(i * 2 + b, b, 512 * b)
        spread_mean(e, 0, FULL)

        def conv_tile(i, chunk0, chunks, base):
            g0 = e.n["g"]

            def modulate(j):
                e.n["g"] = g0 + 2 + 4 * j
                mod_chunk(chunk0 + j, j % 2, after_product=j < 2, last_copied=int(j == 0))

            def projection(n):
                e.n["g"] = g0 + n
                product(e, ah, al, FULL, first=None)
                e.n["q"] += 1

            modulate(0)
            pe.wait_ge(S["al_ready"], KT)
            projection(0)
            modulate(1)
            pe.wait_ge(S["mod_free"], i + 5)
            turn_mod(chunk0, 0, base)
            if chunks == 3:
                modulate(2)
            projection(1)
            for j in range(1, chunks):
                turn_mod(chunk0 + j, j % 2, base + 8 * j)
            e.n["g"] = g0 + 2 + 4 * chunks

        pe.wait_ge(S["y_ready"], 1)
        with e.loop(KT // 2, g=24, q=4, u=4) as i:
            conv_tile(i * 2, i * 5 + 4, 2, 512)
            conv_tile(i * 2 + 1, i * 5 + 6, 3, 0)
        pe.wait_ge(S["cv_added"], KT)
        for s0, s1, _ in FULL:
            ins = pe.matmul(pa[:, CTX + s0:CTX + s1], mats[:, M_MEAN, :], cv_sum[:, s0:s1], start=True, stop=True)
        ins.then_inc(S["stat_ready"], 1)
        sum_over_channels(e, sq, FULL, ["ln_sq_ready"], 0)

        def first_and_rest(segs, n, operand):
            for i in range(n):
                product(e, ah, al, segs, operand=None if i else operand)
                e.n["g"] += 1
                e.n["q"] += 1

        def tile(segs, hi=ah, lo=al, **kw):
            return lambda i: product(e, hi, lo, segs, **kw)

        first_and_rest(FULL, KT, 1)

        def mlp(segs, hidden0, operand):
            def down(chunk, j, b):
                if j == 0:
                    pe.wait_ge(S["hid_ready"], chunk * 4 + (hidden0 + 4))
                product(e, hid_hi[b], hid_lo[b], segs, k=4)

            feed_forward(e, lambda chunk, j, b: product(
                e, ah, al, segs, operand=operand if isinstance(chunk, int) and chunk + j == 0 else None), down)

        spread_mean(e, 1, FULL)
        mlp(FULL, 0, 2)
        spread_mean(e, 2, FULL)
        first_and_rest(LATENT, KT, 3)
        for _ in range(2):
            product(e, ah, al, FULL)
            e.n["g"] += 1
            e.n["q"] += 1
        for _ in range(2):
            product_rows(e, range(NB_C + NB_L))
            e.n["g"] += 1
            e.n["q"] += 1

        def head_sums(r, src, n):
            turns = not isinstance(r, int) or r < KT + 2
            pe.wait_ge(S["qk_sq"], r + 1)
            pe.matmul(pa[:, 0:n], mats[:, M_HEAD, :], tmp2[:, 0:n], start=True, stop=True).then_inc(S["qk_stat"], 1)
            pe.wait_ge(S["qk_normed"], r + 1)
            if turns:
                pe.matmul(pbk[:, 0:n], mats[:, M_ROT, :], tmp[:, 0:n], start=True, stop=True
                          ).then_inc(S["qk_rotated"], 1)

        qk_units(e, head_sums)
        pe.wait_ge(S["k_ready"], 1)
        for kv in range(4):
            if kv >= 2:
                pe.wait_ge(S["kdup_ready"], kv - 1)
            for s0, s1, _ in FULL:
                ins = pe.matmul((pa, pbk)[kv % 2][:, CTX + s0:CTX + s1], mats[:, M_DUP0 + kv % 2, :],
                                kf[:, kv // 2, s0:s1], start=True, stop=True)
            ins.then_inc(S["k_doubled"], 1)
        with e.loop(4) as i:
            def scores(m):
                t, h, qb = m // 8, (m // 4) % 2, m % 4
                if m >= 2:
                    pe.wait_ge(S["exp_done"], i * 16 + (m - 1))
                for k0, k1 in ((0, 512), (512, TOK)):
                    ins = pe.matmul(acc[m % 2][:, k0:k1], qst[:, t, qb * P:qb * P + P], kst[h][:, k0:k1],
                                    start=True, stop=True)
                ins.then_inc(S["scores_ready"], 1)

            def values(n):
                pe.wait_ge(S["prt_ready"], i * 16 + (4 * n + 4))
                pe.wait_ge(S["heads_taken"], i * 4 + (n + 1))
                for k in range(6):
                    ins = pe.matmul(pbk[:, 512 * (n % 2):512 * (n % 2) + LAT],
                                    vst[:, k, :, :].rearrange("p a d -> p (a d)"), prt[:, k, :],
                                    start=k == 0, stop=k == 5)
                ins.then_inc(S["heads_done"], 1)

            pe.wait_ge(S["staged"], i + 1)
            scores(0)
            scores(1)
            for m in range(16):
                if m + 2 < 16:
                    scores(m + 2)
                if m % 4 == 0 and m:
                    values(m // 4 - 1)
                pe.wait_ge(S["probs_ready"], i * 16 + (m + 1))
                if m >= 1:
                    pe.wait_ge(S["prt_ready"], i * 16 + m)
                for k in range(6):
                    ins = pe.transpose(pa[:, k * P:k * P + P], pr[m % 2][:, k * P:k * P + P], ident)
                ins.then_inc(S["turned"], 1)
            values(3)
        pe.wait_ge(S["attended"], 1)
        slots(e, KT, tile(LATENT))
        spread_mean(e, 3, LATENT)
        mlp(LATENT, 32, 4)
        pe.wait_ge(S["prep_in"], 80)
        pe.wait_ge(S["mask_row"], 1)
        pe.matmul(pbk[0:8, 0:3 * P], rel[:, :], one_hot[:, :], start=True, stop=True).then_inc(S["rel_ready"], 1)
        pe.wait_ge(S["rev_in"], 16)
        for n, bank in enumerate((pa, pbk)):
            for j in range(2):
                ins = pe.matmul(bank[:, 512 * j:512 * j + 512], mats[:, M_FLIP, :],
                                bias_rev[:, 4 * n + 2 * j:4 * n + 2 * j + 2, :].rearrange("p h s -> p (h s)"),
                                start=True, stop=True)
            ins.then_inc(S["rev_turned"], 1)
        pe.wait_ge(S["bias_done"], 2)
        for g in range(8):
            ins = pe.transpose(pa[:, g * P:g * P + P], ws_in[:, g, :], ident)
        ins.then_inc(S["ws_turned"], 1)
        for t in range(4):
            ins = pe.matmul(pbk[:, t * P:t * P + P], group[:, t * P:t * P + P], bs_rows[:, :], start=True, stop=True)
        ins.then_inc(S["bs_spread"], 1)
        pe.wait_ge(S["wst_ready"], 1)
        spread_mean(e, 4, LATENT)

        def used():
            e.n["g"] += 1
            e.n["q"] += 1

        for n in range(14):
            if n in (4, 5, 6, 7, 13):
                product_rows(e, range(NB_C, NB_C + NB_L))
            else:
                product(e, ah, al, LATENT, operand=None if n else 5)
            used()
        with e.loop(4, g=4, q=4, u=4) as i:
            for j in range(4):
                product(e, ah, al, LATENT)
                used()
        pe.wait_ge(S["acc_free"], e.at("u", 2))
        for kv in range(2):
            pe.matmul((pa, pbk)[kv][:, 0:LAT], mats[:, M_DUP0 + kv, :], k2f[:, :], start=True, stop=True
                      ).then_inc(S["k2_doubled"], 1)
        pe.wait_ge(S["kd2_ready"], 2)
        pe.wait_ge(S["gv_ready"], 4)
        pe.wait_ge(S["wst_masked"], 1)
        for t in range(4):
            for h in range(2):
                g = 2 * t + h
                for c in range(4):
                    at = (t % 2) * 512 + c * P
                    ins = pe.matmul((pa, pbk)[t // 2][HD * h:HD * h + HD, at:at + P], gv[:, c, g * HD:g * HD + HD],
                                    wst[:, g, :], start=True, stop=True)
            ins.then_inc(S["spatial_done"], 1)

        def scores2(h):
            if h >= 2:
                pe.wait_ge(S["nm2_ready"], h - 1)
            for blk in range(4):
                ins = pe.matmul(acc[h % 2][:, blk * 2 * P:blk * 2 * P + 2 * P],
                                q2[:, h // 2, blk * P:blk * P + P],
                                kd2[:, 2 * (h // 4) + h % 2, blk * P:blk * P + 2 * P],
                                start=True, stop=True)
            ins.then_inc(S["scores2"], 1)

        def values2(h):
            pe.wait_ge(S["pt2_ready"], h + 1)
            pe.wait_ge(S["heads2_taken"], h + 1)
            for blk in range(4):
                at = (h % 2) * 512 + blk * P
                for kk in range(2):
                    ins = pe.matmul(pbk[:, at:at + P], v2[:, blk + kk, h // 4, :, :].rearrange("p a d -> p (a d)"),
                                    pt2[:, blk, kk, :], start=kk == 0, stop=kk == 1)
            ins.then_inc(S["heads2"], 1)

        scores2(0)
        scores2(1)
        for h in range(8):
            if h + 2 < 8:
                scores2(h + 2)
            if h >= 1:
                values2(h - 1)
            pe.wait_ge(S["probs2"], h + 1)
            for blk in range(4):
                for kk in range(2):
                    at = (2 * blk + kk) * P
                    ins = pe.transpose(pa[:, at:at + P], sc2[h % 2][:, blk, kk * P:kk * P + P], ident)
            ins.then_inc(S["turned2"], 1)
        values2(7)
        pe.wait_ge(S["heads2_taken"], 2 + 8)
        with e.loop(2, g=4, q=4, u=8) as i:
            for s in range(2):
                for branch in range(2):
                    product(e, ah, al, LATENT, k=4, shift=4 * branch)
                    used()
        pe.wait_ge(S["merged"], 8)
        slots(e, KT, tile([(0, LAT, 0)], mh, ml, out0=512))
        spread_mean(e, 5, LATENT)
        pe.wait_ge(S["y_ready"], KT * 6)
        for b in range(NB_L):
            turn_unit(lambda k: y[:, k, CTX + b * P:CTX + b * P + P])
        pe.wait_ge(S["route_in"], 160)
        for b in range(NB_L):
            for k in range(KT):
                ins = pe.matmul(pbk[:, 20 * b:20 * b + 20], y[:, k, CTX + b * P:CTX + b * P + P], rw[:, k, :],
                                start=k == 0, stop=k == KT - 1)
        ins.then_inc(S["logits_done"], 1)
        pe.wait_ge(S["picks_ready"], 1)
        both = rt[:, 13, 0:64].rearrange("p (b n) -> p b n", b=4)
        for b in range(NB_L):
            for c in range(b + 1):
                pe.matmul(pbk[:, 512 + 16 * b:528 + 16 * b], mats[:, M_TRI if c == b else M_ONE, :], both[:, c, :],
                          start=c == 0, stop=c == b)
        for c in range(NB_L):
            ins = pe.matmul(pbk[:, 576:592], mats[:, M_ONE, :], both[:, c, :], start=c == 0, stop=c == NB_L - 1)
        ins.then_inc(S["ranks_done"], 1)
        for b in range(NB_L):
            turn_unit(lambda k: x[:, k, CTX + b * P:CTX + b * P + P])
        pe.wait_ge(S["meta_ready"], 1)
        n_blocks = pe.value_load(meta[0:1, LIST:LIST + 1], min_val=2 * LAT // P, max_val=SLOTS_MAX)

        def turn_rows(v):
            pe.wait_ge(S["xg_in"], v)
            for k in range(KT):
                ins = pe.transpose(pa[:, k * P:k * P + P], xg[:, :].rearrange("q (p k) -> q k p", k=KT)[:, k, :], ident)
            ins.then_inc(S["xg_turned"], 1)

        pe.wait_ge(S["acc_free"], e.at("u", 2))
        turn_rows(16)
        with pe.Fori(0, n_blocks) as i:
            pe.wait_ge(S["xgt_ready"], i + 1)
            for name, w, c0 in (("wg_in", wg, 0), ("wu_in", wu, 512)):
                pe.wait_ge(S[name], i * 16 + 16)
                for k in range(KT):
                    ins = pe.matmul(acc[0][:, c0:c0 + E_FF], xgt[:, k, :], w[:, k, :], start=k == 0, stop=k == KT - 1)
                ins.then_inc(S["gate_done" if c0 == 0 else "up_done"], 1)
            turn_rows(i * 16 + 32)
            pe.wait_ge(S["hidt_ready"], i + 1)
            for k in range(4):
                ins = pe.transpose(acc[1][:, k * P:k * P + P],
                                   hidt[:, :].rearrange("q (p k) -> q k p", k=4)[:, k, :], ident)
            ins.then_inc(S["hid_turned"], 1)
            pe.wait_ge(S["hidT_ready"], i + 1)
            pe.wait_ge(S["wd_in"], i * 16 + 16)
            pe.wait_ge(S["yo_dve"], i + 1)
            for half in range(2):
                for k in range(4):
                    ins = pe.matmul(pbk[:, 512 * half:512 * half + 512], hidT[:, k, :],
                                    wd[:, k, 512 * half:512 * half + 512], start=k == 0, stop=k == 3)
            ins.then_inc(S["down_done"], 1)


_USED = ['x', 'c', 'ctx', 'c_ctx', 'norm1_g', 'norm2_g', 'w_mod', 'b_mod', 'w_ff1', 'w_ff2', 'conv_w_pw1',
         'conv_w_dw', 'conv_b_dw', 'conv_ln_g', 'conv_ln_b', 'conv_w_pw2', 'gqa_w_qkv', 'gqa_q_norm',
         'gqa_k_norm', 'gqa_w_o', 'attn_norm_g_2', 'w_in_2', 'gm_v_norm_g_2', 'gm_w_spatial_2',
         'gm_b_spatial_2', 'attn_sinks_2', 'rel_bias_2', 'w_proj_a_2', 'w_proj_b_2', 'w_out_2',
         'ffn_norm_g_2', 'router_group_w_2', 'router_group_b_2', 'router_expert_w_2', 'router_expert_b_2',
         'expert_w_gate_2', 'expert_w_up_2', 'expert_w_down_2', 'final_norm_g_2']


def kernel(**inputs):
    import concourse.bacc as bacc
    from concourse.bass_utils import run_bass_kernel_spmd

    nc = bacc.Bacc("TRN2", target_bir_lowering=False, num_devices=1)
    arrays = {name: np.ascontiguousarray(inputs[name]) for name in _USED}
    arrays.update(shape_constants())
    aps = {name: nc.dram_tensor(f"in_{name}", a.shape, mybir.dt.from_np(a.dtype), kind="ExternalInput").ap()
           for name, a in arrays.items()}
    out = nc.dram_tensor("out", (1, LAT, D), F32, kind="ExternalOutput").ap()
    build(nc, aps, out)
    r = run_bass_kernel_spmd(nc, [{f"in_{name}": a for name, a in arrays.items()}], core_ids=[0])
    return r.results[0]["out"]
```

```python
from contextlib import ExitStack, contextmanager

import numpy as np

import concourse.bass as bass
from concourse import mybir

F32 = mybir.dt.float32
F32R = mybir.dt.float32r
I32 = mybir.dt.int32
U32 = mybir.dt.uint32
ALU = mybir.AluOpType
ACT = mybir.ActivationFunctionType
AX = mybir.AxisListType

P = 128
D = 1024
KT = D // P
CTX, LAT = 256, 512
TOK = CTX + LAT
NB_C, NB_L = CTX // P, LAT // P
EPS = 1e-6
TAPS = 31
PAD = TAPS // 2
DFF = 4 * D
HD = 64
NEG = -1e30
N_EXP, E_FF = 16, 512
SLOTS_MAX = N_EXP + (2 * LAT - N_EXP) // P
LIST = SLOTS_MAX + 1
QK_UNITS = 12
AL_POOL = 6
NORMS = 6
RING = 4
BUCKETS = 32
WIN = 128

C_BMOD, C_VEC, C_TAP_A, C_TAP_B = 0, 128, 256, 384
(V_N1, V_N1B, V_N2, V_N2B, V_CB, V_LG, V_LB, V_C, V_CC, V_AN, V_FN) = range(11)
TAP_SPLIT = 15
ACT_TAPS = 10

(M_ID, M_MEAN, M_ROT, M_DUP0, M_DUP1, M_TRI, M_ONE, M_FLIP) = range(8)
N_MATS = 8


def shape_constants():
    m = np.zeros((N_MATS, P, P), np.float32)
    i = np.arange(P)
    m[M_ID] = np.eye(P)
    m[M_MEAN] = 1.0 / D
    for d in range(P):
        if d % 32 < 16:
            m[M_ROT, d + 16, d] = -1.0
        else:
            m[M_ROT, d - 16, d] = 1.0
        m[M_DUP0, d % HD, d] = 1.0
        m[M_DUP1, HD + d % HD, d] = 1.0
    m[M_TRI] = i[:, None] < i[None, :]
    m[M_ONE] = 1.0
    m[M_FLIP] = (i[:, None] + i[None, :]) == P - 1
    quarter = 16
    inv = (np.float32(10000.0) ** (-np.arange(quarter, dtype=np.float32) / np.float32(quarter))).astype(np.float32)
    t = np.arange(LAT)
    row, col = (t // 64).astype(np.float32), (t % 64).astype(np.float32)
    ang = np.zeros((P, LAT), np.float32)
    for d in range(P):
        ang[d] = (row if (d % HD) < 32 else col) * inv[d % 16]
    rope = np.stack([np.cos(ang), np.sin(ang)]).astype(np.float32)
    one_hot = np.zeros((BUCKETS + 1, 3 * P), np.float32)
    half = BUCKETS // 2
    for c in range(3 * P):
        dist = 2 * WIN - 1 - c
        if 0 <= dist < WIN:
            if dist < half:
                b = dist
            else:
                b = half + int(np.float32(np.log(np.float32(dist) / np.float32(half))
                                          / np.float32(np.log(128 / half)) * np.float32(BUCKETS - half)))
                b = min(b, BUCKETS - 1)
            one_hot[b, c] = 1.0
        else:
            one_hot[BUCKETS, c] = 1.0
    head_pick = np.zeros((P, 2 * P), np.float32)
    head_pick[i, P + i // HD] = 1.0 / HD
    head_spread = np.zeros((P, QK_UNITS, P), np.float32)
    for n in range(QK_UNITS):
        head_spread[2 * n + i // HD, n, i] = 1.0
    group = np.zeros((8, 4, P), np.float32)
    for g in range(8):
        group[g, g // 2, (g % 2) * HD:(g % 2) * HD + HD] = 1.0
    ramp = np.zeros((P, 64), np.float32)
    ramp[:, 0:16] = np.arange(16) - 16.0
    ramp[:, 16:16 + LIST] = np.arange(LIST)
    ramp[:, 48:52] = np.arange(4) * 128.0
    ids = (i[:, None] + P * np.arange(4)[None, :]).astype(np.int32)
    return {"mats": m, "rope": rope, "one_hot": one_hot, "group": group.reshape(8, 4 * P),
            "ramp": ramp, "ids": ids, "head_pick": head_pick, "head_spread": head_spread}


class Program:

    def __init__(self, eng, chain=None, counts="cgqu"):
        self.eng, self.chain, self.counts = eng, chain, counts
        self.n = {"c": 0, "g": 0, "q": 0, "u": 0}
        self.r = {"c": 0, "g": 0, "q": 0, "u": 0}

    def at(self, key, more=0):
        return self.n[key] + more + self.r[key]

    def step(self, ins):
        ins.then_inc(self.chain, 1)
        self.n["c"] += 1
        self.eng.wait_ge(self.chain, self.at("c"))

    def laps(self):
        return self.n["g"] // RING + 1 + self.r["g"]

    @contextmanager
    def loop(self, count, start=0, **per):
        assert per.get("g", 0) % RING == 0
        per = {k: v for k, v in per.items() if k in self.counts}
        n0, r0 = dict(self.n), dict(self.r)
        with self.eng.Fori(start, count) as i:
            for k, v in per.items():
                if v:
                    self.r[k] = r0[k] + (i - start if start else i) * (v // RING if k == "g" else v)
            yield i
            for k in self.counts:
                assert self.n[k] - n0[k] == per.get(k, 0), (k, self.n[k] - n0[k], per)
        self.r = r0
        self.n = {k: n0[k] + (count - start) * per.get(k, 0) for k in self.n}


def build(nc, A, out):
    with ExitStack() as ctx:
        _build(nc, ctx, A, out)


def _build(nc, ctx, A, out):
    place = [16512]

    def region(nbytes):
        at = place[0]
        place[0] += nbytes
        assert place[0] <= 229344, place[0]
        return at

    def sb(name, shape, dt=F32, at=None):
        size = int(np.prod(shape[1:])) * 4
        size += -size % 32
        return nc.alloc_sbuf_tensor_at(name, shape, dt, offset=region(size) if at is None else at)

    class Sems(dict):
        def __missing__(self, name):
            self[name] = ctx.enter_context(nc.semaphore(name))
            return self[name]

    S = Sems()

    x = sb("x", [P, KT, TOK])
    ah_at = region(KT * TOK * 4)
    al_at = region(KT * TOK * 4)
    ah = sb("ah", [P, KT, TOK], F32R, ah_at)
    al = sb("al", [P, KT, TOK], F32R, al_at)
    h_at = region(4 * 4 * TOK * 4)
    u_at = region(KT * TOK * 4)
    raw_at = region(RING * D * 4)
    raw = [sb(f"raw{r}", [P, D], at=raw_at + 4 * D * r) for r in range(RING)]
    whi_at = region(2 * D * 4)
    whi = [sb(f"whi{r}", [P, D], F32R, whi_at + 4 * D * r) for r in range(2)]
    wlo = [sb(f"wlo{r}", [P, D], F32R) for r in range(2)]
    mats = sb("mats", [P, N_MATS, P])
    cols = sb("cols", [P, 512])
    mod = sb("mod", [P, 96, 2])
    msc = sb("msc", [P, 4, KT, 2])
    qk_gain = sb("qk_gain", [P, 2])
    e_at = region(20480)

    hid_hi = [sb(f"hid_hi{b}", [P, 4, TOK], F32R, h_at + b * 4 * TOK * 4) for b in range(2)]
    hid_lo = [sb(f"hid_lo{b}", [P, 4, TOK], F32R, h_at + (2 + b) * 4 * TOK * 4) for b in range(2)]
    sq = sb("sq", [P, KT, TOK], at=h_at)
    squares = [sb(f"squares{b}", [P, TOK], at=u_at + 18432 + 3072 * b) for b in range(2)]
    square_sum = [sb("square_sum", [P, TOK], at=e_at + 9216),
                  sb("square_sum_last", [P, TOK], at=h_at)]
    cv_sum = sb("cv_sum", [P, TOK], at=h_at + 36864)
    y = sb("y", [P, KT, TOK], at=u_at)
    rstd = sb("rstd", [P, TOK], at=e_at)
    tmp = sb("tmp", [P, TOK], at=e_at + TOK * 4)
    tmp2 = sb("tmp2", [P, TOK], at=e_at + 2 * TOK * 4)
    tmp3 = sb("tmp3", [P, TOK], at=e_at + 3 * TOK * 4)
    xin = sb("xin", [P, NB_C + NB_L, D], at=u_at)
    vec_rows = sb("vec_rows", [P, 4, P], at=h_at)
    silu_c = sb("silu_c", [P, KT, P], at=h_at + 28672)
    mod_row = [sb(f"mod_row{b}", [P, 512], at=h_at + 32768 + 2048 * b) for b in range(2)]
    cv = sb("cv", [P, KT, TOK], at=u_at)
    sig = sb("sig", [P, TOK], at=h_at)
    upb = sb("upb", [P, PAD + CTX + PAD + LAT + PAD], at=h_at + 3072)
    csum = [sb(f"csum{b}", [P, CTX + PAD + LAT], at=h_at + 6400 + 3200 * b) for b in range(2)]
    taps = sb("taps", [P, 32], at=h_at + 12800)
    prod = [sb(f"prod{b}", [P, CTX + PAD + LAT], at=h_at + 13056 + 3200 * b) for b in range(3)]
    tap_sum = sb("tap_sum", [P, CTX + PAD + LAT], at=h_at + 22656)
    mu = sb("mu", [P, TOK], at=e_at + 4 * TOK * 4)
    zero_rows = sb("zero_rows", [P, D], at=u_at)
    qf = sb("qf", [P, KT, LAT], at=u_at)
    kf = sb("kf", [P, 2, TOK], at=u_at + KT * LAT * 4)
    vt = sb("vt", [P, 6, 256], at=h_at)
    kdup = sb("kdup", [P, 4, TOK], at=h_at + 6144)
    kst = [sb("kst0", [P, TOK], at=h_at + 18432), sb("kst1", [P, TOK], at=e_at + 3072)]
    vst = sb("vst", [P, 6, 2, HD], at=e_at)
    qst = sb("qst", [P, 2, LAT], at=h_at + 23040)
    pr = [sb(f"pr{b}", [P, TOK], at=h_at + 27136 + b * 3072) for b in range(2)]
    prt = sb("prt", [P, 6, LAT], at=h_at + 33280)
    stat = sb("stat", [P, 8], at=e_at + 5 * TOK * 4)
    qk_square = [sb(f"qk_square{b}", [P, LAT], at=e_at + 2048 * b) for b in range(4)]
    qk_cos = [sb(f"qk_cos{b}", [P, LAT], at=e_at + 4096 + 2048 * b) for b in range(2)]
    qk_scaled = [sb(f"qk_scaled{b}", [P, LAT], at=e_at + 8192 + 2048 * b) for b in range(2)]
    head_spread = sb("head_spread", [P, QK_UNITS, P], at=h_at + 33280)
    head_pick = sb("head_pick", [P, 2 * P], at=h_at + 39424)
    rope = sb("rope", [P, 2, LAT], at=e_at + 16384)
    gu = sb("gu", [P, 4, LAT], at=u_at)
    gv = sb("gv", [P, NB_L, 4 * P], at=u_at + 8192)
    q2 = sb("q2", [P, 4, LAT], at=u_at + 16384)
    sg = sb("sg", [P, 16, LAT], at=h_at)
    kd2 = sb("kd2", [P, 4, P + LAT], at=h_at + 32768)
    v2 = sb("v2", [P, 5, 2, 2, HD], at=h_at + 43008)
    k2f = sb("k2f", [P, LAT], at=e_at)
    bias2 = x[:, :, 0:CTX]
    sc2 = [sb(f"sc2_{b}", [P, 4, 2 * P], at=e_at + 4096 * b) for b in range(2)]
    pt2 = sb("pt2", [P, 4, 2, P], at=e_at + 8192)
    wst = sb("wst", [P, 8, P], at=e_at + 12288)
    bsp = sb("bsp", [P, 4, P], at=e_at + 16384)
    gvn = sb("gvn", [P, LAT], at=e_at + 6144)
    st2 = sb("st2", [P, 2, 32], at=e_at + 18432)
    sinks = sb("sinks", [P, 8], at=e_at + 18688)
    gst = sb("gst", [P, 16], at=e_at + 18720)
    bias_rev = sb("bias_rev", [P, 8, 2 * P], at=u_at)
    ws_in = sb("ws_in", [P, 8, P], at=u_at + 8192)
    rel = sb("rel", [BUCKETS + 1, 8], at=u_at + 12288)
    one_hot = sb("one_hot", [BUCKETS + 1, 3 * P], at=u_at + 12320)
    rel_line = sb("rel_line", [8, 3 * P], at=u_at + 13856)
    bs_rows = sb("bs_rows", [8, P], at=u_at + 15392)
    group = sb("group", [8, 4 * P], at=u_at + 15904)
    mh = sb("mh", [P, KT, LAT], F32R, u_at)
    ml = sb("ml", [P, KT, LAT], F32R, e_at)
    wg = sb("wg", [P, KT, E_FF], at=ah_at)
    wu = sb("wu", [P, KT, E_FF], at=ah_at + 16384)
    wd = sb("wd", [P, 4, D], at=ah_at + 32768)
    ht = sb("ht", [P, NB_L, D], at=raw_at)
    fgain = sb("fgain", [P, D], at=whi_at)
    hn = sb("hn", [P, NB_L, D], at=h_at)
    xg = sb("xg", [P, D], at=h_at + 16384)
    xgt = sb("xgt", [P, KT, P], at=h_at + 20480)
    gate_s = sb("gate_s", [P, E_FF], at=h_at + 24576)
    hidt = sb("hidt", [P, E_FF], at=h_at + 26624)
    hidT = sb("hidT", [P, 4, P], at=h_at + 28672)
    yo = sb("yo", [P, D], at=h_at + 30720)
    rw = sb("rw", [P, KT, 20], at=h_at + 34816)
    rb = sb("rb", [P, 20], at=h_at + 35456)
    ramp = sb("ramp", [P, 64], at=h_at + 35552)
    ids = sb("ids", [P, 4], I32, h_at + 35808)
    lg = sb("lg", [P, 4, 20], at=h_at + 35840)
    rt = sb("rt", [P, 24, 64], at=h_at + 36160)
    pos_i = sb("pos_i", [P, 8], U32, h_at + 42304)
    idx_all = sb("idx_all", [P, LIST], I32, h_at + 42336)
    idx1 = sb("idx1", [P, 1], U32, h_at + 42464)
    meta = sb("meta", [P, 32], I32, h_at + 42496)
    zero_i = sb("zero_i", [P, LIST], I32, h_at + 42624)
    wk = sb("wk", [P, 2, NB_L], at=h_at + 42752)
    fin_s = sb("fin_s", [P, 8], at=h_at + 42784)
    ga = [sb(f"ga{n}", [P, D], at=ah_at + 4096 * n) for n in range(8)]
    osum = [sb(f"osum{n}", [P, D], at=ah_at + 4096 * (8 + n)) for n in range(4)]

    def pb(name):
        return ctx.enter_context(nc.psum_tensor(name, [P, 1024], F32))

    acc = [pb("acc0"), pb("acc1")]
    pa, pbk = pb("pa"), pb("pb")

    rel_t = nc.dram_tensor("rel_line_dram", [8, 3 * P], F32, kind="Internal")
    hn_d = nc.dram_tensor("normed_rows_dram", [LAT, D], F32, kind="Internal").ap()
    list_d = nc.dram_tensor("slot_list_dram", [LIST * P, 1], I32, kind="Internal").ap()
    yo_d = nc.dram_tensor("expert_rows_dram", [LIST * P, D], F32, kind="Internal").ap()


    FULL = [(0, CTX, 1), (CTX, TOK, 0)]
    LATENT = [(CTX, TOK, 0)]

    def token_cols(bank, c0=0):
        return bank[:, CTX + c0:CTX + TOK]

    def slots(e, n, one, units=1, steps=0):
        def slot(i):
            one(i)
            e.n["g"] += 1
            e.n["q"] += 1

        turns = n // RING
        if turns > 1 and n % RING == 0:
            with e.loop(turns, g=RING, q=RING, u=RING * units, c=RING * steps) as i:
                for j in range(RING):
                    slot(i * RING + j)
        else:
            turns = 0
        for j in range(turns * RING, n):
            slot(j)

    def split_only(e, n, one):
        def four(count):
            for _ in range(count):
                one()
                e.n["g"] += 1
                e.n["q"] += 1

        with e.loop(n // RING, g=RING, q=RING) as i:
            four(RING)
        four(n % RING)

    qk_list = [(qf[:, n, :], 0, LAT) for n in range(KT)]
    for n in range(2):
        qk_list += [(kf[:, n, CTX:TOK], 0, LAT), (kf[:, n, 0:CTX], LAT, CTX)]

    def of_product(n):
        return [n] if 0 <= n < KT else {KT: [8, 9], KT + 1: [10, 11]}.get(n, [])

    def feed_forward(e, up, down, up_steps=0, beside=None):
        def at(place):
            if beside and place in beside:
                beside[place]()

        def four(one, chunk, b):
            for j in range(4):
                one(chunk, j, b)
                e.n["g"] += 1
                e.n["q"] += 1

        four(up, 0, 0)
        at("after the first chunk")
        with e.loop(3, g=16, q=16, u=24, c=8 * up_steps) as i:
            four(up, i * 2 + 1, 1)
            four(down, i * 2, 0)
            four(up, i * 2 + 2, 0)
            four(down, i * 2 + 1, 1)
        at("before the last up")
        four(up, 7, 1)
        at("after the last up")
        four(down, 6, 0)
        at("before the last down")
        four(down, 7, 1)

    wide = CTX + PAD + LAT

    def load_slot(e, src, k):
        r = e.n["g"] % RING
        e.eng.wait_ge(S["lo_ready"], e.at("q", 1 - RING))
        e.eng.dma_start(raw[r][:, :].rearrange("p (k n) -> p k n", k=k),
                        src.rearrange("(k p) n -> p k n", p=P)).then_inc(S[f"raw_in{r}"], 16)

    def split_high(e):
        r = e.n["g"] % RING
        e.eng.wait_ge(S[f"raw_in{r}"], 16 * e.laps() if isinstance(e.laps(), int) else e.laps() * 16)
        e.eng.wait_ge(S["split_started"], e.at("q", 1))
        e.eng.activation(whi[e.n["q"] % 2][:, :], raw[r][:, :], ACT.Copy).then_inc(S["hi_ready"], 1)

    def split_first(e, split):
        split(e)
        e.n["g"] += 1
        e.n["q"] += 1

    def split_low(e):
        b = e.n["q"] % 2
        e.eng.wait_ge(S["hi_ready"], e.at("q", 1))
        e.eng.tensor_tensor(wlo[b][:, :], raw[e.n["g"] % RING][:, :], whi[b][:, :].bitcast(F32),
                            ALU.subtract).then_inc(S["lo_ready"], 1)

    def run_group(e, group, first=None, last=None, operand=None, per_tile=1):
        keys = [g[0] for g in group]
        ins = None
        for n, (key, o, w, m) in enumerate(group):
            if operand is not None and n % per_tile == 0:
                t = n // per_tile
                if t < AL_POOL:
                    e.eng.wait_ge(S["al_ready"], AL_POOL * operand + t + 1)
                else:
                    e.eng.wait_ge(S["al_rest"], (KT - AL_POOL) * operand + t - AL_POOL + 1)
            ins = e.eng.matmul(o, w, m, start=keys.index(key) == n,
                               stop=len(keys) - 1 - keys[::-1].index(key) == n)
            if n == 0 and first:
                ins.then_inc(S[first], 1)
        if last:
            ins.then_inc(S[last], 1)

    def product(e, act_hi, act_lo, segs, k=KT, shift=0, out0=CTX, first="split_started",
                operand=None):
        h, l = whi[e.n["q"] % 2], wlo[e.n["q"] % 2]
        e.eng.wait_ge(S["lo_ready"], e.at("q", 1))
        wide = D // k
        for j in range(KT // k):
            bank = acc[e.n["u"] % 2]
            group = []
            for t in range(k):
                c = t * wide + j * P
                for w, a in ((h, act_hi), (h, act_lo), (l, act_hi)):
                    for s0, s1, _ in segs:
                        group.append((s0, bank[:, out0 + s0:out0 + s1], w[:, c:c + P], a[:, t + shift, s0:s1]))
            e.eng.wait_ge(S["acc_free"], e.at("u", 1))
            run_group(e, group, first if j == 0 else None, "acc_ready", operand, 3 * len(segs))
            e.n["u"] += 1

    def product_rows(e, blocks):
        h, l = whi[e.n["q"] % 2], wlo[e.n["q"] % 2]
        e.eng.wait_ge(S["lo_ready"], e.at("q", 1))
        e.eng.wait_ge(S["acc_free"], e.at("u", 1))
        bank = acc[e.n["u"] % 2]
        group = [(b, bank[:, CTX + b * P:CTX + b * P + P], a[:, t, b * P:b * P + P], w[:, t * P:t * P + P])
                 for b in blocks for t in range(KT) for a, w in ((ah, h), (ah, l), (al, h))]
        run_group(e, group, "split_started", "acc_ready")
        e.n["u"] += 1

    def sum_over_channels(e, src, segs, ready, done0):
        for t in range(KT):
            for sem in ready:
                e.eng.wait_ge(S[sem], done0 + t + 1)
            for s0, s1, _ in segs:
                ins = e.eng.matmul(pa[:, CTX + s0:CTX + s1], mats[:, M_MEAN, :], src[:, t, s0:s1],
                                   start=t == 0, stop=t == KT - 1)
        ins.then_inc(S["stat_ready"], 1)

    def take_unit(e):
        e.eng.wait_ge(S["acc_ready"], e.at("u", 1))
        return acc[e.n["u"] % 2]

    def free_unit(e, ins, then_read=False):
        ins.then_inc(S["acc_free"], 1)
        e.n["u"] += 1
        if then_read:
            e.eng.wait_ge(S["acc_free"], e.at("u", 2))

    def column(i):
        return bass.ds(i, 1)

    def tile_of(ap, i, *rest):
        return ap[(slice(None), bass.ds(i, 1)) + rest].rearrange("p a t -> p (a t)")

    def norm_act(e, n, k, segs, k_root, split=True, early=None):
        c0 = segs[0][0]
        total = square_sum[n == NORMS - 1]
        for i in range(KT):
            e.eng.wait_ge(S["acc_free"], e.at("u", 2 if n == 0 else 3 - KT + i))
            if i >= 3:
                e.eng.wait_ge(S["sq_added"], (KT - 1) * n + i - 2)
            e.eng.activation((squares[(i - 1) % 2] if i else total)[:, c0:TOK], x[:, i, c0:TOK],
                             ACT.Square).then_inc(S["sq_ready"], 1)
        if early:
            early()
        root(e, k_root, rstd[:, c0:TOK])
        if split:
            for i in range(KT):
                e.eng.wait_ge(S["y_ready"], KT * max(k - 1, 0) + i + 1)
                e.eng.activation(ah[:, i, c0:TOK], y[:, i, c0:TOK], ACT.Copy).then_inc(S["ah_ready"], 1)
                if k and i == KT - 3:
                    early()

    def add_squares(e, n, segs):
        c0 = segs[0][0]
        total = square_sum[n == NORMS - 1][:, c0:TOK]
        for i in range(1, KT):
            e.eng.wait_ge(S["sq_ready"], KT * n + i + 1)
            if i >= 2:
                e.eng.wait_ge(S["sq_added"], (KT - 1) * n + i - 1)
            e.eng.tensor_tensor(total, total, squares[(i - 1) % 2][:, c0:TOK], ALU.add).then_inc(S["sq_added"], 1)

    def spread_mean(e, n, segs):
        e.eng.wait_ge(S["sq_added"], (KT - 1) * (n + 1))
        for s0, s1, _ in segs:
            ins = e.eng.matmul(pa[:, CTX + s0:CTX + s1], mats[:, M_MEAN, :], square_sum[n == NORMS - 1][:, s0:s1],
                               start=True, stop=True)
        ins.then_inc(S["stat_ready"], 1)

    def operand_done(e, k):
        e.eng.wait_ge(S["al_ready"], AL_POOL * k)
        e.eng.wait_ge(S["al_rest"], (KT - AL_POOL) * k)

    def low_rest(e, k, segs):
        c0 = segs[0][0]
        for i in range(AL_POOL, KT):
            e.eng.wait_ge(S["ah_ready"], KT * k + i + 1)
            e.eng.tensor_tensor(al[:, i, c0:TOK], y[:, i, c0:TOK], ah[:, i, c0:TOK].bitcast(F32),
                                ALU.subtract).then_inc(S["al_rest"], 1)

    def low_pool(e, k, segs):
        c0 = segs[0][0]
        with e.loop(AL_POOL) as i:
            e.eng.wait_ge(S["ah_ready"], i + (KT * k + 1))
            e.eng.tensor_tensor(tile_of(al, i, slice(c0, TOK)), tile_of(y, i, slice(c0, TOK)),
                                tile_of(ah, i, slice(c0, TOK)).bitcast(F32),
                                ALU.subtract).then_inc(S["al_ready"], 1)

    def reciprocal_for_root(e, ap):
        e.eng.reciprocal(ap, ap).then_inc(S["root_in"], 1)

    def root(e, k, ap):
        e.eng.wait_ge(S["root_in"], k)
        e.eng.activation(ap, ap, ACT.Sqrt).then_inc(S["root_out"], 1)

    def inverse_root(e, stats, segs, k_root):
        c0 = segs[0][0]
        e.eng.wait_ge(S["stat_ready"], stats)
        e.step(e.eng.tensor_scalar(rstd[:, c0:TOK], token_cols(pa, c0), EPS, None, ALU.add))
        reciprocal_for_root(e, rstd[:, c0:TOK])
        e.eng.wait_ge(S["root_out"], k_root)

    def norm_dve(e, stats, segs, k_root, y0, operand=None, scale=None, shift=None, gain=None):
        c0 = segs[0][0]
        inverse_root(e, stats, segs, k_root)
        if gain is not None:
            with e.loop(KT) as i:
                e.eng.scalar_tensor_tensor(
                    out=tile_of(y, i, slice(c0, TOK)), in0=tile_of(x, i, slice(c0, TOK)),
                    scalar=cols[:, column(i + gain)], in1=rstd[:, c0:TOK],
                    op0=ALU.mult, op1=ALU.mult).then_inc(S["y_ready"], 1)
            if operand is not None:
                low_rest(e, operand, segs)
            return
        scaled = (tmp, tmp2)

        def by_root(i):
            if i >= 2:
                e.eng.wait_ge(S["y_ready"], y0 + i - 1)
            e.eng.tensor_tensor(scaled[i % 2][:, c0:TOK], x[:, i, c0:TOK], rstd[:, c0:TOK], ALU.mult
                                ).then_inc(e.chain, 1)
            e.n["c"] += 1

        by_root(0)
        for i in range(KT):
            if i + 1 < KT:
                by_root(i + 1)
            e.eng.wait_ge(e.chain, e.at("c", -1 if i + 1 < KT else 0))
            for s0, s1, v in segs:
                ins = e.eng.tensor_scalar(
                    y[:, i, s0:s1], scaled[i % 2][:, s0:s1], msc[:, scale, i:i + 1, v],
                    mod[:, i + shift:i + shift + 1, v], ALU.mult, ALU.add)
            ins.then_inc(S["y_ready"], 1)
        low_rest(e, operand, segs)

    U_TOTAL = 6 + 16 + 8 + 96 + 12 + 8 + 96 + 30 + 16 + 8
    ctx.enter_context(nc.allow_non_contiguous_dma(reason="short rows of constants"))
    block = ctx.enter_context(nc.Block())

    @block.sync
    def _(sp):
        e = Program(sp, counts="gq")
        sp.dma_start(xin[:, 0:NB_C, :], A["ctx"][0].rearrange("(b p) d -> p b d", p=P)).then_inc(S["x_in"], 16)
        sp.dma_start(xin[:, NB_C:, :], A["x"][0].rearrange("(b p) d -> p b d", p=P)).then_inc(S["x_in"], 16)

        def load_direct(layer, chunk, k):
            r = e.n["g"] % RING
            sp.dma_start(raw[r][:, :].rearrange("p (k n) -> p k n", k=2),
                         A["w_mod"][layer, 256 * k:256 * k + 256, bass.ds(chunk * 512, 512)].rearrange(
                             "(k p) n -> p k n", p=P)).then_inc(S[f"raw_in{r}"], 16)
            e.n["g"] += 1

        for k in range(RING):
            load_direct(0, 0, k)
        with e.loop(4, start=1, g=RING) as i:
            for k in range(RING):
                sp.wait_ge(S["direct_done"], i * 4 + (k - 3))
                load_direct(0, i, k)
        pw1 = A["conv_w_pw1"][0]
        order = (["P"] + ["D"] * 4) * 4
        per = len(order)
        with e.loop(KT // 2, g=per, q=4) as i:
            for n, kind in enumerate(order):
                before = order[n - RING]
                at = order[:(n - RING) % per].count(before) - (0 if n >= RING else order.count(before))
                if before == "D":
                    sp.wait_ge(S["direct_done"], i * 16 + (16 + at + 1))
                else:
                    sp.wait_ge(S["lo_ready"], i * 4 + (at + 1))
                here = order[:n].count(kind)
                if kind == "D":
                    if here < 8:
                        load_direct(0, i * 2 + (4 + here // 4), here % 4)
                    else:
                        load_direct(1, i * 2 + (here - 8) // 4, here % 4)
                else:
                    r = e.n["g"] % RING
                    sp.dma_start(raw[r][:, :].rearrange("p (k n) -> p k n", k=KT),
                                 pw1[:, bass.ds(i * 256 + (here // 2 * P + here % 2 * D), P)].rearrange(
                                     "(k p) n -> p k n", p=P)).then_inc(S[f"raw_in{r}"], 16)
                    e.n["g"] += 1
                    e.n["q"] += 1
        for n in range(16):
            sp.wait_ge(S["direct_done"], 80 + n - RING + 1)
            load_direct(1, 8 + n // 4, n % 4)
        sp.wait_ge(S["direct_done"], 96)
        slots(e, KT, lambda i: load_slot(e, A["conv_w_pw2"][0][:, bass.ds(i * P, P)], KT))

        def load_ff(layer, beside=None):
            up = A["w_ff1"][layer]
            down = A["w_ff2"][layer]
            feed_forward(
                e, lambda c, j, b: load_slot(e, up[:, bass.ds(c * 512 + j * P, P)], KT),
                lambda c, j, b: load_slot(e, down[bass.ds(c * 512, 512), j * 256:j * 256 + 256], 4), beside=beside)

        load_ff(0)
        slots(e, 12, lambda i: load_slot(e, A["gqa_w_qkv"][0][:, bass.ds(i * P, P)], KT))
        slots(e, KT, lambda i: load_slot(e, A["gqa_w_o"][0][:, bass.ds(i * P, P)], KT))

        def prepare_loads():
            operand_done(e, 5)
            sp.wait_ge(S["mask_row"], 1)
            for dst, src in ((rel[0:BUCKETS, :], A["rel_bias_2"]), (one_hot[:, :], A["one_hot"]),
                             (ws_in[:, :, :], A["gm_w_spatial_2"][0].rearrange("g t s -> t g s")),
                             (bs_rows[:, :], A["gm_b_spatial_2"][0]), (group[:, :], A["group"])):
                sp.dma_start(dst, src).then_inc(S["prep_in"], 16)

        def prepare_line():
            sp.wait_ge(S["line_ready"], 1)
            sp.dma_start(rel_t.ap(), rel_line[:, :]).then_inc(S["line_out"], 16)
            sp.wait_ge(S["line_out"], 16)
            sp.dma_start(bias_rev[:, :, :], bass.AP(rel_t, 0, [[1, P], [3 * P, 8], [1, 2 * P]])).then_inc(S["rev_in"], 16)

        load_ff(1, {"after the first chunk": prepare_loads, "after the last up": prepare_line})
        sp.dma_start(gvn[:, :], A["gm_v_norm_g_2"].to_broadcast([P, LAT])).then_inc(S["gains_in"], 16)
        sp.dma_start(sinks[:, :], A["attn_sinks_2"].to_broadcast([P, 8])).then_inc(S["gains_in"], 16)
        slots(e, 30, lambda i: load_slot(e, A["w_in_2"][0][:, bass.ds(i * P, P)], KT))

        with e.loop(2, g=4, q=4) as i:
            for s in range(2):
                for w in ("w_proj_a_2", "w_proj_b_2"):
                    load_slot(e, A[w][0][:, bass.ds(i * 512 + s * 256, 256)], 4)
                    e.n["g"] += 1
                    e.n["q"] += 1
        slots(e, KT, lambda i: load_slot(e, A["w_out_2"][0][:, bass.ds(i * P, P)], KT))
        sp.wait_ge(S["acc_ready"], U_TOTAL)
        sp.dma_start(rw[:, :, 0:4], A["router_group_w_2"][0].rearrange("(k p) n -> p k n", p=P)).then_inc(S["route_in"], 16)
        for g in range(4):
            sp.dma_start(rw[:, :, 4 + 4 * g:8 + 4 * g],
                         A["router_expert_w_2"][0, g].rearrange("(k p) n -> p k n", p=P)).then_inc(S["route_in"], 16)
        sp.dma_start(rb[:, 0:4], A["router_group_b_2"].to_broadcast([P, 4])).then_inc(S["route_in"], 16)
        sp.dma_start(rb[:, 4:20], A["router_expert_b_2"].rearrange("l g e -> l (g e)").to_broadcast([P, 16])
                     ).then_inc(S["route_in"], 16)
        sp.dma_start(ramp[:, :], A["ramp"]).then_inc(S["route_in"], 16)
        sp.dma_start(ids[:, :], A["ids"]).then_inc(S["route_in"], 16)
        sp.dma_start(fgain[:, :], A["final_norm_g_2"].rearrange("(a d) -> a d", a=1).to_broadcast([P, D])
                     ).then_inc(S["route_in"], 16)
        sp.wait_ge(S["hn_ready"], NB_L)
        sp.dma_start(hn_d.rearrange("(b p) d -> p b d", p=P), hn[:, :, :]).then_inc(S["hn_out"], 16)
        sp.wait_ge(S["meta_ready"], 1)
        n_blocks = sp.value_load(meta[0:1, LIST:LIST + 1], min_val=2 * LAT // P, max_val=SLOTS_MAX)
        with sp.Fori(0, n_blocks) as i:
            ex = sp.value_load(meta[0:1, bass.ds(i, 1)], min_val=0, max_val=N_EXP - 1)
            sp.wait_ge(S["gate_done"], i + 1)
            sp.dma_start(wg[:, :, :], A["expert_w_gate_2"][0, bass.ds(ex, 1)].rearrange(
                "e (p k) n -> p (e k) n", k=KT)).then_inc(S["wg_in"], 16)
            sp.wait_ge(S["xg_in"], i * 16 + 16)
            sp.wait_ge(S["up_done"], i + 1)
            sp.dma_start(wu[:, :, :], A["expert_w_up_2"][0, bass.ds(ex, 1)].rearrange(
                "e (p k) n -> p (e k) n", k=KT)).then_inc(S["wu_in"], 16)
            sp.wait_ge(S["down_done"], i + 1)
            sp.dma_start(wd[:, :, :], A["expert_w_down_2"][0, bass.ds(ex, 1)].rearrange(
                "e (p k) n -> p (e k) n", k=4)).then_inc(S["wd_in"], 16)
        for b in range(NB_L):
            sp.wait_ge(S["final_ready"], b + 1)
            sp.dma_start(out[0, b * P:b * P + P, :], osum[b][:, :]).then_inc(S["stored"], 16)
        sp.wait_ge(S["stored"], 16 * NB_L)

    @block.scalar
    def _(act):
        e = Program(act, S["act_chain"])
        vectors = [("norm1_g", 2), ("norm2_g", 2), ("conv_b_dw", 1), ("conv_ln_g", 1), ("conv_ln_b", 1),
                   ("c", 1), ("c_ctx", 1), ("attn_norm_g_2", 1), ("ffn_norm_g_2", 1)]
        act.dma_start(mats[:, :, :], A["mats"].rearrange("n p q -> p n q")).then_inc(S["mats_in"], 16)
        act.dma_start(vec_rows[0:96, 0, :], A["b_mod"].rearrange("l (m p) -> (l m) p", p=P)).then_inc(S["consts_in"], 16)
        row = 0
        for name, count in vectors:
            src = A[name].rearrange("(c p) -> c p", p=P) if name == "c_ctx" else \
                A[name].rearrange("l (c p) -> (l c) p", p=P)
            act.dma_start(vec_rows[row:row + 8 * count, 1, :], src).then_inc(S["consts_in"], 16)
            row += 8 * count
        dw = A["conv_w_dw"][0].rearrange("t (c p) -> (t c) p", p=P)
        act.dma_start(vec_rows[0:120, 2, :], dw[0:120, :]).then_inc(S["consts_in"], 16)
        act.dma_start(vec_rows[0:128, 3, :], dw[120:248, :]).then_inc(S["consts_in"], 16)
        act.dma_start(rope[:, :, :], A["rope"].rearrange("n p t -> p n t")).then_inc(S["consts_in"], 16)
        for n, name in enumerate(("gqa_q_norm", "gqa_k_norm")):
            for h in range(2):
                act.dma_start(qk_gain[HD * h:HD * h + HD, n:n + 1],
                              A[name].rearrange("l (d o) -> (l d) o", o=1)).then_inc(S["consts_in"], 16)
        act.wait_ge(S["cols_ready"], 1)
        act.wait_ge(S["pad_zeroed"], 1)
        act.sem_inc(S["mod_copied"], 2)
        for v, c in enumerate((V_C, V_CC)):
            act.activation(silu_c[:, :, v], cols[:, C_VEC + 8 * c:C_VEC + 8 * c + 8], ACT.Silu
                           ).then_inc(S["silu_ready"], 1)

        def copy_row(n, b):
            act.wait_ge(S["direct_done"], n * 4 + 4)
            act.activation(mod_row[b][0:2, :], pa[0:2, 512 * b:512 * b + 512], ACT.Copy).then_inc(S["mod_copied"], 1)

        def first_rows():
            with e.loop(2) as i:
                for b in range(2):
                    copy_row(i * 2 + b, b)
            split_high(e)
            e.n["g"] += 5
            e.n["q"] += 1

        e.n["g"] += 16
        e.n["u"] += NB_C + NB_L
        norm_act(e, 0, 0, FULL, 1, early=first_rows)
        def projection_split():
            split_high(e)
            e.n["g"] += 5
            e.n["q"] += 1

        def tap_products(i, first, last):
            for j in range(first, last):
                t = TAPS - ACT_TAPS + j
                if j:
                    act.wait_ge(S["conv_added"], i * (ACT_TAPS - 1) + j)
                act.activation((prod[(j - 1) % 3] if j else tap_sum)[:, :], upb[:, t:t + wide], ACT.Copy,
                               scale=taps[:, t:t + 1]).then_inc(S["tap_product"], 1)

        def before_sigmoid(chunk0, i=None):
            if i is not None:
                projection_split()
            projection_split()
            if i is not None:
                act.wait_ge(S["acc_free"], e.at("u", 1))
                tap_products(i, 0, 4)
            copy_row(chunk0, 0)
            if i is not None:
                tap_products(i, 4, ACT_TAPS)
            copy_row(chunk0 + 1, 1)
            e.n["u"] += 1
            act.wait_ge(S["acc_ready"], e.at("u", 1))
            act.activation(sig[:, :], token_cols(acc[e.n["u"] % 2]), ACT.Sigmoid).then_inc(S["sig_ready"], 1)
            e.n["u"] += 1

        before_sigmoid(4)
        with e.loop(KT // 2 - 1, g=20, q=4, u=4) as i:
            before_sigmoid(i * 4 + 6, i * 2)
            before_sigmoid(i * 4 + 8, i * 2 + 1)
        before_sigmoid(18, KT - 2)
        act.wait_ge(S["acc_free"], e.at("u", 1))
        tap_products(KT - 1, 0, 5)
        copy_row(20, 0)
        tap_products(KT - 1, 5, ACT_TAPS)
        for n in (21, 22, 23):
            copy_row(n, n % 2)
        e.n["g"] += 16

        def high(*_):
            split_high(e)

        def early():
            split_first(e, split_high)

        with e.loop(KT) as i:
            act.wait_ge(S["centred"], i + 1)
            act.activation(tile_of(sq, i, slice(0, TOK)), tile_of(cv, i, slice(0, TOK)), ACT.Square
                           ).then_inc(S["ln_sq_ready"], 1)
        early()
        root(e, 2, rstd[:, :])
        for i in range(KT):
            act.wait_ge(S["ln_ready"], i + 1)
            lb, lgain = C_VEC + 8 * V_LB + i, C_VEC + 8 * V_LG + i
            e.step(act.activation(y[:, i, :], cv[:, i, :], ACT.Silu, bias=cols[:, lb:lb + 1],
                                  scale=cols[:, lgain:lgain + 1]))
            act.activation(ah[:, i, :], y[:, i, :], ACT.Copy).then_inc(S["ah_ready"], 1)
            if i == KT - 3:
                early()

        slots(e, KT - 2, high, units=0)
        e.n["u"] += KT
        norm_act(e, 1, 2, FULL, 3, early=early)

        def high_ff():
            u0 = e.n["u"]
            split_only(e, 62, high)
            e.n["u"] = u0 + 96

        high_ff()
        norm_act(e, 2, 3, FULL, 4, early=early)
        act.dma_start(head_pick[:, :], A["head_pick"]).then_inc(S["heads_in"], 16)
        act.dma_start(head_spread[:, :, :], A["head_spread"]).then_inc(S["heads_in"], 16)
        u0 = e.n["u"]
        for slot in range(1, 14):
            if 2 <= slot < 12:
                high()
                e.n["g"] += 1
                e.n["q"] += 1
            for n in of_product(slot - 2) if slot >= 2 else ():
                src, _, width = qk_list[n]
                act.wait_ge(S["acc_free"], u0 + slot - 2 + 3)
                if n >= 4:
                    act.wait_ge(S["qk_summed"], n - 3)
                act.activation(qk_square[n % 4][:, 0:width], src, ACT.Square).then_inc(S["qk_squared"], 1)
        e.n["u"] += 12
        root(e, 5, rstd[:, :])
        with e.loop(4) as i:
            def exps(m):
                act.wait_ge(S["nmax_ready"], i * 16 + (m + 1))
                if m >= 2:
                    act.wait_ge(S["turned"], i * 16 + (m - 1))
                b = m % 2
                act.activation(pr[b][:, :], acc[b][:, 0:TOK], ACT.Exp, bias=stat[:, 4 * b + 1:4 * b + 2],
                               scale=HD ** -0.5, accum_out=stat[:, 4 * b + 2:4 * b + 3]).then_inc(S["exp_done"], 1)

            exps(0)
            for m in range(16):
                if m + 1 < 16:
                    exps(m + 1)
                act.wait_ge(S["turned"], i * 16 + (m + 1))
                qb = m % 4
                act.activation(prt[:, :, qb * P:qb * P + P],
                               pa[:, 0:TOK].rearrange("p (k q) -> p k q", q=P), ACT.Copy).then_inc(S["prt_ready"], 1)
        slots(e, KT, high, units=0)
        e.n["u"] += KT
        norm_act(e, 3, 4, LATENT, 6, early=early)
        high_ff()
        norm_act(e, 4, 5, LATENT, 7, early=early)
        e.n["u"] += 2
        for _ in range(12):
            high()
            e.n["g"] += 1
            e.n["q"] += 1
            e.n["u"] += 1
        act.wait_ge(S["acc_free"], e.at("u", -6 + 2))
        for j in range(4):
            act.activation(gv[:, j, :], gv[:, j, :], ACT.Gelu_apprx_tanh).then_inc(S["gelu_done"], 1)
        for j in range(4):
            act.activation(gu[:, j, :], gu[:, j, :], ACT.Gelu_apprx_tanh).then_inc(S["gelu_done"], 1)
        u0 = e.n["u"]
        for j in range(16 + 3):
            if j < 16:
                high()
                e.n["g"] += 1
                e.n["q"] += 1
            if j >= 3:
                act.wait_ge(S["acc_free"], u0 + j - 3 + 3)
                act.activation(sg[:, j - 3, :], sg[:, j - 3, :], ACT.Sigmoid).then_inc(S["gates_ready"], 1)
            if j == 14:
                root(e, 8, gst[:, 12:16])
        e.n["u"] += 16
        for h in range(8):
            b = h % 2
            act.wait_ge(S["nm2_ready"], h + 1)
            for blk in range(4):
                act.activation(sc2[b][:, blk, :], sc2[b][:, blk, :], ACT.Exp, bias=st2[:, b, 4 + blk:5 + blk],
                               accum_out=st2[:, b, 8 + blk:9 + blk])
            act.activation(st2[:, b, 12:16], st2[:, b, 4:8], ACT.Exp, bias=sinks[:, h:h + 1]
                           ).then_inc(S["exp2_done"], 1)
            act.wait_ge(S["turned2"], h + 1)
            act.activation(pt2[:, :, :, :].rearrange("p a b q -> p (a b q)"), pa[:, :], ACT.Copy
                           ).then_inc(S["pt2_ready"], 1)
        with e.loop(2, g=4, q=4, u=8) as i:
            for j in range(4):
                high()
                e.n["g"] += 1
                e.n["q"] += 1
                e.n["u"] += 2
        slots(e, KT, high, units=0)
        e.n["u"] += KT
        norm_act(e, 5, 6, LATENT, 9, split=False)
        act.wait_ge(S["route_args"], 1)
        act.activation(rt[:, 1, 0:20], rt[:, 0, 0:20], ACT.Exp).then_inc(S["route_exp"], 1)
        act.sem_inc(S["yo_out"], 16)
        act.wait_ge(S["meta_ready"], 1)
        n_blocks = act.value_load(meta[0:1, LIST:LIST + 1], min_val=2 * LAT // P, max_val=SLOTS_MAX)
        with act.Fori(0, n_blocks) as i:
            act.wait_ge(S["gate_done"], i + 2)
            act.activation(gate_s[:, :], acc[0][:, 0:E_FF], ACT.Silu).then_inc(S["silu_gate"], 1)
            act.wait_ge(S["down_done"], i + 2)
            act.wait_ge(S["yo_out"], i * 16 + 16)
            act.activation(yo[:, 0:512], pbk[:, 0:512], ACT.Copy).then_inc(S["yo_act"], 1)
            act.wait_ge(S["yo_act"], i + 1)
            act.wait_ge(S["yo_dve"], i + 2)
            act.dma_start(yo_d[bass.ds(i * P, P), :], yo[:, :]).then_inc(S["yo_out"], 16)
        for b in range(NB_L):
            act.wait_ge(S["osum_ready"], b + 1)
            act.activation(ga[2 * b][:, :], osum[b][:, :], ACT.Square, accum_out=fin_s[:, b:b + 1]
                           ).then_inc(S["fin_sq"], 1)
            root(e, 10 + b, fin_s[:, 4 + b:5 + b])

    @block.gpsimd
    def _(pool):
        e = Program(pool, S["pool_chain"], "cgq")
        add_squares(e, 0, FULL)
        e.n["g"] += 16
        split_low(e)
        e.n["g"] += 5
        e.n["q"] += 1
        low_pool(e, 0, FULL)
        pool.sem_inc(S["conv_added"], 3)

        def projection_split():
            split_low(e)
            e.n["g"] += 5
            e.n["q"] += 1

        def add_products(i, first, last):
            for j in range(max(first, 1), last):
                pool.wait_ge(S["tap_product"], i * ACT_TAPS + (j + 1))
                pool.wait_ge(S["conv_added"], i * (ACT_TAPS - 1) + (j + 2))
                pool.tensor_tensor(tap_sum[:, :], tap_sum[:, :], prod[(j - 1) % 3][:, :], ALU.add
                                   ).then_inc(S["conv_added"], 1)

        def splits(i=None):
            if i is not None:
                projection_split()
            projection_split()
            if i is not None:
                add_products(i, 0, ACT_TAPS)

        def add_tile(i):
            pool.wait_ge(S["cv_ready"], i + 1)
            if isinstance(i, int) and i == 0:
                pool.tensor_copy(cv_sum[:, :], cv[:, 0, :]).then_inc(S["cv_added"], 1)
                return
            pool.wait_ge(S["cv_added"], i)
            pool.tensor_tensor(cv_sum[:, :], cv_sum[:, :], tile_of(cv, i, slice(0, TOK)), ALU.add
                               ).then_inc(S["cv_added"], 1)

        splits()
        splits(0)
        add_tile(0)
        splits(1)
        with e.loop(KT // 2 - 2, g=20, q=4) as i:
            add_tile(i * 2 + 1)
            splits(i * 2 + 2)
            add_tile(i * 2 + 2)
            splits(i * 2 + 3)
        add_tile(KT - 3)
        splits(KT - 2)
        add_tile(KT - 2)
        add_products(KT - 1, 0, ACT_TAPS)
        add_tile(KT - 1)
        e.n["g"] += 16
        split_first(e, split_low)
        low_pool(e, 1, FULL)

        def low(*_):
            split_low(e)

        slots(e, KT - 1, low, units=0)
        add_squares(e, 1, FULL)
        split_first(e, split_low)
        low_pool(e, 2, FULL)
        pool.wait_ge(S["zero_rows_ready"], 1)
        pool.dma_start(yo_d.rearrange("(j p) d -> p j d", p=P),
                       zero_rows[:, :].unsqueeze(1).to_broadcast([P, LIST, D])).then_inc(S["rows_zeroed"], 16)
        split_only(e, 63, low)
        add_squares(e, 2, FULL)
        split_first(e, split_low)
        low_pool(e, 3, FULL)
        slots(e, 11, low, units=0)
        slots(e, KT, low, units=0)
        add_squares(e, 3, LATENT)
        split_first(e, split_low)
        low_pool(e, 4, LATENT)
        split_only(e, 63, low)
        pool.wait_ge(S["wst_ready"], 1)
        pool.affine_select(out=wst[:, :, :], in_=wst[:, :, :], compare_op=ALU.is_ge, fill=0.0, base=0,
                           pattern=[[0, 8], [1, P]], channel_multiplier=-1).then_inc(S["wst_masked"], 1)
        add_squares(e, 4, LATENT)
        split_first(e, split_low)
        low_pool(e, 5, LATENT)
        split_only(e, 27, low)
        for _ in range(2):
            low()
            e.n["g"] += 1
            e.n["q"] += 1
        slots(e, KT, low, units=0)
        slots(e, KT, low, units=0)
        add_squares(e, 5, LATENT)
        pool.wait_ge(S["acc_free"], U_TOTAL + 2)
        pool.memset(zero_i[:, :], 0).then_inc(S["zeroed"], 1)
        pool.wait_ge(S["zeroed"], 1)
        pool.dma_start(list_d.rearrange("(p j) o -> p (j o)", p=P), zero_i[:, :]).then_inc(S["list_zero"], 16)
        pool.wait_ge(S["list_zero"], 16)
        pool.wait_ge(S["pos_ready"], 1)
        pool.wait_ge(S["route_in"], 160)
        for n in range(2 * NB_L):
            pool.indirect_dma_start(
                out=list_d, out_offset=bass.IndirectOffsetOnAxis(ap=pos_i[:, n:n + 1], axis=0),
                in_=ids[:, n % NB_L:n % NB_L + 1], in_offset=None).then_inc(S["scattered"], 16)
        pool.wait_ge(S["scattered"], 16 * 2 * NB_L)
        pool.dma_start(idx_all[:, :], list_d.rearrange("(j p) o -> p (j o)", p=P)).then_inc(S["idx_in"], 16)
        pool.wait_ge(S["idx_in"], 16)
        pool.wait_ge(S["hn_out"], 16)
        pool.wait_ge(S["meta_ready"], 1)
        n_blocks = pool.value_load(meta[0:1, LIST:LIST + 1], min_val=2 * LAT // P, max_val=SLOTS_MAX)
        with pool.Fori(0, n_blocks + 1) as i:
            pool.tensor_copy(idx1[:, :], idx_all[:, column(i)].bitcast(U32)).then_inc(S["idx_ready"], 1)
            pool.wait_ge(S["idx_ready"], i + 1)
            pool.wait_ge(S["xg_turned"], i + 1)
            pool.sem_inc(S["gathers"], 1)
            pool.indirect_dma_start(
                out=xg[:, :], out_offset=None, in_=hn_d,
                in_offset=bass.IndirectOffsetOnAxis(ap=idx1[:, 0:1], axis=0)).then_inc(S["xg_in"], 16)
            pool.wait_ge(S["xg_in"], i * 16 + 16)
        pool.wait_ge(S["yo_out"], (n_blocks + 1) * 16)
        pool.sem_inc(S["gathers"], 1)
        for n in range(NB_L):
            for k in range(2):
                pool.indirect_dma_start(
                    out=ga[2 * n + k][:, :], out_offset=None, in_=yo_d,
                    in_offset=bass.IndirectOffsetOnAxis(ap=pos_i[:, k * NB_L + n:k * NB_L + n + 1], axis=0)
                ).then_inc(S[f"rows_in{n}"], 16)

    @block.vector
    def _(dve):
        e = Program(dve, S["dve_chain"], "cu")
        TT, TS, STT = dve.tensor_tensor, dve.tensor_scalar, dve.scalar_tensor_tensor
        dve.sem_inc(S["acc_free"], 2)
        dve.sem_inc(S["mod_free"], 2)
        dve.memset(silu_c[:, :, :], 0.0).then_inc(S["pad_zeroed"], 1)
        dve.sem_inc(S["yo_dve"], 1)
        dve.sem_inc(S["heads_taken"], 2)
        dve.sem_inc(S["heads2_taken"], 2)
        for b in range(NB_C + NB_L):
            bank = take_unit(e)
            free_unit(e, dve.tensor_copy(x[:, :, b * P:b * P + P], bank[:, :].rearrange("p (k t) -> p k t", t=P)))
        dve.wait_ge(S["vec_turned"], 1)
        for n, rows in enumerate((96, 88, 120, 128)):
            ins = dve.tensor_copy(cols[:, P * n:P * n + rows], pbk[:, P * n:P * n + rows])
        ins.then_inc(S["cols_ready"], 1)
        dve.wait_ge(S["cols_ready"], 1)

        def modulation(at, ps, n):
            return TT(mod[:, bass.ds(at, n), :], pbk[:, ps:ps + 2 * n].rearrange("p (n v) -> p n v", v=2),
                      cols[:, bass.ds(at, n)].unsqueeze(2).to_broadcast([P, n, 2]), ALU.add)

        def scales(n, layer, chunk, gain):
            return STT(out=msc[:, n, :, :], in0=mod[:, layer * 48 + chunk * 8:layer * 48 + chunk * 8 + 8, :],
                       scalar=1.0, in1=cols[:, C_VEC + 8 * gain:C_VEC + 8 * gain + 8].unsqueeze(2).to_broadcast([P, KT, 2]),
                       op0=ALU.add, op1=ALU.mult)

        with e.loop(2) as i:
            for b in range(2):
                dve.wait_ge(S["mod_turned"], i * 2 + (b + 1))
                modulation(i * 8 + 4 * b, 512 * b, 4).then_inc(S["mod_free"], 1)
        dve.wait_ge(S["mod_free"], 2 + 4)
        e.step(scales(0, 0, 1, V_N1))
        norm_dve(e, 1, FULL, 1, 0, operand=0, scale=0, shift=0)
        e.step(dve.memset(upb[:, :], 0.0))
        tap_a = cols[:, C_TAP_A:C_TAP_A + 8 * TAP_SPLIT].rearrange("p (t c) -> p t c", c=8)
        tap_b = cols[:, C_TAP_B:C_TAP_B + 8 * (TAPS - TAP_SPLIT)].rearrange("p (t c) -> p t c", c=8)
        def conv_tile(i, turned, at, n, base):
            dve.tensor_copy(taps[:, 0:TAP_SPLIT], tap_a[:, :, column(i)].rearrange("p t c -> p (t c)"))
            dve.tensor_copy(taps[:, TAP_SPLIT:TAPS], tap_b[:, :, column(i)].rearrange("p t c -> p (t c)"))
            e.step(dve.tensor_copy(taps[:, TAPS:TAPS + 1], cols[:, column(i + (C_VEC + 8 * V_CB))]))
            bank = take_unit(e)
            dve.wait_ge(S["sig_ready"], i + 1)
            TT(upb[:, PAD:PAD + CTX], bank[:, CTX:2 * CTX], sig[:, 0:CTX], ALU.mult)
            free_unit(e, TT(upb[:, 2 * PAD + CTX:2 * PAD + TOK], bank[:, 2 * CTX:], sig[:, CTX:TOK], ALU.mult),
                      then_read=True)
            free_unit(e, TS(csum[0][:, :], upb[:, 0:wide], taps[:, 0:1], taps[:, TAPS:TAPS + 1], ALU.mult, ALU.add))
            TS(csum[1][:, :], upb[:, 1:1 + wide], taps[:, 1:2], None, ALU.mult).then_inc(S["dve_chain"], 1)
            e.n["c"] += 1
            for t in range(2, TAPS - ACT_TAPS):
                if t == 2:
                    dve.wait_ge(S["acc_free"], e.at("u", 2))
                else:
                    dve.wait_ge(S["dve_chain"], e.at("c", -1))
                part = csum[t % 2][:, :]
                STT(out=part, in0=upb[:, t:t + wide], scalar=taps[:, t:t + 1], in1=part,
                    op0=ALU.mult, op1=ALU.add).then_inc(S["dve_chain"], 1)
                e.n["c"] += 1
            dve.wait_ge(S["dve_chain"], e.at("c"))
            e.step(TT(csum[0][:, :], csum[0][:, :], csum[1][:, :], ALU.add))
            dve.wait_ge(S["conv_added"], i * (ACT_TAPS - 1) + (ACT_TAPS + 2))
            TT(tile_of(cv, i, slice(0, CTX)), csum[0][:, 0:CTX], tap_sum[:, 0:CTX], ALU.add)
            e.step(TT(tile_of(cv, i, slice(CTX, TOK)), csum[0][:, CTX + PAD:], tap_sum[:, CTX + PAD:], ALU.add))
            dve.sem_inc(S["cv_ready"], 1)
            dve.wait_ge(S["mod_turned"], turned)
            modulation(at, base, n).then_inc(S["mod_free"], 1)

        with e.loop(KT // 2, u=4, c=2 * (2 + TAPS - ACT_TAPS)) as i:
            conv_tile(i * 2, i * 4 + 6, i * 8 + 16, 8, 512)
            conv_tile(i * 2 + 1, i * 4 + 8, i * 8 + 48, 8, 0)
        for turned, at, base in ((22, 80, 512), (24, 88, 0)):
            dve.wait_ge(S["mod_turned"], turned)
            modulation(at, base, 8).then_inc(S["mod_free"], 1)
        dve.wait_ge(S["mod_free"], 2 + 4 + KT + 2)
        scales(1, 0, 4, V_N2)
        scales(2, 1, 1, V_N1B)
        e.step(scales(3, 1, 4, V_N2B))
        dve.wait_ge(S["stat_ready"], 2)
        e.step(dve.tensor_copy(mu[:, :], token_cols(pa)))
        with e.loop(KT) as i:
            TT(tile_of(cv, i, slice(0, TOK)), tile_of(cv, i, slice(0, TOK)), mu[:, :], ALU.subtract
               ).then_inc(S["centred"], 1)
        inverse_root(e, 3, FULL, 2)
        with e.loop(KT) as i:
            TT(tile_of(cv, i, slice(0, TOK)), tile_of(cv, i, slice(0, TOK)), rstd[:, :], ALU.mult
               ).then_inc(S["ln_ready"], 1)
        low_rest(e, 1, FULL)

        def to_stream(gate, segs):
            def one(i):
                bank = take_unit(e)
                for s0, s1, v in segs:
                    xs = tile_of(x, i, slice(s0, s1))
                    ins = STT(out=xs, in0=bank[:, CTX + s0:CTX + s1], scalar=mod[:, column(i + gate), v], in1=xs,
                              op0=ALU.mult, op1=ALU.add)
                free_unit(e, ins)
            return one

        def mlp(layer, segs, beside=None):
            c0 = segs[0][0]

            def up(chunk, j, b):
                bank = take_unit(e)
                free_unit(e, TS(tmp[:, c0:TOK], token_cols(bank, c0), 0.0, None, ALU.max), then_read=True)
                e.step(TT(tmp2[:, c0:TOK], tmp[:, c0:TOK], tmp[:, c0:TOK], ALU.mult))
                e.step(dve.tensor_copy(hid_hi[b][:, j, c0:TOK], tmp2[:, c0:TOK]))
                TT(hid_lo[b][:, j, c0:TOK], tmp2[:, c0:TOK], hid_hi[b][:, j, c0:TOK].bitcast(F32), ALU.subtract
                   ).then_inc(S["hid_ready"], 1)

            def down(chunk, j, b):
                for n in (2 * j, 2 * j + 1):
                    bank = take_unit(e)
                    for s0, s1, v in segs:
                        g = layer * 48 + 40 + n
                        ins = STT(out=x[:, n, s0:s1], in0=bank[:, CTX + s0:CTX + s1], scalar=mod[:, g, v:v + 1],
                                  in1=x[:, n, s0:s1], op0=ALU.mult, op1=ALU.add)
                    free_unit(e, ins)

            feed_forward(e, up, down, up_steps=2, beside=beside)

        slots(e, KT, to_stream(16, FULL))
        norm_dve(e, 4, FULL, 3, 8, operand=2, scale=1, shift=24)
        operand_done(e, 3)
        dve.memset(zero_rows[:, :], 0.0).then_inc(S["zero_rows_ready"], 1)
        mlp(0, FULL)
        dve.wait_ge(S["rows_zeroed"], 16)
        norm_dve(e, 5, FULL, 4, 16, operand=3, scale=2, shift=48)

        def to_q(i):
            bank = take_unit(e)
            free_unit(e, dve.tensor_copy(tile_of(qf, i, slice(0, LAT)), bank[:, 512:1024]))

        slots(e, KT, to_q)
        for j in range(2):
            bank = take_unit(e)
            free_unit(e, dve.tensor_copy(kf[:, j, :], token_cols(bank)))
            e.n["g"] += 1
            e.n["q"] += 1
        for j in range(2):
            bank = take_unit(e)
            free_unit(e, dve.tensor_copy(vt[:, :, j * P:j * P + P],
                                         token_cols(bank).rearrange("p (b n) -> p b n", n=P)))
            e.n["g"] += 1
            e.n["q"] += 1
        dve.wait_ge(S["acc_free"], e.at("u", 2))

        dve.wait_ge(S["qk_summed"], QK_UNITS)
        e.step(TS(rstd[:, :], pa[:, 0:TOK], EPS, None, ALU.add))
        reciprocal_for_root(e, rstd[:, :])

        def scale_pair(n):
            src, at, width = qk_list[n]
            gain = qk_gain[:, 0:1] if n < KT else qk_gain[:, 1:2]
            dve.wait_ge(S["qk_spread"], n + 1)
            dst = qk_scaled[n % 2][:, 0:width] if at == 0 else src
            STT(out=dst, in0=src, scalar=gain, in1=acc[n % 2][:, 0:width], op0=ALU.mult, op1=ALU.mult
                ).then_inc(S["qk_normed"], 1)

        turned = [n for n in range(QK_UNITS) if qk_list[n][1] == 0]
        added = {}
        scale_pair(0)
        for n in range(QK_UNITS):
            if n + 1 < QK_UNITS:
                scale_pair(n + 1)
            if n not in turned:
                continue
            src, _, width = qk_list[n]
            t = turned.index(n)
            dve.wait_ge(S["qk_normed"], n + 1)
            if t >= 2:
                dve.wait_ge(S["dve_chain"], added[t - 2])
            TT(qk_cos[t % 2][:, :], qk_scaled[n % 2][:, :], rope[:, 0, :], ALU.mult).then_inc(S["dve_chain"], 1)
            e.n["c"] += 1
            dve.wait_ge(S["qk_rotated"], t + 1)
            TT(src, pbk[:, 512 * (t % 2):512 * (t % 2) + LAT], rope[:, 1, :], ALU.mult).then_inc(S["qk_sined"], 1)
            dve.wait_ge(S["dve_chain"], e.at("c"))
            dve.wait_ge(S["qk_sined"], t + 1)
            TT(src, src, qk_cos[t % 2][:, :], ALU.add).then_inc(S["dve_chain"], 1)
            e.n["c"] += 1
            added[t] = e.n["c"]
        dve.wait_ge(S["qk_normed"], QK_UNITS)
        dve.wait_ge(S["dve_chain"], e.at("c"))
        dve.sem_inc(S["k_ready"], 1)
        for kv in range(4):
            dve.wait_ge(S["k_doubled"], kv + 1)
            dve.tensor_copy(kdup[:, kv, :], token_cols((pa, pbk)[kv % 2])).then_inc(S["kdup_ready"], 1)
        dve.wait_ge(S["kdup_ready"], 4)
        dve.memset(kst[0][HD:P, :], 0.0)
        dve.memset(kst[1][0:HD, :], 0.0)
        with e.loop(4, c=2 * 16 + 4) as i:
            keys = tile_of(kdup, i, slice(0, TOK))
            dve.tensor_copy(kst[0][0:HD, :], keys[0:HD, :])
            dve.tensor_copy(kst[1][HD:P, :], keys[HD:P, :])
            for twice in range(2):
                dve.tensor_copy(vst[:, :, twice, :], vt[:, :, bass.ds(i * HD, HD)])
            dve.tensor_copy(qst[:, 0, :], tile_of(qf, i * 2, slice(0, LAT)))
            dve.tensor_copy(qst[:, 1, :], tile_of(qf, i * 2 + 1, slice(0, LAT))).then_inc(S["staged"], 1)

            def maxima(m):
                s = 4 * (m % 2)
                dve.wait_ge(S["scores_ready"], i * 16 + (m + 1))
                e.step(dve.tensor_reduce(stat[:, s:s + 1], acc[m % 2][:, 0:TOK], AX.X, ALU.max))
                TS(stat[:, s + 1:s + 2], stat[:, s:s + 1], -HD ** -0.5, None, ALU.mult).then_inc(S["nmax_ready"], 1)

            def normalise(m):
                s = 4 * (m % 2)
                dve.wait_ge(S["exp_done"], i * 16 + (m + 1))
                e.step(dve.reciprocal(stat[:, s + 3:s + 4], stat[:, s + 2:s + 3]))
                TS(pr[m % 2][:, :], pr[m % 2][:, :], stat[:, s + 3:s + 4], None, ALU.mult
                   ).then_inc(S["probs_ready"], 1)

            def take_head(n):
                t, h = n // 2, n % 2
                rows = slice(HD * h, HD * h + HD)
                dve.wait_ge(S["heads_done"], i * 4 + (n + 1))
                o = pbk[rows, 512 * h:512 * h + LAT]
                hi, lo = (tile_of(part, i * 2 + t, slice(CTX, TOK))[rows, :] for part in (ah, al))
                e.step(dve.tensor_copy(hi, o))
                TT(lo, o, hi.bitcast(F32), ALU.subtract).then_inc(S["heads_taken"], 1)

            maxima(0)
            maxima(1)
            for m in range(16):
                normalise(m)
                if m + 2 < 16:
                    maxima(m + 2)
                if m % 4 == 0 and m:
                    take_head(m // 4 - 1)
            take_head(3)
        dve.wait_ge(S["heads_taken"], 2 + 16)
        dve.sem_inc(S["attended"], 1)
        slots(e, KT, to_stream(48 + 16, LATENT))
        norm_dve(e, 6, LATENT, 6, 24, operand=4, scale=3, shift=72)
        operand_done(e, 5)
        dve.memset(rel[:, :], NEG).then_inc(S["mask_row"], 1)

        def prepare_tables():
            dve.wait_ge(S["rel_ready"], 1)
            dve.tensor_copy(rel_line[:, :], pbk[0:8, 0:3 * P]).then_inc(S["line_ready"], 1)
            dve.wait_ge(S["ws_turned"], 1)
            dve.tensor_copy(wst[:, :, :], pa[:, :].rearrange("p (g t) -> p g t", g=8)).then_inc(S["wst_ready"], 1)
            dve.wait_ge(S["bs_spread"], 1)
            dve.tensor_copy(bsp[:, :, :], pbk[:, 512:1024].rearrange("p (t q) -> p t q", t=4)).then_inc(S["bsp_ready"], 1)

        def prepare_bias():
            dve.wait_ge(S["rev_turned"], 2)
            for n, bank in enumerate((pa, pbk)):
                dve.tensor_copy(bias2[:, 4 * n:4 * n + 4, :], bank[:, :].rearrange("p (h s) -> p h s", h=4)
                                ).then_inc(S["bias_done"], 1)

        mlp(1, LATENT, {"before the last up": prepare_tables, "before the last down": prepare_bias})

        norm_dve(e, 7, LATENT, 7, 32, operand=5, gain=C_VEC + 8 * V_AN)

        def keep(dst, n=None):
            bank = take_unit(e)
            src = bank[:, 512:1024]
            free_unit(e, dve.tensor_copy(dst, src if n is None else src.rearrange("p (b n) -> p b n", n=n)))
            e.n["g"] += 1
            e.n["q"] += 1

        for j in range(4):
            keep(gu[:, j, :])
        for j in range(4):
            keep(gv[:, :, j * P:j * P + P], P)
        for j in range(4):
            keep(q2[:, j, :])
        keep(k2f[:, :])
        bank = take_unit(e)
        for twice in range(2):
            ins = dve.tensor_copy(v2[:, 1:5, :, twice, :],
                                  bank[:, 512:1024].rearrange("p (b g d) -> p b g d", b=NB_L, g=2))
        free_unit(e, ins)
        e.n["g"] += 1
        e.n["q"] += 1
        def zero_rims():
            dve.memset(v2[:, 0, :, :, :], 0.0)
            dve.memset(kd2[:, :, 0:P], 0.0)

        def place_keys(kv):
            dve.wait_ge(S["k2_doubled"], kv + 1)
            for j in range(2):
                rows, others = slice(HD * j, HD * j + HD), slice(HD - HD * j, P - HD * j)
                dve.memset(kd2[others, 2 * kv + j, P:], 0.0)
                ins = dve.tensor_copy(kd2[rows, 2 * kv + j, P:], (pa, pbk)[kv][rows, 0:LAT])
            ins.then_inc(S["kd2_ready"], 1)

        def v_mean():
            dve.wait_ge(S["gelu_done"], 8)
            dve.wait_ge(S["gains_in"], 32)
            e.step(dve.tensor_reduce(gst[:, 0:4], gv[:, :, :], AX.X, ALU.add))
            e.step(TS(gst[:, 4:8], gst[:, 0:4], 1.0 / 512, None, ALU.mult))

        def v_square(b):
            e.step(TS(gv[:, b, :], gv[:, b, :], gst[:, 4 + b:5 + b], None, ALU.subtract))
            e.step(STT(out=tmp[:, 0:LAT], in0=gv[:, b, :], scalar=1.0, in1=gv[:, b, :], op0=ALU.mult, op1=ALU.mult,
                       accum_out=gst[:, 8 + b:9 + b]))

        def v_root():
            e.step(TS(gst[:, 12:16], gst[:, 8:12], 1.0 / 512, EPS, ALU.mult, ALU.add))
            reciprocal_for_root(e, gst[:, 12:16])

        between = [zero_rims, lambda: place_keys(0), lambda: place_keys(1), None, None, v_mean] + \
            [lambda b=b: v_square(b) for b in range(4)] + [v_root]
        for j in range(16):
            keep(sg[:, j, :])
            if j < len(between) and between[j]:
                between[j]()
        dve.wait_ge(S["root_out"], 8)
        for b in range(4):
            STT(out=gv[:, b, :], in0=gv[:, b, :], scalar=gst[:, 12 + b:13 + b], in1=gvn[:, :], op0=ALU.mult,
                op1=ALU.mult).then_inc(S["gv_ready"], 1)
        dve.wait_ge(S["gv_ready"], 4)
        for t in range(4):
            dve.wait_ge(S["spatial_done"], t + 1)
            s = (pa, pbk)[t // 2][:, (t % 2) * 512:(t % 2) * 512 + 512].rearrange("p (c q) -> p c q", q=P)
            t4 = tmp[:, 0:LAT].rearrange("p (c q) -> p c q", q=P)
            e.step(TT(t4, s, bsp[:, t, :].unsqueeze(1).to_broadcast([P, 4, P]), ALU.add))
            e.step(TT(tmp[:, 0:LAT], tmp[:, 0:LAT], gu[:, t, :], ALU.mult))
            e.step(dve.tensor_copy(ah[:, t, CTX:TOK], tmp[:, 0:LAT]))
            e.step(TT(al[:, t, CTX:TOK], tmp[:, 0:LAT], ah[:, t, CTX:TOK].bitcast(F32), ALU.subtract))

        def logits(h):
            b = h % 2
            dve.wait_ge(S["scores2"], h + 1)
            if h >= 2:
                dve.wait_ge(S["turned2"], h - 1)
            e.step(STT(out=sc2[b][:, :, :], in0=acc[b][:, :].rearrange("p (c s) -> p c s", c=4), scalar=HD ** -0.5,
                       in1=bias2[:, h, :].unsqueeze(1).to_broadcast([P, 4, 2 * P]), op0=ALU.mult, op1=ALU.add))
            e.step(dve.memset(sc2[b][:, 0, 0:P], NEG))
            e.step(dve.tensor_reduce(st2[:, b, 0:4], sc2[b][:, :, :], AX.X, ALU.max))
            TS(st2[:, b, 4:8], st2[:, b, 0:4], sinks[:, h:h + 1], -1.0, ALU.max, ALU.mult
               ).then_inc(S["nm2_ready"], 1)

        def take_head2(h):
            rows = slice(HD * (h % 2), HD * (h % 2) + HD)
            dve.wait_ge(S["heads2"], h + 1)
            o = pbk[rows, (h % 2) * 512:(h % 2) * 512 + 512]
            hi, lo = ah[rows, 4 + h // 2, CTX:TOK], al[rows, 4 + h // 2, CTX:TOK]
            e.step(dve.tensor_copy(hi, o))
            TT(lo, o, hi.bitcast(F32), ALU.subtract).then_inc(S["heads2_taken"], 1)

        logits(0)
        for h in range(8):
            b = h % 2
            if h + 1 < 8:
                logits(h + 1)
            dve.wait_ge(S["exp2_done"], h + 1)
            e.step(TT(st2[:, b, 16:20], st2[:, b, 8:12], st2[:, b, 12:16], ALU.add))
            e.step(dve.reciprocal(st2[:, b, 20:24], st2[:, b, 16:20]))
            TT(sc2[b][:, :, :], sc2[b][:, :, :], st2[:, b, 20:24].unsqueeze(2).to_broadcast([P, 4, 2 * P]), ALU.mult
               ).then_inc(S["probs2"], 1)
            if h >= 1:
                take_head2(h - 1)
        take_head2(7)

        dve.wait_ge(S["gates_ready"], 16)
        with e.loop(2, g=4, q=4, u=8, c=8) as i:
            for s in range(2):
                for branch in range(2):
                    for j in range(2):
                        n = i * 4 + (2 * s + j)
                        bank = take_unit(e)
                        g = tile_of(sg, n + 8 * branch, slice(0, LAT))
                        free_unit(e, TT(g, bank[:, 512:1024], g, ALU.mult), then_read=True)
                    e.n["g"] += 1
                    e.n["q"] += 1
                for j in range(2):
                    n = i * 4 + (2 * s + j)
                    g0, g1 = tile_of(sg, n, slice(0, LAT)), tile_of(sg, n + 8, slice(0, LAT))
                    e.step(TT(g0, g0, g1, ALU.add))
                    e.step(dve.tensor_copy(tile_of(mh, n, slice(0, LAT)), g0))
                    TT(tile_of(ml, n, slice(0, LAT)), g0, tile_of(mh, n, slice(0, LAT)).bitcast(F32), ALU.subtract
                       ).then_inc(S["merged"], 1)

        def plain(i):
            bank = take_unit(e)
            xs = tile_of(x, i, slice(CTX, TOK))
            free_unit(e, TT(xs, bank[:, 512:1024], xs, ALU.add))

        slots(e, KT, plain)
        norm_dve(e, 8, LATENT, 9, 40, gain=C_VEC + 8 * V_FN)

        for b in range(NB_L):
            bank = take_unit(e)
            free_unit(e, dve.tensor_copy(hn[:, b, :], bank[:, :]), then_read=True)
            dve.sem_inc(S["hn_ready"], 1)
        dve.wait_ge(S["logits_done"], 1)
        dve.wait_ge(S["route_in"], 160)

        def line(n, a=4, b=4):
            return rt[:, n, 0:a * b].rearrange("p (a b) -> p a b", a=a)

        def spread(ap, n):
            return ap.unsqueeze(2).to_broadcast([P, ap.shape[1], n])

        from16 = ramp[:, 0:4].unsqueeze(1).to_broadcast([P, 4, 4])

        def first_of_max(dst, src, most, s1, s2):
            e.step(dve.tensor_reduce(most, src, AX.X, ALU.max))
            e.step(TT(s1, src, spread(most, 4), ALU.is_equal))
            e.step(TT(s1, s1, from16, ALU.mult))
            e.step(dve.tensor_reduce(s2, s1, AX.X, ALU.min))
            e.step(TT(dst, from16, spread(s2, 4), ALU.is_equal))

        e.step(TT(lg[:, :, :], pbk[:, 0:80].rearrange("p (b n) -> p b n", b=4),
                  rb[:, :].unsqueeze(1).to_broadcast([P, 4, 20]), ALU.add))
        oh_g, oh_1, oh_2 = line(2), line(3), line(4)
        gm, m1, m2 = rt[:, 5, 0:4], rt[:, 5, 4:8], rt[:, 5, 8:12]
        first_of_max(oh_g, lg[:, :, 0:4], gm, line(6), rt[:, 7, 0:4])
        e.step(TT(line(0), lg[:, :, 0:4], spread(gm, 4), ALU.subtract))
        four = rt[:, 8, 0:64].rearrange("p (b g e) -> p b g e", b=4, g=4)
        e.step(TT(four, lg[:, :, 4:20].rearrange("p b (g e) -> p b g e", g=4),
                  oh_g.unsqueeze(3).to_broadcast([P, 4, 4, 4]), ALU.mult))
        el = line(9)
        e.step(dve.tensor_reduce(el, four.rearrange("p b g e -> p b e g"), AX.X, ALU.add))
        first_of_max(oh_1, el, m1, line(6), rt[:, 7, 0:4])
        el2 = line(10)
        e.step(STT(out=el2, in0=oh_1, scalar=NEG, in1=el, op0=ALU.mult, op1=ALU.add))
        first_of_max(oh_2, el2, m2, line(6), rt[:, 7, 0:4])
        TT(rt[:, 0, 16:20], m2, m1, ALU.subtract).then_inc(S["route_args"], 1)
        pick = [rt[:, 11 + k, 0:64].rearrange("p (b n) -> p b n", b=4) for k in range(3)]
        for k, oh in enumerate((oh_1, oh_2)):
            e.step(TT(pick[k].rearrange("p b (g e) -> p b g e", g=4), oh_g.unsqueeze(3).to_broadcast([P, 4, 4, 4]),
                      oh.unsqueeze(2).to_broadcast([P, 4, 4, 4]), ALU.mult))
        TT(pick[2], pick[0], pick[1], ALU.add).then_inc(S["picks_ready"], 1)
        dve.wait_ge(S["route_exp"], 1)
        e.step(dve.tensor_reduce(rt[:, 7, 4:8], line(1), AX.X, ALU.add))
        e.step(TS(rt[:, 7, 8:12], rt[:, 1, 16:20], 1.0, None, ALU.add))
        e.step(dve.reciprocal(rt[:, 7, 12:16], rt[:, 7, 4:8]))
        e.step(dve.reciprocal(rt[:, 7, 16:20], rt[:, 7, 8:12]))
        e.step(TT(wk[:, 0, :], rt[:, 7, 12:16], rt[:, 7, 16:20], ALU.mult))
        e.step(TT(wk[:, 1, :], wk[:, 0, :], rt[:, 1, 16:20], ALU.mult))
        dve.wait_ge(S["ranks_done"], 1)
        n16 = rt[:, 14, 0:16]
        e.step(dve.tensor_copy(n16, pbk[:, 576:592]))
        e.step(TT(rt[:, 15, 0:64].rearrange("p (n k) -> p n k", k=4), spread(n16, 4),
                  ramp[:, 48:52].unsqueeze(1).to_broadcast([P, 16, 4]), ALU.is_gt))
        nb, even, odd = rt[:, 16, 0:16], rt[:, 16, 16:32], rt[:, 16, 32:48]
        e.step(dve.tensor_reduce(nb, rt[:, 15, 0:64].rearrange("p (n k) -> p n k", k=4), AX.X, ALU.add))
        src, dst = nb, even
        for shift in (1, 2, 4, 8):
            e.step(dve.tensor_copy(dst[:, 0:shift], src[:, 0:shift]))
            e.step(TT(dst[:, shift:16], src[:, shift:16], src[:, 0:16 - shift], ALU.add))
            src, dst = dst, (odd if dst is even else even)
        upto = src
        base = rt[:, 17, 0:16]
        e.step(TT(base, upto, nb, ALU.subtract))
        e.step(TS(base, base, float(P), None, ALU.mult))
        where = rt[:, 18, 0:64].rearrange("p (b n) -> p b n", b=4)
        e.step(TT(where, pbk[:, 512:576].rearrange("p (b n) -> p b n", b=4),
                  base.unsqueeze(1).to_broadcast([P, 4, 16]), ALU.add))
        prod = rt[:, 19, 0:64].rearrange("p (b n) -> p b n", b=4)
        for k in range(2):
            e.step(TT(prod, pick[k], where, ALU.mult))
            e.step(dve.tensor_reduce(rt[:, 20, 4 * k:4 * k + 4], prod, AX.X, ALU.add))
        dve.tensor_copy(pos_i[:, :], rt[:, 20, 0:8]).then_inc(S["pos_ready"], 1)
        table = rt[:, 0:6, :].rearrange("p a b -> p (a b)").rearrange("p (j n) -> p j n", n=16)
        e.step(TT(table, upto.unsqueeze(1).to_broadcast([P, LIST, 16]), spread(ramp[:, 16:16 + LIST], 16), ALU.is_le))
        e.step(dve.tensor_reduce(rt[:, 21, 0:LIST], table, AX.X, ALU.add))
        e.step(TS(rt[:, 21, 0:LIST], rt[:, 21, 0:LIST], float(N_EXP - 1), None, ALU.min))
        e.step(dve.tensor_copy(rt[:, 21, LIST:LIST + 1], upto[:, 15:16]))
        dve.tensor_copy(meta[:, 0:LIST + 1], rt[:, 21, 0:LIST + 1]).then_inc(S["meta_ready"], 1)
        for b in range(NB_L):
            bank = take_unit(e)
            free_unit(e, dve.tensor_copy(ht[:, b, :], bank[:, :]))
        dve.wait_ge(S["meta_ready"], 1)
        n_blocks = dve.value_load(meta[0:1, LIST:LIST + 1], min_val=2 * LAT // P, max_val=SLOTS_MAX)

        def take_rows(v):
            dve.wait_ge(S["xg_turned"], v)
            dve.tensor_copy(xgt[:, :, :], pa[:, :].rearrange("p (k q) -> p k q", q=P)).then_inc(S["xgt_ready"], 1)

        take_rows(2)
        with dve.Fori(0, n_blocks) as i:
            dve.wait_ge(S["silu_gate"], i + 1)
            dve.wait_ge(S["up_done"], i + 2)
            TT(hidt[:, :], gate_s[:, :], acc[0][:, 512:1024], ALU.mult).then_inc(S["hidt_ready"], 1)
            dve.wait_ge(S["hid_turned"], i + 1)
            dve.tensor_copy(hidT[:, :, :], acc[1][:, 0:E_FF].rearrange("p (k q) -> p k q", q=P)
                            ).then_inc(S["hidT_ready"], 1)
            take_rows(i + 3)
            dve.wait_ge(S["down_done"], i + 2)
            dve.wait_ge(S["yo_out"], i * 16 + 16)
            dve.tensor_copy(yo[:, 512:1024], pbk[:, 512:1024]).then_inc(S["yo_dve"], 1)
        def add_experts(b):
            dve.wait_ge(S[f"rows_in{b}"], 32)
            e.step(STT(out=osum[b][:, :], in0=ga[2 * b][:, :], scalar=wk[:, 0, b:b + 1], in1=ht[:, b, :],
                       op0=ALU.mult, op1=ALU.add))
            STT(out=osum[b][:, :], in0=ga[2 * b + 1][:, :], scalar=wk[:, 1, b:b + 1], in1=osum[b][:, :],
                op0=ALU.mult, op1=ALU.add).then_inc(S["osum_ready"], 1)

        add_experts(0)
        for b in range(NB_L):
            if b + 1 < NB_L:
                add_experts(b + 1)
            dve.wait_ge(S["fin_sq"], b + 1)
            e.step(TS(fin_s[:, 4 + b:5 + b], fin_s[:, b:b + 1], 1.0 / D, EPS, ALU.mult, ALU.add))
            reciprocal_for_root(e, fin_s[:, 4 + b:5 + b])
            dve.wait_ge(S["root_out"], 10 + b)
            STT(out=osum[b][:, :], in0=osum[b][:, :], scalar=fin_s[:, 4 + b:5 + b], in1=fgain[:, :],
                op0=ALU.mult, op1=ALU.mult).then_inc(S["final_ready"], 1)

    @block.tensor
    def _(pe):
        e = Program(pe, counts="gqu")
        ident = mats[:, M_ID, :]
        pe.sem_inc(S["split_started"], 1)
        for name in ("gate_done", "up_done", "down_done", "xg_turned"):
            pe.sem_inc(S[name], 1)
        pe.wait_ge(S["mats_in"], 16)
        pe.wait_ge(S["x_in"], 32)

        def turn_unit(rows):
            pe.wait_ge(S["acc_free"], e.at("u", 1))
            for k in range(KT):
                ins = pe.transpose(acc[e.n["u"] % 2][:, k * P:k * P + P], rows(k), ident)
            ins.then_inc(S["acc_ready"], 1)
            e.n["u"] += 1

        for b in range(NB_C + NB_L):
            turn_unit(lambda k: xin[:, b, k * P:k * P + P])
        pe.wait_ge(S["consts_in"], 16 * 17)
        for n, rows in enumerate((96, 88, 120, 128)):
            ins = pe.transpose(pbk[:, P * n:P * n + rows], vec_rows[0:rows, n, :], ident[0:rows, 0:rows])
        ins.then_inc(S["vec_turned"], 1)

        def mod_chunk(n, b, after_product=False):
            pe.wait_ge(S["mod_copied"], n + 1)
            for s in range(4):
                r = e.n["g"] % RING
                pe.wait_ge(S[f"raw_in{r}"], 16 * e.laps() if isinstance(e.laps(), int) else e.laps() * 16)
                for k in range(2):
                    ins = pe.matmul(pa[:, 512 * b:512 * b + 512], silu_c[:, 2 * s + k, :],
                                    raw[r][:, 512 * k:512 * k + 512], start=s == 0 and k == 0, stop=s == 3 and k == 1)
                    if after_product and s == 0 and k == 0:
                        ins.then_inc(S["split_started"], 1)
                ins.then_inc(S["direct_done"], 1)
                e.n["g"] += 1

        def turn_mod(n, b, at):
            pe.wait_ge(S["mod_copied"], n + 3)
            pe.sem_inc(S["rows_to_turn"], 1)
            for j in range(4):
                ins = pe.transpose(pbk[:, at + 2 * j:at + 2 * j + 2], mod_row[b][0:2, P * j:P * j + P],
                                   ident[0:2, 0:2])
            ins.then_inc(S["mod_turned"], 1)

        pe.wait_ge(S["silu_ready"], 2)
        with e.loop(2, g=8) as i:
            for b in range(2):
                mod_chunk(i * 2 + b, b)
                pe.wait_ge(S["mod_free"], i * 2 + (b + 1))
                turn_mod(i * 2 + b, b, 512 * b)
        spread_mean(e, 0, FULL)

        def conv_tile(i, base):
            g0 = e.n["g"]
            chunk0 = i * 2 + 4

            def modulate(j):
                e.n["g"] = g0 + 1 + 5 * j
                mod_chunk(chunk0 + j, j, after_product=True)

            def projection(n):
                e.n["g"] = g0 + 5 * n
                product(e, ah, al, FULL, first=None)
                e.n["q"] += 1

            modulate(0)
            operand_done(e, 1)
            projection(0)
            modulate(1)
            pe.wait_ge(S["mod_free"], i + 5)
            turn_mod(chunk0, 0, base)
            projection(1)
            turn_mod(chunk0 + 1, 1, base + 8)
            e.n["g"] = g0 + 10

        pe.wait_ge(S["y_ready"], 1)
        with e.loop(KT // 2, g=20, q=4, u=4) as i:
            conv_tile(i * 2, 512)
            conv_tile(i * 2 + 1, 0)
        mod_chunk(20, 0)
        mod_chunk(21, 1)
        pe.wait_ge(S["mod_free"], KT + 5)
        turn_mod(20, 0, 512)
        mod_chunk(22, 0)
        turn_mod(21, 1, 520)
        mod_chunk(23, 1)
        pe.wait_ge(S["mod_free"], KT + 6)
        turn_mod(22, 0, 0)
        turn_mod(23, 1, 8)
        pe.wait_ge(S["cv_added"], KT)
        for s0, s1, _ in FULL:
            ins = pe.matmul(pa[:, CTX + s0:CTX + s1], mats[:, M_MEAN, :], cv_sum[:, s0:s1], start=True, stop=True)
        ins.then_inc(S["stat_ready"], 1)
        sum_over_channels(e, sq, FULL, ["ln_sq_ready"], 0)

        def first_and_rest(segs, n, operand):
            for i in range(n):
                product(e, ah, al, segs, operand=None if i else operand)
                e.n["g"] += 1
                e.n["q"] += 1

        def tile(segs, hi=ah, lo=al, **kw):
            return lambda i: product(e, hi, lo, segs, **kw)

        first_and_rest(FULL, KT, 1)

        def mlp(segs, hidden0, operand, beside=None):
            def down(chunk, j, b):
                if j == 0:
                    pe.wait_ge(S["hid_ready"], chunk * 4 + (hidden0 + 4))
                product(e, hid_hi[b], hid_lo[b], segs, k=4)

            feed_forward(e, lambda chunk, j, b: product(
                e, ah, al, segs, operand=operand if isinstance(chunk, int) and chunk + j == 0 else None), down,
                beside=beside)

        spread_mean(e, 1, FULL)
        mlp(FULL, 0, 2)
        spread_mean(e, 2, FULL)
        def sum_heads(product_number):
            for n in of_product(product_number):
                _, at, width = qk_list[n]
                if n == 0:
                    pe.wait_ge(S["heads_in"], 32)
                pe.wait_ge(S["qk_squared"], n + 1)
                pe.matmul(pa[:, at:at + width], head_pick[:, P - 2 * n:2 * P - 2 * n], qk_square[n % 4][:, 0:width],
                          start=n in (0, 9), stop=n in (10, 11)).then_inc(S["qk_summed"], 1)

        for n in range(12):
            if n < KT:
                product(e, ah, al, LATENT, operand=None if n else 3)
            elif n < KT + 2:
                product(e, ah, al, FULL)
            else:
                product_rows(e, range(NB_C + NB_L))
            e.n["g"] += 1
            e.n["q"] += 1
            sum_heads(n - 2)

        def spread_root(n):
            _, at, width = qk_list[n]
            if n >= 2:
                pe.wait_ge(S["qk_normed"], n - 1)
            pe.matmul(acc[n % 2][:, 0:width], head_spread[:, n, :], rstd[:, at:at + width], start=True, stop=True
                      ).then_inc(S["qk_spread"], 1)

        pe.wait_ge(S["acc_free"], e.at("u", 2))
        pe.wait_ge(S["root_out"], 5)
        spread_root(0)
        spread_root(1)
        t = 0
        for n in range(QK_UNITS):
            if n + 2 < QK_UNITS:
                spread_root(n + 2)
            if qk_list[n][1] == 0:
                pe.wait_ge(S["qk_normed"], n + 1)
                if t >= 2:
                    pe.wait_ge(S["qk_sined"], t - 1)
                pe.matmul(pbk[:, 512 * (t % 2):512 * (t % 2) + LAT], mats[:, M_ROT, :], qk_scaled[n % 2][:, :],
                          start=True, stop=True).then_inc(S["qk_rotated"], 1)
                t += 1
        pe.wait_ge(S["k_ready"], 1)
        for kv in range(4):
            if kv >= 2:
                pe.wait_ge(S["kdup_ready"], kv - 1)
            for s0, s1, _ in FULL:
                ins = pe.matmul((pa, pbk)[kv % 2][:, CTX + s0:CTX + s1], mats[:, M_DUP0 + kv % 2, :],
                                kf[:, kv // 2, s0:s1], start=True, stop=True)
            ins.then_inc(S["k_doubled"], 1)
        with e.loop(4) as i:
            def scores(m):
                t, h, qb = m // 8, (m // 4) % 2, m % 4
                if m >= 2:
                    pe.wait_ge(S["exp_done"], i * 16 + (m - 1))
                for k0, k1 in ((0, 512), (512, TOK)):
                    ins = pe.matmul(acc[m % 2][:, k0:k1], qst[:, t, qb * P:qb * P + P], kst[h][:, k0:k1],
                                    start=True, stop=True)
                ins.then_inc(S["scores_ready"], 1)

            def values(n):
                pe.wait_ge(S["prt_ready"], i * 16 + (4 * n + 4))
                pe.wait_ge(S["heads_taken"], i * 4 + (n + 1))
                for k in range(6):
                    ins = pe.matmul(pbk[:, 512 * (n % 2):512 * (n % 2) + LAT],
                                    vst[:, k, :, :].rearrange("p a d -> p (a d)"), prt[:, k, :],
                                    start=k == 0, stop=k == 5)
                ins.then_inc(S["heads_done"], 1)

            pe.wait_ge(S["staged"], i + 1)
            scores(0)
            scores(1)
            for m in range(16):
                if m + 2 < 16:
                    scores(m + 2)
                if m % 4 == 0 and m:
                    values(m // 4 - 1)
                pe.wait_ge(S["probs_ready"], i * 16 + (m + 1))
                if m >= 1:
                    pe.wait_ge(S["prt_ready"], i * 16 + m)
                for k in range(6):
                    ins = pe.transpose(pa[:, k * P:k * P + P], pr[m % 2][:, k * P:k * P + P], ident)
                ins.then_inc(S["turned"], 1)
            values(3)
        pe.wait_ge(S["attended"], 1)
        slots(e, KT, tile(LATENT))
        spread_mean(e, 3, LATENT)

        def prepare_tables():
            pe.wait_ge(S["prep_in"], 80)
            pe.wait_ge(S["mask_row"], 1)
            pe.matmul(pbk[0:8, 0:3 * P], rel[:, :], one_hot[:, :], start=True, stop=True).then_inc(S["rel_ready"], 1)
            for g in range(8):
                ins = pe.transpose(pa[:, g * P:g * P + P], ws_in[:, g, :], ident)
            ins.then_inc(S["ws_turned"], 1)
            for t in range(4):
                ins = pe.matmul(pbk[:, 512 + t * P:512 + t * P + P], group[:, t * P:t * P + P], bs_rows[:, :],
                                start=True, stop=True)
            ins.then_inc(S["bs_spread"], 1)

        def prepare_bias():
            pe.wait_ge(S["wst_ready"], 1)
            pe.wait_ge(S["bsp_ready"], 1)
            pe.wait_ge(S["rev_in"], 16)
            for n, bank in enumerate((pa, pbk)):
                for j in range(2):
                    ins = pe.matmul(bank[:, 512 * j:512 * j + 512], mats[:, M_FLIP, :],
                                    bias_rev[:, 4 * n + 2 * j:4 * n + 2 * j + 2, :].rearrange("p h s -> p (h s)"),
                                    start=True, stop=True)
                ins.then_inc(S["rev_turned"], 1)

        mlp(LATENT, 32, 4, {"before the last up": prepare_tables, "before the last down": prepare_bias})
        pe.wait_ge(S["bias_done"], 2)
        spread_mean(e, 4, LATENT)

        def used():
            e.n["g"] += 1
            e.n["q"] += 1

        for n in range(14):
            if n in (4, 5, 6, 7, 13):
                product_rows(e, range(NB_C, NB_C + NB_L))
            else:
                product(e, ah, al, LATENT, operand=None if n else 5)
            used()
        pe.wait_ge(S["acc_free"], e.at("u", 1))
        for kv in range(2):
            pe.matmul((pa, pbk)[kv][:, 0:LAT], mats[:, M_DUP0 + kv, :], k2f[:, :], start=True, stop=True
                      ).then_inc(S["k2_doubled"], 1)
        with e.loop(4, g=4, q=4, u=4) as i:
            for j in range(4):
                product(e, ah, al, LATENT)
                used()
        pe.wait_ge(S["kd2_ready"], 2)
        pe.wait_ge(S["gv_ready"], 4)
        pe.wait_ge(S["wst_masked"], 1)
        for t in range(4):
            for h in range(2):
                g = 2 * t + h
                for c in range(4):
                    at = (t % 2) * 512 + c * P
                    ins = pe.matmul((pa, pbk)[t // 2][HD * h:HD * h + HD, at:at + P], gv[:, c, g * HD:g * HD + HD],
                                    wst[:, g, :], start=True, stop=True)
            ins.then_inc(S["spatial_done"], 1)

        def scores2(h):
            if h >= 2:
                pe.wait_ge(S["nm2_ready"], h - 1)
            for blk in range(4):
                ins = pe.matmul(acc[h % 2][:, blk * 2 * P:blk * 2 * P + 2 * P],
                                q2[:, h // 2, blk * P:blk * P + P],
                                kd2[:, 2 * (h // 4) + h % 2, blk * P:blk * P + 2 * P],
                                start=True, stop=True)
            ins.then_inc(S["scores2"], 1)

        def values2(h):
            pe.wait_ge(S["pt2_ready"], h + 1)
            pe.wait_ge(S["heads2_taken"], h + 1)
            for blk in range(4):
                at = (h % 2) * 512 + blk * P
                for kk in range(2):
                    ins = pe.matmul(pbk[:, at:at + P], v2[:, blk + kk, h // 4, :, :].rearrange("p a d -> p (a d)"),
                                    pt2[:, blk, kk, :], start=kk == 0, stop=kk == 1)
            ins.then_inc(S["heads2"], 1)

        scores2(0)
        scores2(1)
        for h in range(8):
            if h + 2 < 8:
                scores2(h + 2)
            if h >= 1:
                values2(h - 1)
            pe.wait_ge(S["probs2"], h + 1)
            for blk in range(4):
                for kk in range(2):
                    at = (2 * blk + kk) * P
                    ins = pe.transpose(pa[:, at:at + P], sc2[h % 2][:, blk, kk * P:kk * P + P], ident)
            ins.then_inc(S["turned2"], 1)
        values2(7)
        pe.wait_ge(S["heads2_taken"], 2 + 8)
        with e.loop(2, g=4, q=4, u=8) as i:
            for s in range(2):
                for branch in range(2):
                    product(e, ah, al, LATENT, k=4, shift=4 * branch)
                    used()
        pe.wait_ge(S["merged"], 8)
        slots(e, KT, tile([(0, LAT, 0)], mh, ml, out0=512))
        spread_mean(e, 5, LATENT)
        pe.wait_ge(S["y_ready"], KT * 6)
        for b in range(NB_L):
            turn_unit(lambda k: y[:, k, CTX + b * P:CTX + b * P + P])
        pe.wait_ge(S["route_in"], 160)
        for b in range(NB_L):
            for k in range(KT):
                ins = pe.matmul(pbk[:, 20 * b:20 * b + 20], y[:, k, CTX + b * P:CTX + b * P + P], rw[:, k, :],
                                start=k == 0, stop=k == KT - 1)
        ins.then_inc(S["logits_done"], 1)
        pe.wait_ge(S["picks_ready"], 1)
        both = rt[:, 13, 0:64].rearrange("p (b n) -> p b n", b=4)
        for b in range(NB_L):
            for c in range(b + 1):
                pe.matmul(pbk[:, 512 + 16 * b:528 + 16 * b], mats[:, M_TRI if c == b else M_ONE, :], both[:, c, :],
                          start=c == 0, stop=c == b)
        for c in range(NB_L):
            ins = pe.matmul(pbk[:, 576:592], mats[:, M_ONE, :], both[:, c, :], start=c == 0, stop=c == NB_L - 1)
        ins.then_inc(S["ranks_done"], 1)
        for b in range(NB_L):
            turn_unit(lambda k: x[:, k, CTX + b * P:CTX + b * P + P])
        pe.wait_ge(S["meta_ready"], 1)
        n_blocks = pe.value_load(meta[0:1, LIST:LIST + 1], min_val=2 * LAT // P, max_val=SLOTS_MAX)

        def turn_rows(first, last):
            for k in range(first, last):
                ins = pe.transpose(pa[:, k * P:k * P + P], xg[:, :].rearrange("q (p k) -> q k p", k=KT)[:, k, :], ident)
            if last == KT:
                ins.then_inc(S["xg_turned"], 1)

        pe.wait_ge(S["acc_free"], e.at("u", 2))
        pe.wait_ge(S["xg_in"], 16)
        turn_rows(0, KT)
        with pe.Fori(0, n_blocks) as i:
            pe.wait_ge(S["xgt_ready"], i + 1)
            for name, w, c0 in (("wg_in", wg, 0), ("wu_in", wu, 512)):
                pe.wait_ge(S[name], i * 16 + 16)
                for k in range(KT):
                    ins = pe.matmul(acc[0][:, c0:c0 + E_FF], xgt[:, k, :], w[:, k, :], start=k == 0, stop=k == KT - 1)
                ins.then_inc(S["gate_done" if c0 == 0 else "up_done"], 1)
            pe.wait_ge(S["xg_in"], i * 16 + 32)
            turn_rows(0, KT // 2)
            pe.wait_ge(S["hidt_ready"], i + 1)
            for k in range(4):
                ins = pe.transpose(acc[1][:, k * P:k * P + P],
                                   hidt[:, :].rearrange("q (p k) -> q k p", k=4)[:, k, :], ident)
            ins.then_inc(S["hid_turned"], 1)
            turn_rows(KT // 2, KT)
            pe.wait_ge(S["hidT_ready"], i + 1)
            pe.wait_ge(S["wd_in"], i * 16 + 16)
            pe.wait_ge(S["yo_dve"], i + 1)
            for half in range(2):
                for k in range(4):
                    ins = pe.matmul(pbk[:, 512 * half:512 * half + 512], hidT[:, k, :],
                                    wd[:, k, 512 * half:512 * half + 512], start=k == 0, stop=k == 3)
            ins.then_inc(S["down_done"], 1)


_USED = ['x', 'c', 'ctx', 'c_ctx', 'norm1_g', 'norm2_g', 'w_mod', 'b_mod', 'w_ff1', 'w_ff2', 'conv_w_pw1',
         'conv_w_dw', 'conv_b_dw', 'conv_ln_g', 'conv_ln_b', 'conv_w_pw2', 'gqa_w_qkv', 'gqa_q_norm',
         'gqa_k_norm', 'gqa_w_o', 'attn_norm_g_2', 'w_in_2', 'gm_v_norm_g_2', 'gm_w_spatial_2',
         'gm_b_spatial_2', 'attn_sinks_2', 'rel_bias_2', 'w_proj_a_2', 'w_proj_b_2', 'w_out_2',
         'ffn_norm_g_2', 'router_group_w_2', 'router_group_b_2', 'router_expert_w_2', 'router_expert_b_2',
         'expert_w_gate_2', 'expert_w_up_2', 'expert_w_down_2', 'final_norm_g_2']


def kernel(**inputs):
    import concourse.bacc as bacc
    from concourse.bass_utils import run_bass_kernel_spmd

    nc = bacc.Bacc("TRN2", target_bir_lowering=False, num_devices=1)
    arrays = {name: np.ascontiguousarray(inputs[name]) for name in _USED}
    arrays.update(shape_constants())
    aps = {name: nc.dram_tensor(f"in_{name}", a.shape, mybir.dt.from_np(a.dtype), kind="ExternalInput").ap()
           for name, a in arrays.items()}
    out = nc.dram_tensor("out", (1, LAT, D), F32, kind="ExternalOutput").ap()
    build(nc, aps, out)
    r = run_bass_kernel_spmd(nc, [{f"in_{name}": a for name, a in arrays.items()}], core_ids=[0])
    return r.results[0]["out"]
```
